# Optimizing a Trainium2 kernel written in Bass

```python
import math
import jax, jax.numpy as jnp
from jax import lax
import numpy as np

D_MODEL = 1024
BATCH = 1
SEQ = 256
DEPTH = 2

N_A_LAYERS = (DEPTH + 1) // 2
N_B_LAYERS = DEPTH // 2
N_DENSE = (DEPTH + 1) // 2
N_MOE = DEPTH // 2

MLA_HEADS = 8
QK_NOPE = 128
QK_ROPE = 64
V_HEAD = 128
Q_LORA = 384
KV_LORA = 256
ROPE_THETA = 10000.0
Q_BLOCK = 128

SWA_HEADS = 16
SWA_KV_HEADS = 2
SWA_HEAD_DIM = 64
WINDOW = 128
BLOCK = 128

REL_BUCKETS = 32
REL_MAX_DIST = 128

D_FF = 2816
N_EXPERTS = 8
TOP_K = 2
D_FF_EXPERT = 3584

EPS = 1e-6
NEG_INF = -1e30

kernel_name = "yoco_mla_swa_sink_t5_moe_trunk"

def rmsnorm(x, g):
    xf = x.astype(jnp.float32)
    y = xf * lax.rsqrt(jnp.mean(xf * xf, axis=-1, keepdims=True) + EPS)
    return (y * g.astype(jnp.float32)).astype(x.dtype)

def rope(x, positions):
    half = x.shape[-1] // 2
    inv = ROPE_THETA ** (-jnp.arange(half, dtype=jnp.float32) / half)
    ang = positions.astype(jnp.float32)[..., None] * inv
    if x.ndim == 4:
        ang = ang[:, :, None, :]
    cos, sin = jnp.cos(ang), jnp.sin(ang)
    xf = x.astype(jnp.float32)
    x1, x2 = xf[..., :half], xf[..., half:]
    return jnp.concatenate([x1 * cos - x2 * sin, x2 * cos + x1 * sin], axis=-1).astype(x.dtype)

def t5_bucket(dist):
    n = jnp.maximum(dist, 0)
    max_exact = REL_BUCKETS // 2
    nf = jnp.maximum(n, 1).astype(jnp.float32)
    large = max_exact + (jnp.log(nf / max_exact) / math.log(REL_MAX_DIST / max_exact)
                         * (REL_BUCKETS - max_exact)).astype(jnp.int32)
    large = jnp.minimum(large, REL_BUCKETS - 1)
    return jnp.where(n < max_exact, n, large)

def mla(xn, positions, w_in, g_q, g_kv, w_uq, w_ukv, w_o):
    B, S, _ = xn.shape
    lat = xn @ w_in
    c_q = rmsnorm(lat[..., :Q_LORA], g_q)
    c_kv = rmsnorm(lat[..., Q_LORA:Q_LORA + KV_LORA], g_kv)
    k_rope = rope(lat[..., Q_LORA + KV_LORA:], positions)
    q = (c_q @ w_uq).reshape(B, S, MLA_HEADS, QK_NOPE + QK_ROPE)
    q_nope = q[..., :QK_NOPE]
    q_rope = rope(q[..., QK_NOPE:], positions)
    kv = (c_kv @ w_ukv).reshape(B, S, MLA_HEADS, QK_NOPE + V_HEAD)
    k_nope, v = kv[..., :QK_NOPE], kv[..., QK_NOPE:]
    scale = (QK_NOPE + QK_ROPE) ** -0.5
    nb = S // Q_BLOCK
    k_idx = jnp.arange(S)

    def to_blocks(t):
        return jnp.moveaxis(t.reshape(B, nb, Q_BLOCK, *t.shape[2:]), 1, 0)

    def block(args):
        qn, qr, i = args
        s = (jnp.einsum('bqhd,bkhd->bhqk', qn, k_nope, preferred_element_type=jnp.float32)
             + jnp.einsum('bqhr,bkr->bhqk', qr, k_rope, preferred_element_type=jnp.float32)) * scale
        q_idx = i * Q_BLOCK + jnp.arange(Q_BLOCK)
        s = jnp.where(k_idx[None, :] <= q_idx[:, None], s, NEG_INF)
        p = jax.nn.softmax(s, axis=-1).astype(v.dtype)
        return jnp.einsum('bhqk,bkhd->bqhd', p, v)

    o = lax.map(block, (to_blocks(q_nope), to_blocks(q_rope), jnp.arange(nb)))
    o = jnp.moveaxis(o, 0, 1).reshape(B, S, MLA_HEADS * V_HEAD)
    return o @ w_o

def shared_band_kv(h, positions, kv_g, kv_w, kv_b):
    B, S, _ = h.shape
    nb = S // BLOCK
    kv = rmsnorm(h, kv_g) @ kv_w + kv_b
    kvw = SWA_KV_HEADS * SWA_HEAD_DIM
    k = kv[..., :kvw].reshape(B, S, SWA_KV_HEADS, SWA_HEAD_DIM)
    v = kv[..., kvw:].reshape(B, S, SWA_KV_HEADS, SWA_HEAD_DIM)

    def band(t):
        pad = jnp.zeros((B, BLOCK) + t.shape[2:], t.dtype)
        tb = jnp.concatenate([pad, t], axis=1).reshape(B, nb + 1, BLOCK, *t.shape[2:])
        tb = jnp.concatenate([tb[:, :-1], tb[:, 1:]], axis=2)
        return jnp.moveaxis(tb, 1, 0)

    return band(k), band(v), band(positions)

def swa_sink(xn, positions, k_band, v_band, pos_band, rel_bias, w_q, b_q, sinks, w_o, b_o):
    B, S, _ = xn.shape
    nb = S // BLOCK
    G = SWA_HEADS // SWA_KV_HEADS
    scale = SWA_HEAD_DIM ** -0.5
    q = (xn @ w_q + b_q).reshape(B, nb, BLOCK, SWA_KV_HEADS, G, SWA_HEAD_DIM)
    q = jnp.moveaxis(q, 1, 0)
    qpos = jnp.moveaxis(positions.reshape(B, nb, BLOCK), 1, 0)
    off = jnp.arange(2 * BLOCK) - BLOCK
    rel_idx = jnp.arange(BLOCK)[:, None] - off[None, :]
    struct_ok = (rel_idx >= 0) & (rel_idx < WINDOW)
    sink = sinks.astype(jnp.float32).reshape(SWA_KV_HEADS, G)
    bias_tab = rel_bias.astype(jnp.float32).reshape(REL_BUCKETS, SWA_KV_HEADS, G)

    def block(args):
        qb, kb, vb, qp, kp, i = args
        s = jnp.einsum('bqhgd,bkhd->bhgqk', qb, kb, preferred_element_type=jnp.float32) * scale
        bucket = t5_bucket(qp[:, :, None] - kp[:, None, :])
        s = s + jnp.transpose(bias_tab[bucket], (0, 3, 4, 1, 2))
        valid = struct_ok & ((i * BLOCK + off) >= 0)[None, :]
        s = jnp.where(valid, s, NEG_INF)
        sink_col = jnp.broadcast_to(sink[None, :, :, None, None], s.shape[:-1] + (1,))
        p = jax.nn.softmax(jnp.concatenate([s, sink_col], axis=-1), axis=-1)[..., :-1]
        return jnp.einsum('bhgqk,bkhd->bqhgd', p.astype(vb.dtype), vb)

    o = lax.map(block, (q, k_band, v_band, qpos, pos_band, jnp.arange(nb)))
    o = jnp.moveaxis(o, 0, 1).reshape(B, S, SWA_HEADS * SWA_HEAD_DIM)
    return o @ w_o + b_o

def swiglu(xn, w_gate, w_up, w_down):
    return (jax.nn.silu(xn @ w_gate) * (xn @ w_up)) @ w_down

def moe(xn, w_router, w_gate, w_up, w_down):
    logits = (xn @ w_router).astype(jnp.float32)
    top_val, top_idx = lax.top_k(logits, TOP_K)
    top_w = jax.nn.softmax(top_val, axis=-1)
    gates = jnp.sum(jax.nn.one_hot(top_idx, N_EXPERTS, dtype=jnp.float32) * top_w[..., None], axis=-2)

    def per_seq(args):
        xs, gs = args
        hg = jnp.einsum('sd,edf->sef', xs, w_gate)
        hu = jnp.einsum('sd,edf->sef', xs, w_up)
        hh = jax.nn.silu(hg) * hu * gs[..., None].astype(xs.dtype)
        return jnp.einsum('sef,efd->sd', hh, w_down)

    return lax.map(per_seq, (xn, gates))

def setup_inputs(seed: int = 0) -> dict:
    key = jax.random.key(seed)
    ks = iter(jax.random.split(key, 40))
    f32 = jnp.float32

    def w(shape, fan_in):
        return jax.random.normal(next(ks), shape, f32) * (fan_in ** -0.5)

    def gain(shape):
        return 1.0 + 0.1 * jax.random.normal(next(ks), shape, f32)

    def small(shape, s=0.02):
        return s * jax.random.normal(next(ks), shape, f32)

    x = jax.random.normal(next(ks), (BATCH, SEQ, D_MODEL), f32)
    offset = jax.random.randint(next(ks), (BATCH, 1), 0, 1024, dtype=jnp.int32)
    positions = (offset + jnp.arange(SEQ, dtype=jnp.int32)[None, :]).astype(jnp.int32)
    kvw = SWA_KV_HEADS * SWA_HEAD_DIM
    return {
        "x": x,
        "positions": positions,
        "mla_w_in": w((N_A_LAYERS, D_MODEL, Q_LORA + KV_LORA + QK_ROPE), D_MODEL),
        "mla_g_q": gain((N_A_LAYERS, Q_LORA)),
        "mla_g_kv": gain((N_A_LAYERS, KV_LORA)),
        "mla_w_uq": w((N_A_LAYERS, Q_LORA, MLA_HEADS * (QK_NOPE + QK_ROPE)), Q_LORA),
        "mla_w_ukv": w((N_A_LAYERS, KV_LORA, MLA_HEADS * (QK_NOPE + V_HEAD)), KV_LORA),
        "mla_w_o": w((N_A_LAYERS, MLA_HEADS * V_HEAD, D_MODEL), MLA_HEADS * V_HEAD),
        "kv_g": gain((D_MODEL,)),
        "kv_w": w((D_MODEL, 2 * kvw), D_MODEL),
        "kv_b": small((2 * kvw,)),
        "swa_w_q": w((N_B_LAYERS, D_MODEL, SWA_HEADS * SWA_HEAD_DIM), D_MODEL),
        "swa_b_q": small((N_B_LAYERS, SWA_HEADS * SWA_HEAD_DIM)),
        "swa_sinks": small((N_B_LAYERS, SWA_HEADS), 0.5),
        "swa_w_o": w((N_B_LAYERS, SWA_HEADS * SWA_HEAD_DIM, D_MODEL), SWA_HEADS * SWA_HEAD_DIM),
        "swa_b_o": small((N_B_LAYERS, D_MODEL)),
        "rel_bias": small((REL_BUCKETS, SWA_HEADS), 0.5),
        "g_attn": gain((DEPTH, D_MODEL)),
        "g_ffn": gain((DEPTH, D_MODEL)),
        "ffn_w_gate": w((N_DENSE, D_MODEL, D_FF), D_MODEL),
        "ffn_w_up": w((N_DENSE, D_MODEL, D_FF), D_MODEL),
        "ffn_w_down": w((N_DENSE, D_FF, D_MODEL), D_FF),
        "moe_w_router": w((N_MOE, D_MODEL, N_EXPERTS), D_MODEL),
        "moe_w_gate": w((N_MOE, N_EXPERTS, D_MODEL, D_FF_EXPERT), D_MODEL),
        "moe_w_up": w((N_MOE, N_EXPERTS, D_MODEL, D_FF_EXPERT), D_MODEL),
        "moe_w_down": w((N_MOE, N_EXPERTS, D_FF_EXPERT, D_MODEL), D_FF_EXPERT),
        "g_final": gain((D_MODEL,)),
    }

def reference(x, positions, mla_w_in, mla_g_q, mla_g_kv, mla_w_uq, mla_w_ukv, mla_w_o,
              kv_g, kv_w, kv_b, swa_w_q, swa_b_q, swa_sinks, swa_w_o, swa_b_o, rel_bias,
              g_attn, g_ffn, ffn_w_gate, ffn_w_up, ffn_w_down,
              moe_w_router, moe_w_gate, moe_w_up, moe_w_down, g_final):
    h = x
    k_band = v_band = pos_band = None
    for l in range(DEPTH):
        xn = rmsnorm(h, g_attn[l])
        if l < N_A_LAYERS:
            a = l
            h = h + mla(xn, positions, mla_w_in[a], mla_g_q[a], mla_g_kv[a],
                        mla_w_uq[a], mla_w_ukv[a], mla_w_o[a])
        else:
            b = l - N_A_LAYERS
            if b == 0:
                k_band, v_band, pos_band = shared_band_kv(h, positions, kv_g, kv_w, kv_b)
            h = h + swa_sink(xn, positions, k_band, v_band, pos_band, rel_bias,
                             swa_w_q[b], swa_b_q[b], swa_sinks[b], swa_w_o[b], swa_b_o[b])
        xn = rmsnorm(h, g_ffn[l])
        if l % 2 == 0:
            j = l // 2
            h = h + swiglu(xn, ffn_w_gate[j], ffn_w_up[j], ffn_w_down[j])
        else:
            j = l // 2
            h = h + moe(xn, moe_w_router[j], moe_w_gate[j], moe_w_up[j], moe_w_down[j])
    return rmsnorm(h, g_final)


_drawn_inputs = setup_inputs


def setup_inputs(seed=0):
    import zlib

    import numpy as np

    out = dict(_drawn_inputs(seed))
    spreads = {}
    factors = {'swa_b_q': 5.837, 'swa_sinks': 7.107}
    for name, (base, spread) in spreads.items():
        noise = np.random.default_rng([zlib.crc32(name.encode()), seed]).standard_normal(out[name].shape)
        drawn = base * np.exp(spread * noise) if base else spread * noise
        out[name] = __import__('jax').numpy.asarray(drawn.astype(out[name].dtype))
    for name, factor in factors.items():
        out[name] = (out[name] * factor).astype(out[name].dtype)
    return out
```

```python
from contextlib import ExitStack

import numpy as np
import concourse.bass as bass
from concourse import mybir

ALU = mybir.AluOpType
ACT = mybir.ActivationFunctionType
AX = mybir.AxisListType
F32 = mybir.dt.float32
I32 = mybir.dt.int32
U32 = mybir.dt.uint32

P = 128
D = 1024
KD = D // P
S = 256
TT = S // P
EPS = 1e-6
NEG = -1e30

MH, NOPE, ROPE, VH = 8, 128, 64, 128
HALF = ROPE // 2
QL, KVL = 384, 256
MLA_SCALE = float((NOPE + ROPE) ** -0.5)

AH, KVH, HD = 16, 2, 64
G = AH // KVH
SWA_SCALE = float(HD ** -0.5)
WINDOW = 128
BUCKETS = 32

DFF = 2816
FC = 512
FCH = (DFF + FC - 1) // FC
NE, DFE = 8, 3584
ECH = DFE // FC

SLOTS = 96
SG_N = SLOTS // 32
NARROW = 64
SWEEPS = -(-S // SLOTS)
ITEMS_MAX = NE * SWEEPS
LASTQ = 256

RING = 7
SLOT = 4096

C_ID, C_TRI, C_ONE, C_MLA, C_WIN, C_IOTA = 0, 128, 256, 384, 768, 1024
C_E8 = C_IOTA + SLOTS
C_THR = C_E8 + NE
C_INV = C_THR + 1
C_MH = C_INV + HALF
C_N = C_MH + TT

V_GA0, V_GF0, V_GA1, V_KVG, V_GQ, V_GKV, V_KVB, V_BQ = 0, 8, 16, 24, 32, 35, 37, 38
V_N = V_BQ + G

MAGIC = 1.5 * 2.0 ** 23
TWO_PI = 2 * np.pi
C1 = float(np.float32(6.28125))
C2 = float(np.float32(np.round((TWO_PI - 6.28125) * 2 ** 20) / 2 ** 20))
C3 = float(np.float32(TWO_PI - 6.28125 - np.round((TWO_PI - 6.28125) * 2 ** 20) / 2 ** 20))
PI_LO = float(np.nextafter(np.float32(np.pi), np.float32(0)))


def constants():
    c = np.zeros((P, C_N), np.float32)
    r = np.arange(P)
    c[:, C_ID:C_ID + P] = np.eye(P)
    c[:, C_TRI:C_TRI + P] = r[:, None] < r[None, :]
    c[:, C_ONE:C_ONE + P] = 1.0
    causal = np.where(r[None, :] <= r[:, None], 0.0, NEG)
    c[:, C_MLA:C_MLA + P] = causal
    c[:, C_MLA + 2 * P:C_MLA + 3 * P] = causal
    c[:, C_WIN:C_WIN + P] = np.where(r[:, None] + P - r[None, :] < WINDOW, 0.0, NEG)
    c[:, C_WIN + P:C_WIN + 2 * P] = causal
    c[:, C_IOTA:C_IOTA + SLOTS] = np.arange(SLOTS)
    c[:, C_E8:C_E8 + NE] = np.arange(NE)
    exact = BUCKETS // 2
    log = [int(np.ceil(exact * 8.0 ** (j / 16) - 1e-9)) for j in range(1, BUCKETS - exact)]
    thr = [-1e9] + list(range(1, exact + 1)) + log
    c[:, C_THR] = np.tile(np.array(thr, np.float32), P // BUCKETS)
    c[:, C_INV:C_INV + HALF] = (10000.0 ** (-np.arange(HALF) / HALF)).astype(np.float32)
    c[:, C_MH:C_MH + TT] = -0.5
    return c


class Semaphores:
    def __init__(self, sem):
        self.consts_loaded = sem("consts_loaded")
        self.x_loaded = sem("x_loaded")
        self.smalls_loaded = sem("smalls_loaded")
        self.biasrows_loaded = sem("biasrows_loaded")
        self.rel_loaded = sem("rel_loaded")
        self.out_stored = sem("out_stored")
        self.slot0 = sem("slot0")
        self.slot1 = sem("slot1")
        self.slot2 = sem("slot2")
        self.slot3 = sem("slot3")
        self.slot4 = sem("slot4")
        self.slot5 = sem("slot5")
        self.slot6 = sem("slot6")
        self.dve_chain = sem("dve_chain")
        self.act_chain = sem("act_chain")
        self.pool_chain = sem("pool_chain")
        self.vecT_mm = sem("vecT_mm")
        self.vecT_ready = sem("vecT_ready")
        self.ssq_ready = sem("ssq_ready")
        self.ms_ready = sem("ms_ready")
        self.rstd_ready = sem("rstd_ready")
        self.xn_ready = sem("xn_ready")
        self.xT_mm = sem("xT_mm")
        self.xT_ready_v = sem("xT_ready_v")
        self.xT_ready_a = sem("xT_ready_a")
        self.rope_arg = sem("rope_arg")
        self.sincos_ready = sem("sincos_ready")
        self.latq_mm = sem("latq_mm")
        self.latkv_mm = sem("latkv_mm")
        self.cq_ready = sem("cq_ready")
        self.ckv_ready = sem("ckv_ready")
        self.krope_ready = sem("krope_ready")
        self.cT_mm = sem("cT_mm")
        self.cqT_ready = sem("cqT_ready")
        self.ckvT_ready = sem("ckvT_ready")
        self.krT_ready = sem("krT_ready")
        self.qk_mm = sem("qk_mm")
        self.qk_ready = sem("qk_ready")
        self.qrope_mm = sem("qrope_mm")
        self.qrope_ready = sem("qrope_ready")
        self.ukv_v_mm = sem("ukv_v_mm")
        self.v_ready = sem("v_ready")
        self.qrT_mm = sem("qrT_mm")
        self.qrT_ready = sem("qrT_ready")
        self.score_mm = sem("score_mm")
        self.s_ready = sem("s_ready")
        self.negmax_ready = sem("negmax_ready")
        self.exp_ready = sem("exp_ready")
        self.p_ready = sem("p_ready")
        self.pT_mm = sem("pT_mm")
        self.pT_ready = sem("pT_ready")
        self.pv_mm = sem("pv_mm")
        self.oT_ready = sem("oT_ready")
        self.wo_mm = sem("wo_mm")
        self.h_attn0 = sem("h_attn0")
        self.fgu_mm = sem("fgu_mm")
        self.fsg_ready = sem("fsg_ready")
        self.fhh_ready = sem("fhh_ready")
        self.ftr_mm = sem("ftr_mm")
        self.fhhT_ready = sem("fhhT_ready")
        self.fdown_mm = sem("fdown_mm")
        self.fh_added = sem("fh_added")
        self.delta_ready = sem("delta_ready")
        self.onehot_ready = sem("onehot_ready")
        self.bias_mm = sem("bias_mm")
        self.bias_ready = sem("bias_ready")
        self.kT_mm = sem("kT_mm")
        self.kT_ready = sem("kT_ready")
        self.sv_mm = sem("sv_mm")
        self.sv_ready = sem("sv_ready")
        self.sq_mm = sem("sq_mm")
        self.sq_ready = sem("sq_ready")
        self.bo_added = sem("bo_added")
        self.sscore_mm = sem("sscore_mm")
        self.ss_ready = sem("ss_ready")
        self.snegmax_ready = sem("snegmax_ready")
        self.sexp_ready = sem("sexp_ready")
        self.esink_ready = sem("esink_ready")
        self.sp_ready = sem("sp_ready")
        self.spT_mm = sem("spT_mm")
        self.spT_ready = sem("spT_ready")
        self.spv_mm = sem("spv_mm")
        self.soT_ready = sem("soT_ready")
        self.swo_mm = sem("swo_mm")
        self.h_attn1 = sem("h_attn1")
        self.router_mm = sem("router_mm")
        self.route_mask = sem("route_mask")
        self.gate_exp = sem("gate_exp")
        self.route_cum_mm = sem("route_cum_mm")
        self.counts_ready = sem("counts_ready")
        self.gu_mm = sem("gu_mm")
        self.sg_ready = sem("sg_ready")
        self.hh_ready = sem("hh_ready")
        self.tr_mm = sem("tr_mm")
        self.hhT_ready = sem("hhT_ready")
        self.down_mm = sem("down_mm")
        self.y_ready_a = sem("y_ready_a")
        self.y_ready_v = sem("y_ready_v")
        self.y_last = sem("y_last")
        self.sel_ready = sem("sel_ready")
        self.gath_mm = sem("gath_mm")
        self.xgT_ready_a = sem("xgT_ready_a")
        self.xgT_ready_v = sem("xgT_ready_v")
        self.selg_ready = sem("selg_ready")
        self.sgt_mm = sem("sgt_mm")
        self.sgt_ready = sem("sgt_ready")
        self.scat_mm = sem("scat_mm")
        self.h_added = sem("h_added")


def build(nc, x, positions, w_in, g_q, g_kv, w_uq, w_ukv, w_o, kv_g, kv_w, kv_b, swa_w_q, swa_b_q,
          swa_sinks, swa_w_o, swa_b_o, rel_bias, g_attn, g_ffn, f_gate, f_up, f_down, w_router,
          e_gate, e_up, e_down, g_final, consts, out):
    with ExitStack() as ctx:
        def sb(name, shape, dt=F32):
            return ctx.enter_context(nc.sbuf_tensor(name, shape, dt))

        ps = ctx.enter_context(nc.psum_tensor("ps", [P, 8, 512], F32))
        s = Semaphores(lambda name: ctx.enter_context(nc.semaphore(name)))
        slot_landed = [s.slot0, s.slot1, s.slot2, s.slot3, s.slot4, s.slot5, s.slot6]

        ring = sb("ring", [P, RING, SLOT])
        h = sb("h", [P, TT, D])
        xn = sb("xn", [P, TT, D])
        xT = sb("xT", [P, KD, S])
        xT2 = sb("xT2", [P, KD, S])
        arena = sb("arena", [P, 12288])
        cst = sb("cst", [P, C_N])
        vecs = sb("vecs", [V_N, P])
        vecT = sb("vecT", [P, V_N])
        pos_i = sb("pos_i", [P, TT], I32)
        pos_f = sb("pos_f", [P, TT])
        stat = sb("stat", [P, 16])
        wr = sb("wr", [P, KD, NE])
        kvb_row = sb("kvb_row", [1, P])
        sinks_h = sb("sinks_h", [P, AH])
        sinks = sb("sinks", [P, AH])
        n_items = sb("n_items", [P, 2], I32)
        wide = sb("wide", [P, ITEMS_MAX], I32)
        slots = sb("slots", [P, TT, ITEMS_MAX + 1])
        gates = sb("gates", [P, TT, ITEMS_MAX + 1])
        rt = sb("rt", [P, TT, 72])
        ridx = sb("ridx", [P, TT, 8], U32)

        ident = cst[:, C_ID:C_ID + P]

        def gcol(base, k):
            return vecT[:, base + k:base + k + 1]

        used = [0]

        def carve(n, pattern=None, **dims):
            v = arena[:, used[0]:used[0] + n]
            used[0] += n
            return v.rearrange(pattern, **dims) if pattern else v

        cq = carve(TT * QL, "p (t n) -> p t n", t=TT)
        ckv = carve(TT * KVL, "p (t n) -> p t n", t=TT)
        cqT = carve(3 * S, "p (k n) -> p k n", k=3)
        ckvT = carve(2 * S, "p (k n) -> p k n", k=2)
        qT = carve(MH * S, "p (k n) -> p k n", k=MH)
        qr = carve(TT * MH * ROPE, "p (t n) -> p t n", t=TT)
        qrT = carve(4 * S, "p (k n) -> p k n", k=4)
        krT = carve(S)
        kr = carve(TT * P, "p (t n) -> p t n", t=TT)
        probs = carve(MH * 3 * P, "p (k n) -> p k n", k=MH)
        pT = carve(2 * 3 * P, "p (k n) -> p k n", k=2)
        cosn = carve(TT * 2 * HALF, "p (t n) -> p t n", t=TT)
        ang = carve(6 * TT * HALF, "p (a t n) -> p a t n", a=6, t=TT)
        rtmp = carve(2 * MH * HALF, "p (a n) -> p a n", a=2)
        mstat = carve(MH * 8, "p (k n) -> p k n", k=MH)
        kT = xn[:].rearrange("p t n -> p (t n)").rearrange("p (k n) -> p k n", k=MH)
        v_rows = xT[:].rearrange("p k n -> p (k n)").rearrange("p (t n) -> p t n", t=TT)
        oT = xT2
        used[0] = 0
        fhhT = carve(2 * 4 * S, "p (a j n) -> p a j n", a=2, j=4)
        fhh = carve(2 * FC, "p (a n) -> p a n", a=2)
        fsg = carve(2 * FC, "p (a n) -> p a n", a=2)
        bias0 = carve(AH * P, "p (k n) -> p k n", k=AH)
        bias1 = carve(AH * S, "p (k n) -> p k n", k=AH)
        onehot = carve(2 * 2 * S, "p (a j n) -> p a j n", a=2, j=2)
        posq_i = sb("posq_i", [P, S], I32)
        posq = sb("posq", [P, S])
        posk_i = sb("posk_i", [P, 64], I32)
        posk = sb("posk", [P, 64])
        tabs_h = sb("tabs_h", [P, 2, 64])
        tabs = sb("tabs", [P, 64])
        used[0] = 0
        sqT = carve(G * S, "p (k n) -> p k n", k=G)
        skT = carve(S)
        sv = carve(TT * P, "p (t n) -> p t n", t=TT)
        spT = carve(2 * 3 * P, "p (k n) -> p k n", k=2)
        assert used[0] <= 4096
        used[0] = 4096 + AH * 3 * P
        sstat = carve(8 * 2 * AH, "p (a b n) -> p a b n", a=8, b=2)
        soT = xT
        bo_row = xT2[:].rearrange("p k n -> p (k n)")[:, 0:D]
        used[0] = 0
        sel = carve(TT * SLOTS, "p (t n) -> p t n", t=TT)
        selg = carve(TT * SLOTS, "p (t n) -> p t n", t=TT)
        sgt = carve(TT * P, "p (t n) -> p t n", t=TT)
        xgT = carve(KD * SLOTS, "p (k n) -> p k n", k=KD)
        hh = carve(2 * FC, "p (a n) -> p a n", a=2)
        sg = carve(2 * FC, "p (a n) -> p a n", a=2)
        upl = carve(2 * FC, "p (a n) -> p a n", a=2)
        hhT = carve(2 * 4 * SLOTS, "p (a j n) -> p a j n", a=2, j=4)
        ysb = carve(D)
        grow = carve(D)
        gfin = carve(D)
        assert used[0] <= 12288

        BIAS_ROUNDS = S // 8

        def bias_rounds(u):
            return range(min(4 * u, BIAS_ROUNDS), min(4 * u + 4, BIAS_ROUNDS))

        def rows_of(w):
            return w.rearrange("(k p) n -> p k n", p=P)

        def slot_view(n, k):
            sl = (n + RING_OFF) % RING
            return lambda cols: ring[:, sl, 0:k * cols].rearrange("p (k n) -> p k n", k=k)

        RING_OFF = 5
        win, wuq, wukv, wo = (rows_of(w[0]) for w in (w_in, w_uq, w_ukv, w_o))
        fg, fu, fd = (rows_of(w[0]) for w in (f_gate, f_up, f_down))
        kvw, swq, swo = rows_of(kv_w), rows_of(swa_w_q[0]), rows_of(swa_w_o[0])
        stream = [
            ("win_q", win[:, :, 0:QL], KD, QL, s.latq_mm, 2),
            ("win_kv", win[:, :, QL:QL + KVL + ROPE], KD, KVL + ROPE, s.latkv_mm, 2),
            ("uq0", wuq[:, :, 0:768], 3, 768, s.qrope_mm, 2),
            ("uq1", wuq[:, :, 768:1536], 3, 768, s.qrope_mm, 4),
            ("ukv", wukv, 2, 2048, s.ukv_v_mm, 4),
            ("wo0", wo[:, :, 0:512], KD, 512, s.wo_mm, 2),
            ("wo1", wo[:, :, 512:1024], KD, 512, s.wo_mm, 4),
        ]

        def f_cols(c):
            return min(FC, DFF - c * FC)

        def ffn_gu(c):
            n = f_cols(c)
            return [("fg%d" % c, fg[:, :, c * FC:c * FC + n], KD, n, s.fgu_mm, 2 * c + 2),
                    ("fu%d" % c, fu[:, :, c * FC:c * FC + n], KD, n, s.fgu_mm, 2 * c + 2)]

        def ffn_d(c):
            return [("fd%d" % c, fd[:, 4 * c:4 * c + f_cols(c) // P, :], f_cols(c) // P, D, s.fdown_mm, 4 * c + 4)]

        stream += ffn_gu(0)
        for c in range(1, FCH):
            stream += ffn_gu(c) + ffn_d(c - 1)
        stream += ffn_d(FCH - 1)
        stream += [
            ("kvw", kvw, KD, 256, s.sv_mm, 2),
            ("wq0", swq[:, 0:4, :], 4, D, s.sq_mm, 4),
            ("wq1", swq[:, 4:8, :], 4, D, s.sq_mm, 4),
            ("swo0", swo[:, :, 0:512], KD, 512, s.swo_mm, 2),
            ("swo1", swo[:, :, 512:1024], KD, 512, s.swo_mm, 4),
        ]
        DENSE = len(stream)
        assert (DENSE + RING_OFF) % RING == 0
        where = {t[0]: n for n, t in enumerate(stream)}

        def fills(n):
            v = n + RING_OFF
            return v // RING + (1 if v % RING >= RING_OFF else 0)

        def w_of(name):
            n = where[name]
            _, _, k, cols, _, _ = stream[n]
            return slot_view(n, k)(cols)

        def weights_here(eng, name):
            n = where[name]
            eng.wait_ge(slot_landed[(n + RING_OFF) % RING], 16 * fills(n))

        pieces = [("g", 0), ("u", 0), ("g", 1), ("u", 1)]
        for c in range(2, ECH):
            pieces += [("g", c), ("u", c), ("d", c - 2)]
        pieces += [("d", ECH - 2), ("d", ECH - 1)]
        NP = len(pieces)
        assert NP % RING == 0
        ppos = {p_: m for m, p_ in enumerate(pieces)}
        base_fill = (DENSE + RING_OFF) // RING

        def piece_here(eng, i, kind, c):
            m = ppos[(kind, c)]
            extra = 1 if m % RING >= RING_OFF else 0
            eng.wait_ge(slot_landed[m % RING], i * (16 * NP // RING) + 16 * (base_fill + m // RING + extra))

        def piece(kind, c):
            sl = ppos[(kind, c)] % RING
            return ring[:, sl, :].rearrange("p (k n) -> p k n", k=4 if kind == "d" else KD)

        eg = e_gate[0].rearrange("e (k p) f -> p e k f", p=P)
        eu = e_up[0].rearrange("e (k p) f -> p e k f", p=P)
        ed = e_down[0].rearrange("e (k p) n -> p e k n", p=P)

        block = ctx.enter_context(nc.Block())

        @block.sync
        def _(sp):
            sp.dma_start(h[:], x[0].rearrange("(t p) d -> p t d", p=P)).then_inc(s.x_loaded, 16)
            loads = [
                (vecs[V_GA0:V_GA0 + 8, :], g_attn[0].rearrange("(k n) -> k n", n=P)),
                (vecs[V_GF0:V_GF0 + 8, :], g_ffn[0].rearrange("(k n) -> k n", n=P)),
                (vecs[V_GA1:V_GA1 + 8, :], g_attn[1].rearrange("(k n) -> k n", n=P)),
                (vecs[V_KVG:V_KVG + 8, :], kv_g.rearrange("(k n) -> k n", n=P)),
                (vecs[V_GQ:V_GQ + 3, :], g_q[0].rearrange("(k n) -> k n", n=P)),
                (vecs[V_GKV:V_GKV + 2, :], g_kv[0].rearrange("(k n) -> k n", n=P)),
                (vecs[V_KVB:V_KVB + 1, :], kv_b[0:P].rearrange("(k n) -> k n", n=P)),
                (vecs[V_BQ:V_BQ + G, 0:HD], swa_b_q[0, 0:512].rearrange("(k n) -> k n", n=HD)),
                (vecs[V_BQ:V_BQ + G, HD:P], swa_b_q[0, 512:1024].rearrange("(k n) -> k n", n=HD)),
                (pos_i[:], positions[0].rearrange("(t p) -> p t", p=P)),
            ]
            sp.dma_start(cst[:], consts).then_inc(s.consts_loaded, 16)
            for dst, src in loads:
                sp.dma_start(dst, src, allow_slow_non_contiguous=dst.dtype == I32).then_inc(s.smalls_loaded, 16)
            for n, (name, src, k, cols, _, _) in enumerate(stream):
                if n >= RING:
                    sp.wait_ge(stream[n - RING][4], stream[n - RING][5])
                sl = (n + RING_OFF) % RING
                sp.dma_start(slot_view(n, k)(cols), src).then_inc(slot_landed[sl], 16)

            def load_item(i, expert, first):
                for m, (kind, c) in enumerate(pieces):
                    if m < RING:
                        if first:
                            old = stream[DENSE - RING + m]
                            sp.wait_ge(old[4], old[5])
                        else:
                            k0, c0 = pieces[m - RING + NP]
                            sp.wait_ge(s.down_mm if k0 == "d" else s.gu_mm, i * ECH + (c0 + 2 - ECH))
                    else:
                        k0, c0 = pieces[m - RING]
                        sp.wait_ge(s.down_mm if k0 == "d" else s.gu_mm, i * ECH + (c0 + 2))
                    if kind == "d":
                        src = ed[:, expert, 4 * c:4 * c + 4, :]
                    else:
                        src = (eg if kind == "g" else eu)[:, expert, :, c * FC:(c + 1) * FC]
                    sp.dma_start(piece(kind, c), src).then_inc(slot_landed[m % RING], 16)

            load_item(0, 0, True)
            with sp.Fori(1, NE) as i:
                load_item(i, i, False)
            sp.wait_ge(s.counts_ready, 1)
            items = sp.value_load(n_items[0:1, 0:1], min_val=NE, max_val=ITEMS_MAX)
            for sweep in range(1, SWEEPS):
                with sp.If(items > sweep * NE):
                    with sp.Fori(0, NE) as e:
                        load_item(e + sweep * NE, e, False)
                with sp.Else():
                    sp.nop()
            sp.wait_ge(s.out_stored, 32)

        @block.gpsimd
        def _(pool):
            more = [
                (posq_i[:], positions[0:1, :].to_broadcast([P, S])),
                (kvb_row[:], kv_b[P:2 * P].rearrange("(a n) -> a n", a=1)),
                (wr[:], w_router[0].rearrange("(k p) e -> p k e", p=P)),
                (sinks_h[:], swa_sinks[0:1, :].to_broadcast([P, AH])),
            ]
            for kk in range(4):
                more.append((posk_i[32 * kk:32 * kk + 32, :], positions[0:1, 64 * kk:64 * kk + 64].to_broadcast([32, 64])))
            for dst, src in more:
                pool.dma_start(dst, src).then_inc(s.biasrows_loaded, 16)

            def rstd(n):
                pool.wait_ge(s.ms_ready, n + 1)
                nc.gpsimd.tensor_tensor(stat[:, 4:6], stat[:, 2:4], cst[:, C_MH:C_MH + TT], ALU.pow).then_inc(s.rstd_ready, 1)

            pool.wait_ge(s.consts_loaded, 16)
            rstd(0)
            nc.gpsimd.memset(tabs_h[:], 0.0).then_inc(s.pool_chain, 1)
            pool.wait_ge(s.pool_chain, 1)
            for kk in range(4):
                c = slice(AH * kk, AH * kk + AH)
                pool.dma_start(tabs_h[32 * kk:32 * kk + 32, 0, c], rel_bias).then_inc(s.rel_loaded, 16)
                pool.dma_start(tabs_h[32 * kk + 1:32 * kk + 32, 1, c], rel_bias[0:31, :]).then_inc(s.rel_loaded, 16)
            pool.wait_ge(s.ms_ready, 2)
            nc.gpsimd.tensor_tensor(stat[:, 12:14], stat[:, 8:10], cst[:, C_MH:C_MH + TT], ALU.pow).then_inc(s.rstd_ready, 1)
            pool.wait_ge(s.ms_ready, 3)
            nc.gpsimd.tensor_tensor(stat[:, 14:16], stat[:, 10:12], cst[:, C_MH:C_MH + TT], ALU.pow).then_inc(s.rstd_ready, 1)
            rstd(3)
            rstd(4)
            pool.wait_ge(s.sv_mm, 2)
            pool.dma_start(bo_row, swa_b_o[0:1, :].to_broadcast([P, D])).then_inc(s.rel_loaded, 16)
            pool.wait_ge(s.rel_loaded, 16 * 9)
            pool.wait_ge(s.xn_ready, 6)
            for t in range(TT):
                nc.gpsimd.tensor_tensor(h[:, t, :], h[:, t, :], bo_row, ALU.add).then_inc(s.bo_added, 1)
            pool.wait_ge(s.soT_ready, AH)
            pool.dma_start(grow, g_ffn[1:2, :].to_broadcast([P, D])).then_inc(s.rel_loaded, 16)
            pool.dma_start(gfin, g_final.rearrange("(a n) -> a n", a=1).to_broadcast([P, D])).then_inc(s.rel_loaded, 16)
            rstd(5)
            rstd(6)

        @block.scalar
        def _(act):
            def norm_squares(n):
                for t in range(TT):
                    nc.scalar.activation(xn[:, t, :], h[:, t, :], ACT.Square, accum_out=stat[:, t:t + 1]).then_inc(s.ssq_ready, 1)

            act.wait_ge(s.x_loaded, 16)
            norm_squares(0)
            act.wait_ge(s.vecT_mm, 1)
            act.copy(vecT[:], ps[:, 0, 0:V_N]).then_inc(s.vecT_ready, 1)
            act.wait_ge(s.rope_arg, 2)
            act.activation(cosn[:, :, HALF:2 * HALF], ang[:, 4], ACT.Sin).then_inc(s.sincos_ready, 1)
            act.activation(cosn[:, :, 0:HALF], ang[:, 5], ACT.Sin).then_inc(s.sincos_ready, 1)

            def evac_xT(banks, dst, gain, count):
                act.wait_ge(s.xT_mm, count)
                for b, off in banks:
                    for j in range(2):
                        k = 2 * b + j
                        src = ps[:, off + b, j * S:(j + 1) * S]
                        if gain is None:
                            act.copy(dst[:, k, :], src).then_inc(s.xT_ready_a, 1)
                        else:
                            act.activation(dst[:, k, :], src, ACT.Copy, scale=gcol(gain, k)).then_inc(s.xT_ready_a, 1)

            act.wait_ge(s.vecT_ready, 1)
            evac_xT([(2, 0), (3, 0)], xT, V_GA0, 1)
            for t in range(TT):
                act.wait_ge(s.latq_mm, t + 1)
                act.activation(cq[:, t, :], ps[:, 4 + t, 0:QL], ACT.Square, accum_out=stat[:, t:t + 1]).then_inc(s.ssq_ready, 1)
            for t in range(TT):
                act.wait_ge(s.latkv_mm, t + 1)
                act.activation(ckv[:, t, :], ps[:, 6 + t, 0:KVL], ACT.Square, accum_out=stat[:, 6 + t:7 + t]).then_inc(s.ssq_ready, 1)
            act.wait_ge(s.cT_mm, 2)
            for k in range(2):
                act.activation(ckvT[:, k, :], ps[:, 2, k * S:(k + 1) * S], ACT.Copy, scale=gcol(V_GKV, k)).then_inc(s.ckvT_ready, 1)
            act.wait_ge(s.cT_mm, 3)
            act.copy(krT, ps[:, 3, 0:S]).then_inc(s.krT_ready, 1)
            for u in range(8):
                act.wait_ge(s.qk_mm, u + 1)
                dst = qT if u < 4 else kT
                act.copy(dst[:, 2 * (u % 4):2 * (u % 4) + 2, :], ps[:, 6 + u % 2, :].rearrange("p (k n) -> p k n", k=2)).then_inc(s.qk_ready, 1)
            for n in range(4):
                t, half = n // 2, n % 2
                act.wait_ge(s.ukv_v_mm, n + 1)
                act.copy(v_rows[:, t, half * 512:(half + 1) * 512], ps[:, n, :]).then_inc(s.v_ready, 1)
            for i in range(MH + 1):
                if i < MH:
                    act.wait_ge(s.negmax_ready, 2 * i + 2)
                    st = mstat[:, i, :]
                    act.activation(probs[:, i, 0:P], probs[:, i, 0:P], ACT.Exp, scale=MLA_SCALE, bias=st[:, 2:3],
                                   accum_out=st[:, 4:5]).then_inc(s.exp_ready, 1)
                    act.activation(probs[:, i, P:3 * P], probs[:, i, P:3 * P], ACT.Exp, scale=MLA_SCALE, bias=st[:, 3:4],
                                   accum_out=st[:, 5:6]).then_inc(s.exp_ready, 1)
                if i >= 1:
                    act.wait_ge(s.pT_mm, i)
                    if i >= 3:
                        act.wait_ge(s.pv_mm, i - 2)
                    act.copy(pT[:, (i - 1) % 2, :], ps[:, 4 + (i - 1) % 2, 0:3 * P]).then_inc(s.pT_ready, 1)
            act.wait_ge(s.h_attn0, 4)
            norm_squares(1)
            evac_xT([(2, 4), (3, 4)], xT, V_GF0, 2)
            for u in range(2 * FCH + 1):
                if u < 2 * FCH:
                    n = f_cols(u // 2)
                    act.wait_ge(s.fgu_mm, u + 1)
                    if u >= 2:
                        act.wait_ge(s.fhh_ready, u - 1)
                    act.activation(fsg[:, u % 2, 0:n], ps[:, 2 * (u % 2), 0:n], ACT.Silu).then_inc(s.fsg_ready, 1)
                if u >= 1:
                    c, t, n = (u - 1) // 2, (u - 1) % 2, f_cols((u - 1) // 2)
                    act.wait_ge(s.ftr_mm, u)
                    if c >= 2:
                        act.wait_ge(s.fdown_mm, 4 * (c - 1))
                    act.copy(fhhT[:, c % 2, 0:n // P, t * P:(t + 1) * P],
                             ps[:, 4, 0:n].rearrange("p (j n) -> p j n", n=P)).then_inc(s.fhhT_ready, 1)
            act.wait_ge(s.fh_added, 4 * FCH)
            norm_squares(2)
            evac_xT([(2, 0), (3, 0)], xT, V_GA1, 3)
            evac_xT([(2, 0), (3, 0)], xT2, V_KVG, 3)
            act.wait_ge(s.kT_mm, 1)
            act.activation(skT, ps[:, 4, 0:S], ACT.Identity, bias=gcol(V_KVB, 0)).then_inc(s.kT_ready, 1)
            for t in range(TT):
                act.wait_ge(s.sv_mm, t + 1)
                act.copy(sv[:, t, :], ps[:, 5 + t, 0:P]).then_inc(s.sv_ready, 1)
            for u in range(4):
                act.wait_ge(s.sq_mm, u + 1)
                for j in range(2):
                    g = 2 * u + j
                    act.activation(sqT[:, g, :], ps[:, u % 2, j * S:(j + 1) * S], ACT.Identity, bias=gcol(V_BQ, g)).then_inc(s.sq_ready, 1)

            def sexp(i):
                act.wait_ge(s.snegmax_ready, i // 4 + 1)
                if i % 4 == 0:
                    for b in range(2):
                        act.activation(sstat[:, 3, b, i:i + 4], sstat[:, 2, b, i:i + 4], ACT.Exp).then_inc(s.esink_ready, 1)
                act.activation(bias0[:, i, :], bias0[:, i, :], ACT.Exp, bias=sstat[:, 1, 0, i:i + 1],
                               accum_out=sstat[:, 4, 0, i:i + 1]).then_inc(s.sexp_ready, 1)
                act.activation(bias1[:, i, :], bias1[:, i, :], ACT.Exp, bias=sstat[:, 1, 1, i:i + 1],
                               accum_out=sstat[:, 4, 1, i:i + 1]).then_inc(s.sexp_ready, 1)

            def spT_evac(i):
                act.wait_ge(s.spT_mm, i + 1)
                if i >= 2:
                    act.wait_ge(s.spv_mm, i - 1)
                act.copy(spT[:, i % 2, :], ps[:, i % 2, 0:3 * P]).then_inc(s.spT_ready, 1)

            def swa_out(i):
                g, v = i // 2, i % 2
                part = 64 * (g % 2)
                act.wait_ge(s.spv_mm, i + 1)
                act.copy(soT[part:part + 64, 4 * v + g // 2, :], ps[part:part + 64, 6 + i % 2, 0:S]).then_inc(s.soT_ready, 1)

            for q in range(5):
                for j in range(4):
                    if q < 4:
                        sexp(4 * q + j)
                    if q >= 1:
                        i = 4 * (q - 1) + j
                        spT_evac(i)
                        if i >= 1:
                            swa_out(i - 1)
            swa_out(AH - 1)
            act.wait_ge(s.h_attn1, 4)
            norm_squares(3)
            evac_xT([(2, 0), (3, 0)], xT, None, 4)
            for t in range(TT):
                act.wait_ge(s.route_mask, t + 1)
                act.activation(rt[:, t, 49:50], rt[:, t, 48:49], ACT.Exp).then_inc(s.gate_exp, 1)

            def silu_and_last(i, c, narrow):
                a = c % 2
                act.wait_ge(s.gu_mm, i * ECH + (c + 2))
                act.wait_ge(s.hh_ready, i * (2 * ECH) + (2 * max(c - 1, 0) + 1))
                if narrow:
                    act.activation(sg[0:NARROW, a, :], ps[0:NARROW, 2 * a, :], ACT.Silu).then_inc(s.sg_ready, 1)
                    act.copy(upl[0:NARROW, a, :], ps[64:64 + NARROW, 2 * a + 1, :]).then_inc(s.sg_ready, 3)
                    return
                act.activation(sg[0:SLOTS, a, :], ps[0:SLOTS, 2 * a, :], ACT.Silu).then_inc(s.sg_ready, 1)
                for g in range(SG_N):
                    src = ps[96:128, 2 * a + g // 2, (g % 2) * LASTQ:(g % 2 + 1) * LASTQ]
                    act.copy(upl[32 * g:32 * g + 32, a, 0:LASTQ], src).then_inc(s.sg_ready, 1)

            def hhT_evac(i, c, narrow):
                act.wait_ge(s.tr_mm, i * ECH + (c + 2))
                act.wait_ge(s.down_mm, i * ECH + (max(c - 1, 0) + 1))
                m = NARROW if narrow else SLOTS
                act.copy(hhT[:, c % 2, :, 0:m], ps[:, 4, 0:4 * SLOTS].rearrange("p (j n) -> p j n", j=4)[:, :, 0:m]).then_inc(s.hhT_ready, 1)

            act.sem_inc(s.sg_ready, 1)
            act.sem_inc(s.hhT_ready, 1)
            act.sem_inc(s.y_ready_a, 1)
            act.sem_inc(s.sgt_ready, 1)
            act.wait_ge(s.gath_mm, 2)
            act.copy(xgT[:, 4:8, :].rearrange("p k n -> p (k n)"), ps[:, 3, 0:4 * SLOTS]).then_inc(s.xgT_ready_a, 2)
            act.wait_ge(s.counts_ready, 1)
            items = act.value_load(n_items[0:1, 0:1], min_val=NE, max_val=ITEMS_MAX)

            def act_item(i, narrow):
                for c in range(ECH):
                    silu_and_last(i, c, narrow)
                    if c == 4:
                        act.wait_ge(s.sgt_mm, i + 2)
                        act.copy(sgt[0:SLOTS].rearrange("p t n -> p (t n)"), ps[0:SLOTS, 7, 0:S]).then_inc(s.sgt_ready, 1)
                    if c >= 1:
                        hhT_evac(i, c - 1, narrow)
                act.wait_ge(s.gath_mm, i + 3)
                act.copy(xgT[:, 4:8, :].rearrange("p k n -> p (k n)"), ps[:, 3, 0:4 * SLOTS]).then_inc(s.xgT_ready_a, 1)
                hhT_evac(i, ECH - 1, narrow)
                act.wait_ge(s.down_mm, i * ECH + (ECH + 1))
                if narrow:
                    act.copy(ysb[0:NARROW, 0:512], ps[0:NARROW, 5, :]).then_inc(s.y_ready_a, 1)
                    return
                for g in range(2):
                    act.copy(ysb[32 * g:32 * g + 32, 768:1024], ps[96:128, 5, g * LASTQ:(g + 1) * LASTQ]).then_inc(s.act_chain, 1)
                act.copy(ysb[0:SLOTS, 0:512], ps[0:SLOTS, 5, :]).then_inc(s.y_ready_a, 1)

            with act.Fori(0, items) as i:
                many = act.value_load(wide[0:1, bass.ds(i, 1)], min_val=0, max_val=1)
                with act.If(many > 0):
                    act_item(i, False)
                with act.Else():
                    act_item(i, True)
            act.wait_ge(s.h_added, items * 4 + 5)
            for t in range(TT):
                act.activation(xT[:].rearrange("p k n -> p (k n)")[:, t * D:(t + 1) * D], h[:, t, :], ACT.Square,
                               accum_out=stat[:, t:t + 1]).then_inc(s.ssq_ready, 1)
            orow = out[0].rearrange("(t p) d -> t p d", p=P)
            for t in range(TT):
                act.wait_ge(s.xn_ready, 9 + t)
                act.dma_start(orow[t], xn[:, t, :]).then_inc(s.out_stored, 16)

        @block.tensor
        def _(pe):
            def rows_to_T(n, first, off):
                pe.wait_ge(s.xn_ready, first)
                for k in range(KD):
                    for t in range(TT):
                        mm = pe.transpose(ps[:, off + k // 2, (k % 2) * S + t * P:(k % 2) * S + (t + 1) * P],
                                          xn[:, t, k * P:(k + 1) * P], ident)
                mm.then_inc(s.xT_mm, 1)

            pe.wait_ge(s.consts_loaded, 16)
            pe.wait_ge(s.smalls_loaded, 160)
            pe.transpose(ps[:, 0, 0:V_N], vecs[:], ident[0:V_N, 0:V_N]).then_inc(s.vecT_mm, 1)
            pe.wait_ge(s.vecT_ready, 1)
            rows_to_T(0, 2, 0)
            pe.wait_ge(s.xT_ready_v, 4)
            pe.wait_ge(s.xT_ready_a, 4)
            for name, bank, n, sem in (("win_q", 4, QL, s.latq_mm), ("win_kv", 6, KVL + ROPE, s.latkv_mm)):
                weights_here(pe, name)
                w = w_of(name)
                for t in range(TT):
                    for k in range(KD):
                        mm = pe.matmul(ps[:, bank + t, 0:n], xT[:, k, t * P:(t + 1) * P], w[:, k, :],
                                       start=(k == 0), stop=(k == KD - 1))
                    mm.then_inc(sem, 1)
            pe.wait_ge(s.cq_ready, 2)
            for k in range(3):
                for t in range(TT):
                    mm = pe.transpose(ps[:, k // 2, (k % 2) * S + t * P:(k % 2) * S + (t + 1) * P],
                                      cq[:, t, k * P:(k + 1) * P], ident)
            mm.then_inc(s.cT_mm, 1)
            pe.wait_ge(s.ckv_ready, 2)
            for k in range(2):
                for t in range(TT):
                    mm = pe.transpose(ps[:, 2, k * S + t * P:k * S + (t + 1) * P], ckv[:, t, k * P:(k + 1) * P], ident)
            mm.then_inc(s.cT_mm, 1)
            pe.wait_ge(s.krope_ready, 2)
            for t in range(TT):
                mm = pe.transpose(ps[:, 3, t * P:(t + 1) * P], kr[:, t, :], ident)
            mm.then_inc(s.cT_mm, 1)
            pe.wait_ge(s.cqT_ready, 3)
            for half in range(2):
                weights_here(pe, "uq%d" % half)
                w = w_of("uq%d" % half)
                for u in (2 * half, 2 * half + 1):
                    if u >= 2:
                        pe.wait_ge(s.qk_ready, u - 1)
                    for j in range(2):
                        hl = 2 * (u % 2) + j
                        for k in range(3):
                            mm = pe.matmul(ps[:, 6 + u % 2, j * S:(j + 1) * S], w[:, k, hl * 192:hl * 192 + NOPE], cqT[:, k, :],
                                           start=(k == 0), stop=(k == 2))
                    mm.then_inc(s.qk_mm, 1)
                for t in range(TT):
                    for k in range(3):
                        r = w[:, k, :].rearrange("p (h n) -> p h n", n=192)[:, :, NOPE:192]
                        mm = pe.matmul(ps[:, 4 + t, half * S:(half + 1) * S], cqT[:, k, t * P:(t + 1) * P], r,
                                       start=(k == 0), stop=(k == 2))
                    mm.then_inc(s.qrope_mm, 1)
            pe.wait_ge(s.ckvT_ready, 2)
            weights_here(pe, "ukv")
            w = w_of("ukv")
            for u in range(4, 8):
                pe.wait_ge(s.qk_ready, u - 1)
                for j in range(2):
                    hd = 2 * (u - 4) + j
                    for k in range(2):
                        mm = pe.matmul(ps[:, 6 + u % 2, j * S:(j + 1) * S], w[:, k, hd * 256:hd * 256 + NOPE], ckvT[:, k, :],
                                       start=(k == 0), stop=(k == 1))
                mm.then_inc(s.qk_mm, 1)
            pe.wait_ge(s.krT_ready, 1)
            for n in range(4):
                t, half = n // 2, n % 2
                for k in range(2):
                    r = w[:, k, :].rearrange("p (h n) -> p h n", n=256)[:, 4 * half:4 * half + 4, NOPE:256]
                    mm = pe.matmul(ps[:, n, :], ckvT[:, k, t * P:(t + 1) * P], r, start=(k == 0), stop=(k == 1))
                mm.then_inc(s.ukv_v_mm, 1)
            pe.wait_ge(s.qrope_ready, 4)
            for k in range(4):
                for t in range(TT):
                    mm = pe.transpose(ps[:, 4 + k // 2, (k % 2) * S + t * P:(k % 2) * S + (t + 1) * P],
                                      qr[:, t, k * P:(k + 1) * P], ident)
            mm.then_inc(s.qrT_mm, 1)

            def scores(i):
                b, part = i % 4, 64 * (i % 2)
                if i >= 4:
                    pe.wait_ge(s.s_ready, i - 3)
                for t, c0, n in ((0, 0, P), (1, P, 2 * P)):
                    pe.matmul(ps[:, b, c0:c0 + n], qT[:, i, t * P:(t + 1) * P], kT[:, i, 0:n], start=True, stop=False)
                    mm = pe.matmul(ps[:, b, c0:c0 + n], qrT[part:part + 64, i // 2, t * P:(t + 1) * P], krT[part:part + 64, 0:n],
                                   start=False, stop=True)
                mm.then_inc(s.score_mm, 1)

            def probs_T(i):
                pe.wait_ge(s.p_ready, 2 * i + 2)
                if i >= 2:
                    pe.wait_ge(s.pT_ready, i - 1)
                for b in range(3):
                    mm = pe.transpose(ps[:, 4 + i % 2, b * P:(b + 1) * P], probs[:, i, b * P:(b + 1) * P], ident)
                mm.then_inc(s.pT_mm, 1)

            def pv(i):
                pe.wait_ge(s.pT_ready, i + 1)
                if i >= 2:
                    pe.wait_ge(s.oT_ready, i - 1)
                o = ps[:, 6 + i % 2, :]
                v0, v1 = (v_rows[:, t, i * VH:(i + 1) * VH] for t in range(TT))
                pe.matmul(o[:, 0:P], v0, pT[:, i % 2, 0:P], start=True, stop=True)
                pe.matmul(o[:, P:S], v0, pT[:, i % 2, P:S], start=True, stop=False)
                pe.matmul(o[:, P:S], v1, pT[:, i % 2, S:3 * P], start=False, stop=True).then_inc(s.pv_mm, 1)

            pe.wait_ge(s.qk_ready, 8)
            pe.wait_ge(s.v_ready, 4)
            pe.wait_ge(s.qrT_ready, 4)
            for i in range(4):
                scores(i)
            for i in range(MH + 1):
                if i < MH:
                    probs_T(i)
                if i >= 1:
                    pv(i - 1)
                if i + 4 < MH:
                    scores(i + 4)
            pe.wait_ge(s.oT_ready, MH)
            for half in range(2):
                weights_here(pe, "wo%d" % half)
                w = w_of("wo%d" % half)
                for t in range(TT):
                    for k in range(KD):
                        mm = pe.matmul(ps[:, 2 * half + t, :], oT[:, k, t * P:(t + 1) * P], w[:, k, :], start=(k == 0), stop=(k == KD - 1))
                    mm.then_inc(s.wo_mm, 1)

            rows_to_T(1, 4, 4)
            pe.wait_ge(s.xT_ready_v, 8)
            pe.wait_ge(s.xT_ready_a, 8)

            def ffn_products(c, t):
                u, n = 2 * c + t, f_cols(c)
                weights_here(pe, "fg%d" % c)
                weights_here(pe, "fu%d" % c)
                if u >= 2:
                    pe.wait_ge(s.fhh_ready, u - 1)
                rounds = list(bias_rounds(u))
                for b, name in ((0, "fg%d" % c), (1, "fu%d" % c)):
                    w = w_of(name)
                    for k in range(KD):
                        mm = pe.matmul(ps[:, 2 * t + b, 0:n], xT[:, k, t * P:(t + 1) * P], w[:, k, :], start=(k == 0), stop=(k == KD - 1))
                        if k % 4 == 2 and rounds:
                            bias_round(rounds.pop(0))
                mm.then_inc(s.fgu_mm, 1)

            def ffn_T(c, t):
                u = 2 * c + t
                pe.wait_ge(s.fhh_ready, u + 1)
                if u >= 1:
                    pe.wait_ge(s.fhhT_ready, u)
                for j in range(f_cols(c) // P):
                    mm = pe.transpose(ps[:, 4, j * P:(j + 1) * P], fhh[:, t, j * P:(j + 1) * P], ident)
                mm.then_inc(s.ftr_mm, 1)

            def ffn_down(c):
                weights_here(pe, "fd%d" % c)
                w, nj = w_of("fd%d" % c), f_cols(c) // P
                pe.wait_ge(s.fhhT_ready, 2 * c + 2)
                for n in range(4):
                    t, half = n // 2, n % 2
                    if 4 * c + n >= 2:
                        pe.wait_ge(s.fh_added, 4 * c + n - 1)
                    for j in range(nj):
                        mm = pe.matmul(ps[:, 5 + n % 2, :], fhhT[:, c % 2, j, t * P:(t + 1) * P], w[:, j, half * 512:(half + 1) * 512],
                                       start=(j == 0), stop=(j == nj - 1))
                    mm.then_inc(s.fdown_mm, 1)

            def bias_round(r):
                pe.wait_ge(s.onehot_ready, 4 * r // 2 + 2)
                if r == 0:
                    pe.wait_ge(s.delta_ready, 1)
                else:
                    pe.wait_ge(s.bias_ready, 2 * r)
                for j in range(2):
                    pe.matmul(ps[:, 7, j * 64:(j + 1) * 64], onehot[:, r % 2, j, P:S], tabs[:], start=True, stop=True)
                    mm = pe.matmul(ps[:, 7, 128 + j * 32:128 + (j + 1) * 32], onehot[0:64, r % 2, j, 0:P], tabs[0:64, 0:32],
                                   start=True, stop=True)
                mm.then_inc(s.bias_mm, 1)

            for c in range(FCH):
                ffn_products(c, 0)
                if c >= 1:
                    ffn_T(c - 1, 1)
                ffn_products(c, 1)
                ffn_T(c, 0)
                if c >= 1:
                    ffn_down(c - 1)
            ffn_T(FCH - 1, 1)
            ffn_down(FCH - 1)

            rows_to_T(2, 6, 0)
            pe.wait_ge(s.xT_ready_v, 16)
            pe.wait_ge(s.xT_ready_a, 16)
            weights_here(pe, "kvw")
            w = w_of("kvw")
            for k in range(KD):
                mm = pe.matmul(ps[:, 4, 0:S], w[:, k, 0:P], xT2[:, k, :], start=(k == 0), stop=(k == KD - 1))
            mm.then_inc(s.kT_mm, 1)
            pe.wait_ge(s.biasrows_loaded, 16 * 8)
            for t in range(TT):
                for k in range(KD):
                    pe.matmul(ps[:, 5 + t, 0:P], xT2[:, k, t * P:(t + 1) * P], w[:, k, P:2 * P], start=(k == 0), stop=False)
                pe.matmul(ps[:, 5 + t, 0:P], cst[0:1, C_ONE:C_ONE + P], kvb_row[0:1, :], start=False, stop=True).then_inc(s.sv_mm, 1)
            weights_here(pe, "wq0")
            weights_here(pe, "wq1")
            wq = [w_of("wq0"), w_of("wq1")]
            for u in range(4):
                if u >= 2:
                    pe.wait_ge(s.sq_ready, 2 * u - 2)
                for j in range(2):
                    g = 2 * u + j
                    for k in range(KD):
                        for v in range(KVH):
                            c0 = (v * G + g) * HD
                            mm = pe.matmul(ps[v * HD:(v + 1) * HD, u % 2, j * S:(j + 1) * S], wq[k // 4][:, k % 4, c0:c0 + HD],
                                           xT[:, k, :], start=(k == 0), stop=(k == KD - 1))
                mm.then_inc(s.sq_mm, 1)

            def sscores(i):
                g, v = i // 2, i % 2
                if i >= 4:
                    pe.wait_ge(s.ss_ready, 2 * (i - 3))
                b, part = 2 + i % 4, 64 * v
                for t, c0, n in ((0, 0, P), (1, P, 2 * P)):
                    mm = pe.matmul(ps[:, b, c0:c0 + n], sqT[part:part + 64, g, t * P:(t + 1) * P], skT[part:part + 64, 0:n],
                                   start=True, stop=True)
                mm.then_inc(s.sscore_mm, 1)

            def sprobs_T(i):
                pe.wait_ge(s.sp_ready, 2 * i + 2)
                if i >= 2:
                    pe.wait_ge(s.spT_ready, i - 1)
                pe.transpose(ps[:, i % 2, 0:P], bias0[:, i, :], ident)
                pe.transpose(ps[:, i % 2, P:2 * P], bias1[:, i, 0:P], ident)
                pe.transpose(ps[:, i % 2, 2 * P:3 * P], bias1[:, i, P:2 * P], ident).then_inc(s.spT_mm, 1)

            def spv(i):
                g, v = i // 2, i % 2
                pe.wait_ge(s.spT_ready, i + 1)
                if i >= 2:
                    pe.wait_ge(s.soT_ready, i - 1)
                part = 64 * (g % 2)
                o = ps[part:part + 64, 6 + i % 2, :]
                v0, v1 = (sv[:, t, v * HD:(v + 1) * HD] for t in range(TT))
                pe.matmul(o[:, 0:P], v0, spT[:, i % 2, 0:P], start=True, stop=True)
                pe.matmul(o[:, P:S], v0, spT[:, i % 2, P:S], start=True, stop=False)
                pe.matmul(o[:, P:S], v1, spT[:, i % 2, S:3 * P], start=False, stop=True).then_inc(s.spv_mm, 1)

            pe.wait_ge(s.kT_ready, 1)
            pe.wait_ge(s.sv_ready, 2)
            pe.wait_ge(s.sq_ready, 8)
            for i in range(4):
                sscores(i)
            for q in range(5):
                for j in range(4):
                    if q + 1 < 4 and q < 4:
                        sscores(4 * (q + 1) + j)
                for j in range(4):
                    i = 4 * q + j
                    if i < AH:
                        sprobs_T(i)
                    if 1 <= i <= AH:
                        spv(i - 1)
            pe.wait_ge(s.soT_ready, AH)
            for half in range(2):
                weights_here(pe, "swo%d" % half)
                w = w_of("swo%d" % half)
                for t in range(TT):
                    for k in range(KD):
                        mm = pe.matmul(ps[:, 2 * half + t, :], soT[:, k, t * P:(t + 1) * P], w[:, k, :], start=(k == 0), stop=(k == KD - 1))
                    mm.then_inc(s.swo_mm, 1)

            rows_to_T(3, 8, 0)
            pe.wait_ge(s.xT_ready_v, 20)
            pe.wait_ge(s.xT_ready_a, 20)
            for t in range(TT):
                for k in range(KD):
                    mm = pe.matmul(ps[:, 4 + t, 0:NE], xT[:, k, t * P:(t + 1) * P], wr[:, k, :], start=(k == 0), stop=(k == KD - 1))
                mm.then_inc(s.router_mm, 1)
            pe.wait_ge(s.route_mask, 2)
            tri, ones = cst[:, C_TRI:C_TRI + P], cst[:, C_ONE:C_ONE + P]
            m0, m1 = rt[:, 0, 8:16], rt[:, 1, 8:16]
            pe.matmul(ps[:, 6, 0:8], tri, m0, start=True, stop=True)
            pe.matmul(ps[:, 6, 8:16], ones, m0, start=True, stop=False)
            pe.matmul(ps[:, 6, 8:16], tri, m1, start=False, stop=True)
            pe.matmul(ps[:, 6, 16:24], ones, m0, start=True, stop=False)
            pe.matmul(ps[:, 6, 16:24], ones, m1, start=False, stop=True).then_inc(s.route_cum_mm, 1)

            def gather():
                for k in range(KD):
                    for t in range(TT):
                        mm = pe.matmul(ps[:, 2 + k // 4, (k % 4) * SLOTS:(k % 4 + 1) * SLOTS], xn[:, t, k * P:(k + 1) * P], sel[:, t, :],
                                       start=(t == 0), stop=(t == TT - 1))
                mm.then_inc(s.gath_mm, 1)

            def grouped(bank, stationary, streams, first, last):
                for g in range(SG_N):
                    lhs = stationary[:, 32 * g:32 * g + 32]
                    for b, rhs in enumerate(streams[:-1]):
                        pe.matmul(ps[32 * g:32 * g + 32, bank + b, 0:rhs.shape[1]], lhs, rhs, start=first, stop=last,
                                  skip_group_check=True)
                for g in range(SG_N):
                    mm = pe.matmul(ps[96:128, bank + g // 2, (g % 2) * LASTQ:(g % 2 + 1) * LASTQ],
                                   stationary[:, 32 * g:32 * g + 32], streams[-1], start=(first and g % 2 == 0), stop=last,
                                   skip_group_check=True)
                return mm

            def products(i, c, narrow):
                a = c % 2
                piece_here(pe, i, "g", c)
                piece_here(pe, i, "u", c)
                if c == 0:
                    pe.wait_ge(s.xgT_ready_a, i + 2)
                    pe.wait_ge(s.xgT_ready_v, i + 2)
                if c != 1:
                    pe.wait_ge(s.hh_ready, i * (2 * ECH) + (2 * max(c - 1, 0) + 1))
                wg, wu = piece("g", c), piece("u", c)
                for k in range(KD):
                    if narrow:
                        lhs = xgT[:, k, 0:NARROW]
                        pe.matmul(ps[0:NARROW, 2 * a, :], lhs, wg[:, k, :], start=(k == 0), stop=(k == KD - 1))
                        mm = pe.matmul(ps[64:64 + NARROW, 2 * a + 1, :], lhs, wu[:, k, :], start=(k == 0), stop=(k == KD - 1))
                        continue
                    mm = grouped(2 * a, xgT[:, k, :], [wg[:, k, :], wu[:, k, 0:LASTQ], wu[:, k, LASTQ:FC]], k == 0, k == KD - 1)
                mm.then_inc(s.gu_mm, 1)

            def scatter(i, j):
                t, half = j // 2, j % 2
                if j == 0:
                    pe.wait_ge(s.y_ready_a, i + 1)
                    pe.wait_ge(s.y_ready_v, i + 1)
                    pe.wait_ge(s.sgt_ready, i + 1)
                else:
                    pe.wait_ge(s.h_added, i * 4 + (j + 1))
                pe.matmul(ps[:, 7, :], sgt[0:SLOTS, t, :], ysb[0:SLOTS, half * 512:(half + 1) * 512], start=True, stop=True).then_inc(s.scat_mm, 1)

            def scatter_T(i):
                pe.wait_ge(s.selg_ready, i * 2 + 3)
                pe.wait_ge(s.h_added, i * 4 + 5)
                pe.transpose(ps[0:SLOTS, 7, 0:P], selg[:, 0, :], ident)
                pe.transpose(ps[0:SLOTS, 7, P:2 * P], selg[:, 1, :], ident).then_inc(s.sgt_mm, 1)

            def hidden_T(i, c):
                pe.wait_ge(s.hh_ready, i * (2 * ECH) + (2 * c + 3))
                pe.wait_ge(s.hhT_ready, i * ECH + (c + 1))
                for j in range(4):
                    mm = pe.transpose(ps[:, 4, j * SLOTS:(j + 1) * SLOTS], hh[0:SLOTS, c % 2, j * P:(j + 1) * P], ident[0:SLOTS, 0:SLOTS])
                mm.then_inc(s.tr_mm, 1)

            def down(i, c, narrow):
                piece_here(pe, i, "d", c)
                pe.wait_ge(s.hhT_ready, i * ECH + (c + 2))
                if c == 0:
                    pe.wait_ge(s.y_ready_a, i + 1)
                    pe.wait_ge(s.y_ready_v, i + 1)
                w = piece("d", c)
                for j in range(4):
                    if narrow:
                        lhs = hhT[:, c % 2, j, 0:NARROW]
                        first, last = c == 0 and j == 0, c == ECH - 1 and j == 3
                        pe.matmul(ps[0:NARROW, 5, :], lhs, w[:, j, 0:512], start=first, stop=last)
                        mm = pe.matmul(ps[64:64 + NARROW, 6, :], lhs, w[:, j, 512:1024], start=first, stop=last)
                        continue
                    mm = grouped(5, hhT[:, c % 2, j, :], [w[:, j, 0:512], w[:, j, 512:768], w[:, j, 768:1024]],
                                 c == 0 and j == 0, c == ECH - 1 and j == 3)
                mm.then_inc(s.down_mm, 1)

            for q in (s.gu_mm, s.tr_mm, s.down_mm, s.gath_mm, s.sgt_mm, s.scat_mm):
                pe.sem_inc(q, 1)
            pe.wait_ge(s.sel_ready, 3)
            gather()
            pe.wait_ge(s.counts_ready, 1)
            items = pe.value_load(n_items[0:1, 0:1], min_val=NE, max_val=ITEMS_MAX)

            def pe_item(i, narrow):
                for c in range(ECH):
                    products(i, c, narrow)
                    if c < 4:
                        scatter(i, c)
                    if c == 4:
                        scatter_T(i)
                    if c >= 1:
                        hidden_T(i, c - 1)
                    if c >= 2:
                        down(i, c - 2, narrow)
                pe.wait_ge(s.sel_ready, i * 2 + 5)
                pe.wait_ge(s.hh_ready, i * (2 * ECH) + (2 * (ECH - 1) + 1))
                gather()
                hidden_T(i, ECH - 1)
                down(i, ECH - 2, narrow)
                down(i, ECH - 1, narrow)

            with pe.Fori(0, items) as i:
                many = pe.value_load(wide[0:1, bass.ds(i, 1)], min_val=0, max_val=1)
                with pe.If(many > 0):
                    pe_item(i, False)
                with pe.Else():
                    pe_item(i, True)
            for j in range(4):
                scatter(items, j)

        @block.vector
        def _(dve):
            chain = [0]

            def link(ins):
                chain[0] += 1
                ins.then_inc(s.dve_chain, 1)
                dve.wait_ge(s.dve_chain, chain[0])

            def mean_squares(n, ssq, dst, width, squares):
                dve.wait_ge(s.ssq_ready, squares)
                dve.tensor_scalar(stat[:, dst:dst + 2], stat[:, ssq:ssq + 2], 1.0 / width, EPS, ALU.mult, ALU.add).then_inc(s.ms_ready, 1)

            def norm_rows(n, squares, rstds):
                mean_squares(n, 0, 2, D, squares)
                dve.wait_ge(s.rstd_ready, rstds)
                for t in range(TT):
                    dve.tensor_scalar(xn[:, t, :], h[:, t, :], stat[:, 4 + t:5 + t], None, ALU.mult).then_inc(s.xn_ready, 1)

            def evac_xT(banks, dst, gain, count):
                dve.wait_ge(s.xT_mm, count)
                for b, off in banks:
                    for j in range(2):
                        k = 2 * b + j
                        src = ps[:, off + b, j * S:(j + 1) * S]
                        if gain is None:
                            dve.tensor_copy(dst[:, k, :], src).then_inc(s.xT_ready_v, 1)
                        else:
                            dve.tensor_scalar(dst[:, k, :], src, gcol(gain, k), None, ALU.mult).then_inc(s.xT_ready_v, 1)

            dve.wait_ge(s.consts_loaded, 16)
            dve.wait_ge(s.smalls_loaded, 160)
            link(dve.tensor_copy(pos_f[:], pos_i[:]))
            for t in range(TT):
                link(dve.tensor_scalar(ang[:, 0, t, :], cst[:, C_INV:C_INV + HALF], pos_f[:, t:t + 1], None, ALU.mult))

            def reduced(dst, quarter):
                link(dve.tensor_scalar(ang[:, 1], ang[:, 0], float(1 / TWO_PI), quarter, ALU.mult, ALU.add))
                link(dve.tensor_scalar(ang[:, 1], ang[:, 1], MAGIC, MAGIC, ALU.add, ALU.subtract))
                link(dve.scalar_tensor_tensor(out=ang[:, 2], in0=ang[:, 1], scalar=-C1, in1=ang[:, 0], op0=ALU.mult, op1=ALU.add))
                link(dve.scalar_tensor_tensor(out=ang[:, 2], in0=ang[:, 1], scalar=-C2, in1=ang[:, 2], op0=ALU.mult, op1=ALU.add))
                link(dve.scalar_tensor_tensor(out=ang[:, 2], in0=ang[:, 1], scalar=-C3, in1=ang[:, 2], op0=ALU.mult, op1=ALU.add))
                link(dve.tensor_scalar(ang[:, 2], ang[:, 2], quarter * TWO_PI, PI_LO, ALU.add, ALU.min))
                dve.tensor_scalar(ang[:, dst], ang[:, 2], -PI_LO, None, ALU.max).then_inc(s.rope_arg, 1)

            norm_rows(0, 2, 1)
            reduced(4, 0.0)
            dve.wait_ge(s.rope_arg, 1)
            reduced(5, 0.25)
            dve.wait_ge(s.vecT_ready, 1)
            evac_xT([(0, 0), (1, 0)], xT, V_GA0, 1)

            dve.wait_ge(s.ssq_ready, 4)
            dve.tensor_scalar(stat[:, 8:10], stat[:, 0:2], 1.0 / QL, EPS, ALU.mult, ALU.add).then_inc(s.ms_ready, 1)
            dve.wait_ge(s.ssq_ready, 6)
            dve.tensor_scalar(stat[:, 10:12], stat[:, 6:8], 1.0 / KVL, EPS, ALU.mult, ALU.add).then_inc(s.ms_ready, 1)
            dve.wait_ge(s.rstd_ready, 2)
            for t in range(TT):
                dve.tensor_scalar(cq[:, t, :], ps[:, 4 + t, 0:QL], stat[:, 12 + t:13 + t], None, ALU.mult).then_inc(s.cq_ready, 1)
            dve.wait_ge(s.rstd_ready, 3)
            for t in range(TT):
                dve.tensor_scalar(ckv[:, t, :], ps[:, 6 + t, 0:KVL], stat[:, 14 + t:15 + t], None, ALU.mult).then_inc(s.ckv_ready, 1)

            dve.wait_ge(s.sincos_ready, 2)
            for t in range(TT):
                x1, x2 = ps[:, 6 + t, KVL:KVL + HALF], ps[:, 6 + t, KVL + HALF:KVL + ROPE]
                cos, sin = cosn[:, t, 0:HALF], cosn[:, t, HALF:2 * HALF]
                a, b, c, d = (rtmp[:, 0, n * HALF:(n + 1) * HALF] for n in range(4))
                dve.tensor_tensor(a, x1, cos, ALU.mult)
                dve.tensor_tensor(b, x2, sin, ALU.mult)
                dve.tensor_tensor(c, x2, cos, ALU.mult)
                link(dve.tensor_tensor(d, x1, sin, ALU.mult))
                krv = kr[:, t, :].rearrange("p (r n) -> p r n", r=2)
                link(dve.tensor_tensor(krv[:, 0, 0:HALF], a, b, ALU.subtract))
                link(dve.tensor_tensor(krv[:, 0, HALF:ROPE], c, d, ALU.add))
                dve.tensor_copy(krv[:, 1, :], krv[:, 0, :]).then_inc(s.krope_ready, 1)
            dve.wait_ge(s.cT_mm, 1)
            for k in range(3):
                dve.tensor_scalar(cqT[:, k, :], ps[:, k // 2, (k % 2) * S:(k % 2 + 1) * S], gcol(V_GQ, k), None, ALU.mult).then_inc(s.cqT_ready, 1)
            for t in range(TT):
                dve.wait_ge(s.qrope_mm, 3 + t)
                q = ps[:, 4 + t, :].rearrange("p (h n) -> p h n", n=ROPE)
                x1, x2 = q[:, :, 0:HALF], q[:, :, HALF:ROPE]
                o = qr[:, t, :].rearrange("p (h n) -> p h n", n=ROPE)
                cos = cosn[:, t:t + 1, 0:HALF].to_broadcast([P, MH, HALF])
                sin = cosn[:, t:t + 1, HALF:2 * HALF].to_broadcast([P, MH, HALF])
                a = rtmp[:, 0, :].rearrange("p (h n) -> p h n", n=HALF)
                b = rtmp[:, 1, :].rearrange("p (h n) -> p h n", n=HALF)
                link(dve.tensor_tensor(a, x1, cos, ALU.mult))
                link(dve.tensor_tensor(b, x2, sin, ALU.mult))
                dve.tensor_tensor(o[:, :, 0:HALF], a, b, ALU.subtract).then_inc(s.qrope_ready, 1)
                dve.wait_ge(s.qrope_ready, 2 * t + 1)
                link(dve.tensor_tensor(a, x2, cos, ALU.mult))
                link(dve.tensor_tensor(b, x1, sin, ALU.mult))
                dve.tensor_tensor(o[:, :, HALF:ROPE], a, b, ALU.add).then_inc(s.qrope_ready, 1)
                dve.wait_ge(s.qrope_ready, 2 * t + 2)
            dve.wait_ge(s.qrT_mm, 1)
            for k in range(4):
                dve.tensor_copy(qrT[:, k, :], ps[:, 4 + k // 2, (k % 2) * S:(k % 2 + 1) * S]).then_inc(s.qrT_ready, 1)

            def mla_max(i):
                dve.wait_ge(s.score_mm, i + 1)
                st = mstat[:, i, :]
                dve.tensor_tensor(probs[:, i, :], ps[:, i % 4, 0:3 * P], cst[:, C_MLA:C_MLA + 3 * P], ALU.add).then_inc(s.s_ready, 1)
                dve.wait_ge(s.s_ready, i + 1)
                dve.tensor_reduce(st[:, 0:1], probs[:, i, 0:P], AX.X, ALU.max, negate=True)
                link(dve.tensor_reduce(st[:, 1:2], probs[:, i, P:3 * P], AX.X, ALU.max, negate=True))
                dve.tensor_scalar(st[:, 2:4], st[:, 0:2], MLA_SCALE, None, ALU.mult).then_inc(s.negmax_ready, 2)

            def mla_norm(i):
                st = mstat[:, i, :]
                dve.wait_ge(s.exp_ready, 2 * i + 2)
                link(dve.reciprocal(st[:, 6:8], st[:, 4:6]))
                dve.tensor_scalar(probs[:, i, 0:P], probs[:, i, 0:P], st[:, 6:7], None, ALU.mult).then_inc(s.p_ready, 1)
                dve.tensor_scalar(probs[:, i, P:3 * P], probs[:, i, P:3 * P], st[:, 7:8], None, ALU.mult).then_inc(s.p_ready, 1)

            def mla_out(i):
                dve.wait_ge(s.pv_mm, i + 1)
                dve.tensor_copy(oT[:, i, :], ps[:, 6 + i % 2, 0:S]).then_inc(s.oT_ready, 1)

            for i in range(MH + 3):
                if i < MH:
                    mla_max(i)
                if 1 <= i <= MH:
                    mla_norm(i - 1)
                if i >= 3:
                    mla_out(i - 3)
            for n in range(4):
                half, t = n // 2, n % 2
                dve.wait_ge(s.wo_mm, n + 1)
                hv = h[:, t, half * 512:(half + 1) * 512]
                dve.tensor_tensor(hv, hv, ps[:, n, :], ALU.add).then_inc(s.h_attn0, 1)

            dve.wait_ge(s.biasrows_loaded, 16 * 8)
            link(dve.tensor_copy(posq[:], posq_i[:]))
            link(dve.tensor_copy(posk[:], posk_i[:]))
            link(dve.tensor_scalar(posk[:], posk[:], cst[:, C_THR:C_THR + 1], None, ALU.add))
            dve.wait_ge(s.h_attn0, 4)
            norm_rows(1, 8, 4)
            dve.wait_ge(s.rel_loaded, 16 * 8)
            by_h = [tabs_h[:, n, :].rearrange("p (k v g) -> p k v g", k=4, v=KVH) for n in range(2)]
            dve.tensor_tensor(tabs[:].rearrange("p (k g v) -> p k v g", k=4, v=KVH), by_h[0], by_h[1], ALU.subtract).then_inc(s.delta_ready, 1)
            link(dve.tensor_copy(sinks[:].rearrange("p (g v) -> p v g", v=KVH), sinks_h[:].rearrange("p (v g) -> p v g", v=KVH)))
            evac_xT([(0, 4), (1, 4)], xT, V_GF0, 2)

            def onehots(r):
                if r >= 2:
                    dve.wait_ge(s.bias_mm, r - 1)
                for j in range(2):
                    dve.tensor_scalar(onehot[:, r % 2, j, :], posq[:], posk[:, 2 * r + j:2 * r + j + 1], None, ALU.is_ge).then_inc(s.onehot_ready, 1)

            def bias_out(r):
                dve.wait_ge(s.bias_mm, r + 1)
                for dst, c0, nk, m in ((bias1, 0, 4, C_WIN), (bias0, 128, 2, C_WIN + P)):
                    src = ps[:, 7, c0:c0 + nk * 32].rearrange("p (j k h) -> p j k h", j=2, k=nk)
                    mask = cst[:, m:m + nk * 64].rearrange("p (k j) -> p j k", k=nk)[:, 2 * r:2 * r + 2, :]
                    o = dst.rearrange("p h (k j) -> p j k h", k=nk)[:, 2 * r:2 * r + 2]
                    dve.tensor_tensor(o, src, mask.unsqueeze(3).to_broadcast([P, 2, nk, AH]), ALU.add).then_inc(s.bias_ready, 1)

            def ffn_hidden(u):
                n = f_cols(u // 2)
                dve.wait_ge(s.fsg_ready, u + 1)
                if u >= 2:
                    dve.wait_ge(s.ftr_mm, u - 1)
                dve.tensor_tensor(fhh[:, u % 2, 0:n], fsg[:, u % 2, 0:n], ps[:, 2 * (u % 2) + 1, 0:n], ALU.mult).then_inc(s.fhh_ready, 1)

            def ffn_add(c):
                for n in range(4):
                    t, half = n // 2, n % 2
                    dve.wait_ge(s.fdown_mm, 4 * c + n + 1)
                    hv = h[:, t, half * 512:(half + 1) * 512]
                    if c >= 1:
                        dve.wait_ge(s.fh_added, 4 * (c - 1) + n + 1)
                    dve.tensor_tensor(hv, hv, ps[:, 5 + n % 2, :], ALU.add).then_inc(s.fh_added, 1)

            onehots(0)
            for u in range(2 * FCH):
                c = u // 2
                for r in bias_rounds(u):
                    if r + 1 < BIAS_ROUNDS:
                        onehots(r + 1)
                    bias_out(r)
                ffn_hidden(u)
                if u % 2 == 1 and c >= 1:
                    ffn_add(c - 1)
            ffn_add(FCH - 1)

            dve.wait_ge(s.fh_added, 4 * FCH)
            norm_rows(2, 10, 5)
            evac_xT([(0, 0), (1, 0)], xT, V_GA1, 3)
            evac_xT([(0, 0), (1, 0)], xT2, V_KVG, 3)

            def swa_scores(q):
                for i in range(4 * q, 4 * q + 4):
                    dve.wait_ge(s.sscore_mm, i + 1)
                    b = 2 + i % 4
                    dve.scalar_tensor_tensor(out=bias0[:, i, :], in0=ps[:, b, 0:P], scalar=SWA_SCALE, in1=bias0[:, i, :],
                                             op0=ALU.mult, op1=ALU.add).then_inc(s.ss_ready, 1)
                    dve.scalar_tensor_tensor(out=bias1[:, i, :], in0=ps[:, b, P:3 * P], scalar=SWA_SCALE, in1=bias1[:, i, :],
                                             op0=ALU.mult, op1=ALU.add).then_inc(s.ss_ready, 1)
                c = slice(4 * q, 4 * q + 4)
                dve.wait_ge(s.ss_ready, 8 * q + 8)
                dve.tensor_reduce(sstat[:, 0, 0, c], bias0[:, c, :], AX.X, ALU.max)
                link(dve.tensor_reduce(sstat[:, 0, 1, c], bias1[:, c, :], AX.X, ALU.max))
                for b in range(2):
                    link(dve.tensor_tensor(sstat[:, 5, b, c], sstat[:, 0, b, c], sinks[:, c], ALU.max))
                for b in range(2):
                    link(dve.tensor_tensor(sstat[:, 2, b, c], sinks[:, c], sstat[:, 5, b, c], ALU.subtract))
                link(dve.tensor_scalar(sstat[:, 1, 0, c], sstat[:, 5, 0, c], -1.0, None, ALU.mult))
                dve.tensor_scalar(sstat[:, 1, 1, c], sstat[:, 5, 1, c], -1.0, None, ALU.mult).then_inc(s.snegmax_ready, 1)

            def swa_norm(q):
                c = slice(4 * q, 4 * q + 4)
                dve.wait_ge(s.sexp_ready, 8 * q + 8)
                dve.wait_ge(s.esink_ready, 2 * q + 2)
                for b in range(2):
                    link(dve.tensor_tensor(sstat[:, 6, b, c], sstat[:, 4, b, c], sstat[:, 3, b, c], ALU.add))
                for b in range(2):
                    link(dve.reciprocal(sstat[:, 7, b, c], sstat[:, 6, b, c]))
                for i in range(4 * q, 4 * q + 4):
                    dve.tensor_scalar(bias0[:, i, :], bias0[:, i, :], sstat[:, 7, 0, i:i + 1], None, ALU.mult).then_inc(s.sp_ready, 1)
                    dve.tensor_scalar(bias1[:, i, :], bias1[:, i, :], sstat[:, 7, 1, i:i + 1], None, ALU.mult).then_inc(s.sp_ready, 1)

            for q in range(5):
                if q < 4:
                    swa_scores(q)
                if q >= 1:
                    swa_norm(q - 1)
            dve.wait_ge(s.bo_added, 2)
            for n in range(4):
                half, t = n // 2, n % 2
                dve.wait_ge(s.swo_mm, n + 1)
                hv = h[:, t, half * 512:(half + 1) * 512]
                dve.tensor_tensor(hv, hv, ps[:, n, :], ALU.add).then_inc(s.h_attn1, 1)

            dve.wait_ge(s.h_attn1, 4)
            mean_squares(3, 0, 2, D, 12)
            dve.wait_ge(s.rstd_ready, 6)
            dve.wait_ge(s.rel_loaded, 16 * 11)
            for t in range(TT):
                dve.scalar_tensor_tensor(out=xn[:, t, :], in0=h[:, t, :], scalar=stat[:, 4 + t:5 + t], in1=grow,
                                         op0=ALU.mult, op1=ALU.mult).then_inc(s.xn_ready, 1)
            evac_xT([(0, 0), (1, 0)], xT, None, 4)
            link(dve.memset(ysb[:], 0.0))
            link(dve.memset(sgt[:], 0.0))
            link(dve.memset(hh[:], 0.0))
            e8 = cst[:, C_E8:C_E8 + NE]
            for t in range(TT):
                lg, mask, top = rt[:, t, 0:8], rt[:, t, 8:16], rt[:, t, 16:24]
                idx, o1, o2 = rt[:, t, 24:32], rt[:, t, 32:40], rt[:, t, 40:48]
                z = rt[:, t, 48:56]
                dve.wait_ge(s.router_mm, t + 1)
                link(dve.tensor_copy(lg, ps[:, 4 + t, 0:NE]))
                link(dve.max(top, lg))
                link(dve.max_index(ridx[:, t, :], top, lg))
                link(dve.tensor_copy(idx, ridx[:, t, :]))
                link(dve.tensor_scalar(o1, e8, idx[:, 0:1], None, ALU.is_equal))
                link(dve.tensor_scalar(o2, e8, idx[:, 1:2], None, ALU.is_equal))
                link(dve.tensor_tensor(z[:, 0:1], top[:, 1:2], top[:, 0:1], ALU.subtract))
                dve.tensor_tensor(mask, o1, o2, ALU.add).then_inc(s.route_mask, 1)
            dve.wait_ge(s.gate_exp, 2)
            for t in range(TT):
                o1, o2, z = rt[:, t, 32:40], rt[:, t, 40:48], rt[:, t, 48:56]
                link(dve.tensor_scalar(z[:, 2:3], z[:, 1:2], 1.0, None, ALU.add))
                link(dve.reciprocal(z[:, 3:4], z[:, 2:3]))
                link(dve.tensor_tensor(z[:, 4:5], z[:, 1:2], z[:, 3:4], ALU.mult))
                link(dve.tensor_scalar(rt[:, t, 56:64], o1, z[:, 3:4], None, ALU.mult))
                link(dve.scalar_tensor_tensor(out=gates[:, t, 0:NE], in0=o2, scalar=z[:, 4:5], in1=rt[:, t, 56:64],
                                              op0=ALU.mult, op1=ALU.add))
                for w in range(1, SWEEPS):
                    link(dve.tensor_copy(gates[:, t, w * NE:(w + 1) * NE], gates[:, t, 0:NE]))
                link(dve.memset(gates[:, t, ITEMS_MAX:ITEMS_MAX + 1], 0.0))
            dve.wait_ge(s.route_cum_mm, 1)
            for t in range(TT):
                link(dve.tensor_scalar(rt[:, t, 64:72], ps[:, 6, 8 * t:8 * t + 8], 1.0, None, ALU.add))
                link(dve.tensor_tensor(rt[:, t, 64:72], rt[:, t, 64:72], rt[:, t, 8:16], ALU.mult))
                for w in range(SWEEPS):
                    link(dve.tensor_scalar(slots[:, t, w * NE:(w + 1) * NE], rt[:, t, 64:72], -1.0 - w * SLOTS, None, ALU.add))
                link(dve.memset(slots[:, t, ITEMS_MAX:ITEMS_MAX + 1], -1.0))
            link(dve.tensor_reduce(rt[:, 0, 24:25], ps[:, 6, 16:24], AX.X, ALU.max))
            for w in range(1, SWEEPS):
                link(dve.tensor_scalar(rt[:, 0, 24 + w:25 + w], rt[:, 0, 24:25], w * SLOTS + 0.5, float(NE), ALU.is_ge, ALU.mult))
            link(dve.tensor_reduce(rt[:, 0, 28:29], rt[:, 0, 25:25 + SWEEPS - 1], AX.X, ALU.add))
            link(dve.tensor_scalar(rt[:, 0, 28:29], rt[:, 0, 28:29], float(NE), None, ALU.add))
            link(dve.tensor_copy(n_items[:, 0:1], rt[:, 0, 28:29]))
            for w in range(SWEEPS - 1):
                link(dve.tensor_scalar(wide[:, w * NE:(w + 1) * NE], ps[:, 6, 16:24], w * SLOTS + NARROW + 0.5, None, ALU.is_ge))
            w = SWEEPS - 1
            dve.tensor_scalar(wide[:, w * NE:(w + 1) * NE], ps[:, 6, 16:24], w * SLOTS + NARROW + 0.5, None, ALU.is_ge).then_inc(s.counts_ready, 1)
            dve.wait_ge(s.counts_ready, 1)

            iota = cst[:, C_IOTA:C_IOTA + SLOTS]

            def select(i):
                for t in range(TT):
                    dve.tensor_scalar(sel[:, t, :], iota, slots[:, t, i:i + 1], None, ALU.is_equal).then_inc(s.sel_ready, 1)

            for q in (s.sel_ready, s.selg_ready, s.hh_ready, s.y_ready_v, s.xgT_ready_v, s.h_added):
                dve.sem_inc(q, 1)
            select(0)
            dve.wait_ge(s.gath_mm, 2)
            dve.tensor_copy(xgT[:, 0:4, :].rearrange("p k n -> p (k n)"), ps[:, 2, 0:4 * SLOTS]).then_inc(s.xgT_ready_v, 1)
            items = dve.value_load(n_items[0:1, 0:1], min_val=NE, max_val=ITEMS_MAX)

            def add_rows(i, j):
                t, half = j // 2, j % 2
                dve.wait_ge(s.scat_mm, i * 4 + (j + 2))
                hv = h[:, t, half * 512:(half + 1) * 512]
                dve.tensor_tensor(hv, hv, ps[:, 7, :], ALU.add).then_inc(s.h_added, 1)


            def dve_item(i, narrow):
                dve.wait_ge(s.sgt_mm, i + 1)
                for t in range(TT):
                    dve.tensor_scalar(selg[:, t, :], iota, slots[:, t, bass.ds(i, 1)], gates[:, t, bass.ds(i, 1)], ALU.is_equal, ALU.mult).then_inc(s.selg_ready, 1)
                dve.wait_ge(s.gath_mm, i + 2)
                for t in range(TT):
                    dve.tensor_scalar(sel[:, t, :], iota, slots[:, t, bass.ds(i + 1, 1)], None, ALU.is_equal).then_inc(s.sel_ready, 1)
                for c in range(ECH):
                    a = c % 2
                    dve.wait_ge(s.sg_ready, i * (4 * ECH) + (4 * c + 5))
                    dve.wait_ge(s.tr_mm, i * ECH + (max(c - 1, 0) + 1))
                    if narrow:
                        dve.tensor_tensor(hh[0:NARROW, a, :], sg[0:NARROW, a, :], upl[0:NARROW, a, :], ALU.mult).then_inc(s.hh_ready, 2)
                    else:
                        dve.tensor_tensor(hh[0:SLOTS, a, 0:LASTQ], sg[0:SLOTS, a, 0:LASTQ], ps[0:SLOTS, 2 * a + 1, 0:LASTQ], ALU.mult).then_inc(s.hh_ready, 1)
                        dve.tensor_tensor(hh[0:SLOTS, a, LASTQ:FC], sg[0:SLOTS, a, LASTQ:FC], upl[0:SLOTS, a, 0:LASTQ], ALU.mult).then_inc(s.hh_ready, 1)
                    if c < 4:
                        add_rows(i, c)
                dve.wait_ge(s.gath_mm, i + 3)
                dve.tensor_copy(xgT[:, 0:4, :].rearrange("p k n -> p (k n)"), ps[:, 2, 0:4 * SLOTS]).then_inc(s.xgT_ready_v, 1)
                dve.wait_ge(s.down_mm, i * ECH + (ECH + 1))
                if narrow:
                    dve.tensor_copy(ysb[0:NARROW, 512:1024], ps[64:64 + NARROW, 6, :]).then_inc(s.y_ready_v, 1)
                else:
                    dve.tensor_copy(ysb[64:96, 768:1024], ps[96:128, 6, 0:LASTQ]).then_inc(s.y_last, 1)
                    dve.tensor_copy(ysb[0:SLOTS, 512:768], ps[0:SLOTS, 6, 0:LASTQ]).then_inc(s.y_ready_v, 1)

            with dve.Fori(0, items) as i:
                many = dve.value_load(wide[0:1, bass.ds(i, 1)], min_val=0, max_val=1)
                with dve.If(many > 0):
                    dve_item(i, False)
                with dve.Else():
                    dve_item(i, True)
            for j in range(4):
                add_rows(items, j)
            dve.wait_ge(s.h_added, items * 4 + 5)
            mean_squares(4, 0, 2, D, 14)
            dve.wait_ge(s.rstd_ready, 7)
            for t in range(TT):
                dve.scalar_tensor_tensor(out=xn[:, t, :], in0=h[:, t, :], scalar=stat[:, 4 + t:5 + t], in1=gfin,
                                         op0=ALU.mult, op1=ALU.mult).then_inc(s.xn_ready, 1)


_INS = ["x", "positions", "mla_w_in", "mla_g_q", "mla_g_kv", "mla_w_uq", "mla_w_ukv", "mla_w_o", "kv_g", "kv_w", "kv_b",
        "swa_w_q", "swa_b_q", "swa_sinks", "swa_w_o", "swa_b_o", "rel_bias", "g_attn", "g_ffn", "ffn_w_gate", "ffn_w_up",
        "ffn_w_down", "moe_w_router", "moe_w_gate", "moe_w_up", "moe_w_down", "g_final"]


def kernel(**inputs):
    import concourse.bacc as bacc
    from concourse.bass_utils import run_bass_kernel_spmd

    nc = bacc.Bacc("TRN2", target_bir_lowering=False, num_devices=1)
    arrays, args = {}, []
    for name in _INS:
        a = np.ascontiguousarray(inputs[name])
        arrays["in_" + name] = a
        args.append(nc.dram_tensor("in_" + name, a.shape, mybir.dt.from_np(a.dtype), kind="ExternalInput").ap())
    arrays["consts"] = constants()
    args.append(nc.dram_tensor("consts", (P, C_N), F32, kind="ExternalInput").ap())
    args.append(nc.dram_tensor("out_0", (1, S, D), F32, kind="ExternalOutput").ap())
    build(nc, *args)
    r = run_bass_kernel_spmd(nc, [arrays], core_ids=[0])
    return r.results[0]["out_0"]
```

```python
from contextlib import ExitStack

import numpy as np
import concourse.bass as bass
from concourse import mybir

ALU = mybir.AluOpType
ACT = mybir.ActivationFunctionType
AX = mybir.AxisListType
F32 = mybir.dt.float32
I32 = mybir.dt.int32
U32 = mybir.dt.uint32

P = 128
D = 1024
KD = D // P
S = 256
TT = S // P
EPS = 1e-6
NEG = -1e30

MH, NOPE, ROPE, VH = 8, 128, 64, 128
HALF = ROPE // 2
QL, KVL = 384, 256
MLA_SCALE = float((NOPE + ROPE) ** -0.5)

AH, KVH, HD = 16, 2, 64
G = AH // KVH
SWA_SCALE = float(HD ** -0.5)
WINDOW = 128
BUCKETS = 32

DFF = 2816
FC = 512
FCH = (DFF + FC - 1) // FC
NE, DFE = 8, 3584
ECH = DFE // FC

SLOTS = 96
SG_N = SLOTS // 32
NARROW = 64
SWEEPS = -(-S // SLOTS)
ITEMS_MAX = NE * SWEEPS
LASTQ = 256

RING = 7
SLOT = 4096

C_ID, C_TRI, C_ONE, C_MLA, C_WIN, C_IOTA = 0, 128, 256, 384, 768, 1024
C_E8 = C_IOTA + SLOTS
C_THR = C_E8 + NE
C_INV = C_THR + 1
C_MH = C_INV + HALF
C_N = C_MH + TT

V_GA0, V_GF0, V_GA1, V_KVG, V_GQ, V_GKV, V_KVB, V_BQ = 0, 8, 16, 24, 32, 35, 37, 38
V_N = V_BQ + G

MAGIC = 1.5 * 2.0 ** 23
TWO_PI = 2 * np.pi
C1 = float(np.float32(6.28125))
C2 = float(np.float32(np.round((TWO_PI - 6.28125) * 2 ** 20) / 2 ** 20))
C3 = float(np.float32(TWO_PI - 6.28125 - np.round((TWO_PI - 6.28125) * 2 ** 20) / 2 ** 20))
PI_LO = float(np.nextafter(np.float32(np.pi), np.float32(0)))


def constants():
    c = np.zeros((P, C_N), np.float32)
    r = np.arange(P)
    c[:, C_ID:C_ID + P] = np.eye(P)
    c[:, C_TRI:C_TRI + P] = r[:, None] < r[None, :]
    c[:, C_ONE:C_ONE + P] = 1.0
    causal = np.where(r[None, :] <= r[:, None], 0.0, NEG)
    c[:, C_MLA:C_MLA + P] = causal
    c[:, C_MLA + 2 * P:C_MLA + 3 * P] = causal
    c[:, C_WIN:C_WIN + P] = np.where(r[:, None] + P - r[None, :] < WINDOW, 0.0, NEG)
    c[:, C_WIN + P:C_WIN + 2 * P] = causal
    c[:, C_IOTA:C_IOTA + SLOTS] = np.arange(SLOTS)
    c[:, C_E8:C_E8 + NE] = np.arange(NE)
    exact = BUCKETS // 2
    log = [int(np.ceil(exact * 8.0 ** (j / 16) - 1e-9)) for j in range(1, BUCKETS - exact)]
    thr = [-1e9] + list(range(1, exact + 1)) + log
    c[:, C_THR] = np.tile(np.array(thr, np.float32), P // BUCKETS)
    c[:, C_INV:C_INV + HALF] = (10000.0 ** (-np.arange(HALF) / HALF)).astype(np.float32)
    c[:, C_MH:C_MH + TT] = -0.5
    return c


class Semaphores:
    def __init__(self, sem):
        self.consts_loaded = sem("consts_loaded")
        self.x_loaded0 = sem("x_loaded0")
        self.x_loaded1 = sem("x_loaded1")
        self.smalls_loaded = sem("smalls_loaded")
        self.biasrows_loaded = sem("biasrows_loaded")
        self.rel_loaded = sem("rel_loaded")
        self.out_stored = sem("out_stored")
        self.slot0 = sem("slot0")
        self.slot1 = sem("slot1")
        self.slot2 = sem("slot2")
        self.slot3 = sem("slot3")
        self.slot4 = sem("slot4")
        self.slot5 = sem("slot5")
        self.slot6 = sem("slot6")
        self.dve_chain = sem("dve_chain")
        self.act_chain = sem("act_chain")
        self.pool_chain = sem("pool_chain")
        self.vecT_mm = sem("vecT_mm")
        self.vecT_ready = sem("vecT_ready")
        self.ssq_ready = sem("ssq_ready")
        self.ms_ready = sem("ms_ready")
        self.rstd_ready = sem("rstd_ready")
        self.xn_ready = sem("xn_ready")
        self.xT_mm = sem("xT_mm")
        self.xT_ready = sem("xT_ready")
        self.rope_arg = sem("rope_arg")
        self.sincos_ready = sem("sincos_ready")
        self.latq_mm = sem("latq_mm")
        self.latkv_mm = sem("latkv_mm")
        self.cq_ready = sem("cq_ready")
        self.ckv_ready = sem("ckv_ready")
        self.krope_ready = sem("krope_ready")
        self.cT_mm = sem("cT_mm")
        self.cqT_ready = sem("cqT_ready")
        self.ckvT_ready = sem("ckvT_ready")
        self.krT_ready = sem("krT_ready")
        self.qk_mm = sem("qk_mm")
        self.qk_ready = sem("qk_ready")
        self.qrope_mm = sem("qrope_mm")
        self.qrope_ready = sem("qrope_ready")
        self.ukv_v_mm = sem("ukv_v_mm")
        self.v_ready = sem("v_ready")
        self.qrT_mm = sem("qrT_mm")
        self.qrT_ready = sem("qrT_ready")
        self.score_mm = sem("score_mm")
        self.s_ready = sem("s_ready")
        self.negmax_ready = sem("negmax_ready")
        self.exp_ready = sem("exp_ready")
        self.p_ready = sem("p_ready")
        self.pT_mm = sem("pT_mm")
        self.pT_ready = sem("pT_ready")
        self.pv_mm = sem("pv_mm")
        self.oT_ready = sem("oT_ready")
        self.wo_mm = sem("wo_mm")
        self.h_attn0 = sem("h_attn0")
        self.fgu_mm = sem("fgu_mm")
        self.fsg_ready = sem("fsg_ready")
        self.fhh_ready = sem("fhh_ready")
        self.ftr_mm = sem("ftr_mm")
        self.fhhT_ready = sem("fhhT_ready")
        self.fdown_mm = sem("fdown_mm")
        self.fh_added = sem("fh_added")
        self.delta_ready = sem("delta_ready")
        self.onehot_ready = sem("onehot_ready")
        self.bias_mm = sem("bias_mm")
        self.bias_ready = sem("bias_ready")
        self.kT_mm = sem("kT_mm")
        self.kT_ready = sem("kT_ready")
        self.sv_mm = sem("sv_mm")
        self.sv_ready = sem("sv_ready")
        self.sq_mm = sem("sq_mm")
        self.sq_ready = sem("sq_ready")
        self.bo_added = sem("bo_added")
        self.sscore_mm = sem("sscore_mm")
        self.ss_ready = sem("ss_ready")
        self.snegmax_ready = sem("snegmax_ready")
        self.sexp_ready = sem("sexp_ready")
        self.esink_ready = sem("esink_ready")
        self.sp_ready = sem("sp_ready")
        self.spT_mm = sem("spT_mm")
        self.spT_ready = sem("spT_ready")
        self.spv_mm = sem("spv_mm")
        self.soT_ready = sem("soT_ready")
        self.swo_mm = sem("swo_mm")
        self.h_attn1 = sem("h_attn1")
        self.router_mm = sem("router_mm")
        self.route_mask = sem("route_mask")
        self.gate_arg = sem("gate_arg")
        self.gate_exp = sem("gate_exp")
        self.route_cum_mm = sem("route_cum_mm")
        self.counts_ready = sem("counts_ready")
        self.gu_mm = sem("gu_mm")
        self.sg_ready = sem("sg_ready")
        self.hh_ready = sem("hh_ready")
        self.tr_mm = sem("tr_mm")
        self.hhT_ready = sem("hhT_ready")
        self.down_mm = sem("down_mm")
        self.y_ready_a = sem("y_ready_a")
        self.y_ready_v = sem("y_ready_v")
        self.y_last = sem("y_last")
        self.sel_ready = sem("sel_ready")
        self.gath_mm = sem("gath_mm")
        self.xgT_ready_a = sem("xgT_ready_a")
        self.xgT_ready_v = sem("xgT_ready_v")
        self.selg_ready = sem("selg_ready")
        self.sgt_mm = sem("sgt_mm")
        self.sgt_ready = sem("sgt_ready")
        self.scat_mm = sem("scat_mm")
        self.h_added = sem("h_added")


def build(nc, x, positions, w_in, g_q, g_kv, w_uq, w_ukv, w_o, kv_g, kv_w, kv_b, swa_w_q, swa_b_q,
          swa_sinks, swa_w_o, swa_b_o, rel_bias, g_attn, g_ffn, f_gate, f_up, f_down, w_router,
          e_gate, e_up, e_down, g_final, consts, out):
    with ExitStack() as ctx:
        def sb(name, shape, dt=F32):
            return ctx.enter_context(nc.sbuf_tensor(name, shape, dt))

        ps = ctx.enter_context(nc.psum_tensor("ps", [P, 8, 512], F32))
        s = Semaphores(lambda name: ctx.enter_context(nc.semaphore(name)))
        slot_landed = [s.slot0, s.slot1, s.slot2, s.slot3, s.slot4, s.slot5, s.slot6]

        ring = sb("ring", [P, RING, SLOT])
        h = sb("h", [P, TT, D])
        xn = sb("xn", [P, TT, D])
        xT = sb("xT", [P, KD, S])
        xT2 = sb("xT2", [P, KD, S])
        arena = sb("arena", [P, 12288])
        cst = sb("cst", [P, C_N])
        vecs = sb("vecs", [V_N, P])
        vecT = sb("vecT", [P, V_N])
        pos_i = sb("pos_i", [P, TT], I32)
        pos_f = sb("pos_f", [P, TT])
        stat = sb("stat", [P, 16])
        wr = sb("wr", [P, KD, NE])
        kvb_row = sb("kvb_row", [1, P])
        sinks_h = sb("sinks_h", [P, AH])
        sinks = sb("sinks", [P, AH])
        n_items = sb("n_items", [P, 2], I32)
        wide = sb("wide", [P, ITEMS_MAX], I32)
        slots = sb("slots", [P, TT, ITEMS_MAX + 1])
        gates = sb("gates", [P, TT, ITEMS_MAX + 1])
        rt = sb("rt", [P, TT, 72])
        ridx = sb("ridx", [P, TT, 8], U32)

        ident = cst[:, C_ID:C_ID + P]

        def gcol(base, k):
            return vecT[:, base + k:base + k + 1]

        used = [0]

        def carve(n, pattern=None, **dims):
            v = arena[:, used[0]:used[0] + n]
            used[0] += n
            return v.rearrange(pattern, **dims) if pattern else v

        cq = carve(TT * QL, "p (t n) -> p t n", t=TT)
        ckv = carve(TT * KVL, "p (t n) -> p t n", t=TT)
        cqT = carve(3 * S, "p (k n) -> p k n", k=3)
        ckvT = carve(2 * S, "p (k n) -> p k n", k=2)
        qT = carve(MH * S, "p (k n) -> p k n", k=MH)
        qr = carve(TT * MH * ROPE, "p (t n) -> p t n", t=TT)
        qrT = carve(4 * S, "p (k n) -> p k n", k=4)
        krT = carve(S)
        kr = carve(TT * P, "p (t n) -> p t n", t=TT)
        probs = carve(MH * 3 * P, "p (k n) -> p k n", k=MH)
        pT = carve(2 * 3 * P, "p (k n) -> p k n", k=2)
        cosn = carve(TT * 2 * HALF, "p (t n) -> p t n", t=TT)
        ang = carve(6 * TT * HALF, "p (a t n) -> p a t n", a=6, t=TT)
        rtmp = carve(2 * MH * HALF, "p (a n) -> p a n", a=2)
        mstat = carve(MH * 8, "p (k n) -> p k n", k=MH)
        kT = xn[:].rearrange("p t n -> p (t n)").rearrange("p (k n) -> p k n", k=MH)
        v_rows = xT[:].rearrange("p k n -> p (k n)").rearrange("p (t n) -> p t n", t=TT)
        oT = xT2
        used[0] = 0
        fhhT = carve(2 * 4 * S, "p (a j n) -> p a j n", a=2, j=4)
        fhh = carve(2 * FC, "p (a n) -> p a n", a=2)
        fsg = carve(2 * FC, "p (a n) -> p a n", a=2)
        bias0 = carve(AH * P, "p (k n) -> p k n", k=AH)
        bias1 = carve(AH * S, "p (k n) -> p k n", k=AH)
        onehot = carve(2 * 2 * S, "p (a j n) -> p a j n", a=2, j=2)
        posq_i = sb("posq_i", [P, S], I32)
        posq = sb("posq", [P, S])
        posk_i = sb("posk_i", [P, 64], I32)
        posk = sb("posk", [P, 64])
        tabs_h = sb("tabs_h", [P, 2, 64])
        tabs = sb("tabs", [P, 64])
        used[0] = 0
        Q_BANK = (0, 5, 5, 5)
        sqT = carve(G * S, "p (k n) -> p k n", k=G)
        skT = carve(S)
        sv = carve(TT * P, "p (t n) -> p t n", t=TT)
        spT = carve(2 * 3 * P, "p (k n) -> p k n", k=2)
        assert used[0] <= 4096
        used[0] = 4096 + AH * 3 * P
        sstat = carve(8 * 2 * AH, "p (a b n) -> p a b n", a=8, b=2)
        soT = xT2
        bo_row = xn[:, 0, :]
        used[0] = 0
        sel = carve(TT * SLOTS, "p (t n) -> p t n", t=TT)
        selg = carve(TT * SLOTS, "p (t n) -> p t n", t=TT)
        sgt = carve(TT * P, "p (t n) -> p t n", t=TT)
        xgT = carve(KD * SLOTS, "p (k n) -> p k n", k=KD)
        hh = carve(2 * FC, "p (a n) -> p a n", a=2)
        sg = carve(2 * FC, "p (a n) -> p a n", a=2)
        upl = carve(2 * FC, "p (a n) -> p a n", a=2)
        hhT = carve(2 * 4 * SLOTS, "p (a j n) -> p a j n", a=2, j=4)
        ysb = carve(D)
        grow = carve(D)
        gfin = carve(D)
        assert used[0] <= 12288

        BIAS_ROUNDS = S // 8

        def bias_rounds(u):
            return range(min(4 * max(u - 1, 0), BIAS_ROUNDS), min(4 * u, BIAS_ROUNDS))

        def rows_of(w):
            return w.rearrange("(k p) n -> p k n", p=P)

        def slot_view(n, k):
            sl = (n + RING_OFF) % RING
            return lambda cols: ring[:, sl, 0:k * cols].rearrange("p (k n) -> p k n", k=k)

        RING_OFF = 5
        win, wuq, wukv, wo = (rows_of(w[0]) for w in (w_in, w_uq, w_ukv, w_o))
        fg, fu, fd = (rows_of(w[0]) for w in (f_gate, f_up, f_down))
        kvw, swq, swo = rows_of(kv_w), rows_of(swa_w_q[0]), rows_of(swa_w_o[0])
        stream = [
            ("win_q", win[:, :, 0:QL], KD, QL, s.latq_mm, 2),
            ("win_kv", win[:, :, QL:QL + KVL + ROPE], KD, KVL + ROPE, s.latkv_mm, 2),
            ("uq0", wuq[:, :, 0:768], 3, 768, s.qrope_mm, 2),
            ("uq1", wuq[:, :, 768:1536], 3, 768, s.qrope_mm, 4),
            ("ukv", wukv, 2, 2048, s.ukv_v_mm, 4),
            ("wo0", wo[:, :, 0:512], KD, 512, s.wo_mm, 4),
            ("wo1", wo[:, :, 512:1024], KD, 512, s.wo_mm, 4),
        ]

        def f_cols(c):
            return min(FC, DFF - c * FC)

        def ffn_gu(c):
            n = f_cols(c)
            return [("fg%d" % c, fg[:, :, c * FC:c * FC + n], KD, n, s.fgu_mm, 2 * c + 2),
                    ("fu%d" % c, fu[:, :, c * FC:c * FC + n], KD, n, s.fgu_mm, 2 * c + 2)]

        downs = [(c, t, half) for c in range(FCH - 2) for t in range(TT) for half in range(2)]
        downs += [(c, t, half) for t in range(TT) for c in (FCH - 2, FCH - 1) for half in range(2)]

        def ffn_d(c):
            last = max(n for n, d in enumerate(downs) if d[0] == c)
            return [("fd%d" % c, fd[:, 4 * c:4 * c + f_cols(c) // P, :], f_cols(c) // P, D, s.fdown_mm, last + 1)]

        stream += ffn_gu(0)
        for c in range(1, FCH):
            stream += ffn_gu(c) + ffn_d(c - 1)
        stream += ffn_d(FCH - 1)
        stream += [
            ("kvw", kvw, KD, 256, s.sv_mm, 2),
            ("wq0", swq[:, 0:4, :], 4, D, s.sq_mm, 4),
            ("wq1", swq[:, 4:8, :], 4, D, s.sq_mm, 4),
            ("swo0", swo[:, :, 0:512], KD, 512, s.swo_mm, 4),
            ("swo1", swo[:, :, 512:1024], KD, 512, s.swo_mm, 4),
        ]
        DENSE = len(stream)
        assert (DENSE + RING_OFF) % RING == 0
        where = {t[0]: n for n, t in enumerate(stream)}

        def fills(n):
            v = n + RING_OFF
            return v // RING + (1 if v % RING >= RING_OFF else 0)

        def w_of(name):
            n = where[name]
            _, _, k, cols, _, _ = stream[n]
            return slot_view(n, k)(cols)

        def weights_here(eng, name):
            n = where[name]
            eng.wait_ge(slot_landed[(n + RING_OFF) % RING], 16 * fills(n))

        pieces = [("g", 0), ("u", 0), ("g", 1), ("u", 1)]
        for c in range(2, ECH):
            pieces += [("g", c), ("u", c), ("d", c - 2)]
        pieces += [("d", ECH - 2), ("d", ECH - 1)]
        NP = len(pieces)
        assert NP % RING == 0
        ppos = {p_: m for m, p_ in enumerate(pieces)}
        base_fill = (DENSE + RING_OFF) // RING

        def piece_here(eng, i, kind, c):
            m = ppos[(kind, c)]
            extra = 1 if m % RING >= RING_OFF else 0
            eng.wait_ge(slot_landed[m % RING], i * (16 * NP // RING) + 16 * (base_fill + m // RING + extra))

        def piece(kind, c):
            sl = ppos[(kind, c)] % RING
            return ring[:, sl, :].rearrange("p (k n) -> p k n", k=4 if kind == "d" else KD)

        eg = e_gate[0].rearrange("e (k p) f -> p e k f", p=P)
        eu = e_up[0].rearrange("e (k p) f -> p e k f", p=P)
        ed = e_down[0].rearrange("e (k p) n -> p e k n", p=P)

        block = ctx.enter_context(nc.Block())

        @block.sync
        def _(sp):
            for t, landed in enumerate((s.x_loaded0, s.x_loaded1)):
                sp.dma_start(h[:, t, :], x[0, t * P:(t + 1) * P, :]).then_inc(landed, 16)
            loads = [
                (vecs[V_GA0:V_GA0 + 8, :], g_attn[0].rearrange("(k n) -> k n", n=P)),
                (vecs[V_GF0:V_GF0 + 8, :], g_ffn[0].rearrange("(k n) -> k n", n=P)),
                (vecs[V_GA1:V_GA1 + 8, :], g_attn[1].rearrange("(k n) -> k n", n=P)),
                (vecs[V_KVG:V_KVG + 8, :], kv_g.rearrange("(k n) -> k n", n=P)),
                (vecs[V_GQ:V_GQ + 3, :], g_q[0].rearrange("(k n) -> k n", n=P)),
                (vecs[V_GKV:V_GKV + 2, :], g_kv[0].rearrange("(k n) -> k n", n=P)),
                (vecs[V_KVB:V_KVB + 1, :], kv_b[0:P].rearrange("(k n) -> k n", n=P)),
                (vecs[V_BQ:V_BQ + G, 0:HD], swa_b_q[0, 0:512].rearrange("(k n) -> k n", n=HD)),
                (vecs[V_BQ:V_BQ + G, HD:P], swa_b_q[0, 512:1024].rearrange("(k n) -> k n", n=HD)),
                (pos_i[:], positions[0].rearrange("(t p) -> p t", p=P)),
            ]
            sp.dma_start(cst[:], consts).then_inc(s.consts_loaded, 16)
            for dst, src in loads:
                sp.dma_start(dst, src, allow_slow_non_contiguous=dst.dtype == I32).then_inc(s.smalls_loaded, 16)
            for n, (name, src, k, cols, _, _) in enumerate(stream):
                if n >= RING:
                    sp.wait_ge(stream[n - RING][4], stream[n - RING][5])
                sl = (n + RING_OFF) % RING
                sp.dma_start(slot_view(n, k)(cols), src).then_inc(slot_landed[sl], 16)

            def load_item(i, expert, first):
                for m, (kind, c) in enumerate(pieces):
                    if m < RING:
                        if first:
                            old = stream[DENSE - RING + m]
                            sp.wait_ge(old[4], old[5])
                        else:
                            k0, c0 = pieces[m - RING + NP]
                            sp.wait_ge(s.down_mm if k0 == "d" else s.gu_mm, i * ECH + (c0 + 2 - ECH))
                    else:
                        k0, c0 = pieces[m - RING]
                        sp.wait_ge(s.down_mm if k0 == "d" else s.gu_mm, i * ECH + (c0 + 2))
                    if kind == "d":
                        src = ed[:, expert, 4 * c:4 * c + 4, :]
                    else:
                        src = (eg if kind == "g" else eu)[:, expert, :, c * FC:(c + 1) * FC]
                    sp.dma_start(piece(kind, c), src).then_inc(slot_landed[m % RING], 16)

            load_item(0, 0, True)
            with sp.Fori(1, NE) as i:
                load_item(i, i, False)
            sp.wait_ge(s.counts_ready, 1)
            items = sp.value_load(n_items[0:1, 0:1], min_val=NE, max_val=ITEMS_MAX)
            for sweep in range(1, SWEEPS):
                with sp.If(items > sweep * NE):
                    with sp.Fori(0, NE) as e:
                        load_item(e + sweep * NE, e, False)
                with sp.Else():
                    sp.nop()
            sp.wait_ge(s.out_stored, 32)

        @block.gpsimd
        def _(pool):
            more = [
                (posq_i[:], positions[0:1, :].to_broadcast([P, S])),
                (kvb_row[:], kv_b[P:2 * P].rearrange("(a n) -> a n", a=1)),
                (wr[:], w_router[0].rearrange("(k p) e -> p k e", p=P)),
                (sinks_h[:], swa_sinks[0:1, :].to_broadcast([P, AH])),
            ]
            for kk in range(4):
                more.append((posk_i[32 * kk:32 * kk + 32, :], positions[0:1, 64 * kk:64 * kk + 64].to_broadcast([32, 64])))
            for dst, src in more:
                pool.dma_start(dst, src).then_inc(s.biasrows_loaded, 16)

            done = [0]

            def rstd(dst, src, n=1):
                done[0] += 1
                pool.wait_ge(s.ms_ready, done[0])
                nc.gpsimd.tensor_tensor(stat[:, dst:dst + n], stat[:, src:src + n], cst[:, C_MH:C_MH + n], ALU.pow).then_inc(s.rstd_ready, 1)

            def rstd_rows():
                for t in range(TT):
                    rstd(4 + t, 2 + t)

            pool.wait_ge(s.consts_loaded, 16)
            rstd_rows()
            nc.gpsimd.memset(tabs_h[:], 0.0).then_inc(s.pool_chain, 1)
            pool.wait_ge(s.pool_chain, 1)
            for kk in range(4):
                c = slice(AH * kk, AH * kk + AH)
                pool.dma_start(tabs_h[32 * kk:32 * kk + 32, 0, c], rel_bias).then_inc(s.rel_loaded, 16)
                pool.dma_start(tabs_h[32 * kk + 1:32 * kk + 32, 1, c], rel_bias[0:31, :]).then_inc(s.rel_loaded, 16)
            rstd(12, 8, 2)
            rstd(14, 10, 2)
            rstd_rows()
            rstd_rows()
            pool.wait_ge(s.sv_mm, 2)
            pool.dma_start(bo_row, swa_b_o[0:1, :].to_broadcast([P, D])).then_inc(s.rel_loaded, 16)
            pool.wait_ge(s.rel_loaded, 16 * 9)
            pool.wait_ge(s.xn_ready, 6)
            for t in range(TT):
                nc.gpsimd.tensor_tensor(h[:, t, :], h[:, t, :], bo_row, ALU.add).then_inc(s.bo_added, 1)
            pool.wait_ge(s.soT_ready, AH)
            pool.dma_start(grow, g_ffn[1:2, :].to_broadcast([P, D])).then_inc(s.rel_loaded, 16)
            pool.dma_start(gfin, g_final.rearrange("(a n) -> a n", a=1).to_broadcast([P, D])).then_inc(s.rel_loaded, 16)
            rstd_rows()
            rstd_rows()

        @block.scalar
        def _(act):
            def squares(t):
                act.activation(xn[:, t, :], h[:, t, :], ACT.Square, accum_out=stat[:, t:t + 1]).then_inc(s.ssq_ready, 1)

            act.wait_ge(s.x_loaded0, 16)
            squares(0)
            act.wait_ge(s.x_loaded1, 16)
            squares(1)
            act.wait_ge(s.vecT_mm, 1)
            act.copy(vecT[:], ps[:, 0, 0:V_N]).then_inc(s.vecT_ready, 1)
            act.wait_ge(s.rope_arg, 2)
            act.activation(cosn[:, :, HALF:2 * HALF], ang[:, 4], ACT.Sin).then_inc(s.sincos_ready, 1)
            act.activation(cosn[:, :, 0:HALF], ang[:, 5], ACT.Sin).then_inc(s.sincos_ready, 1)

            for t in range(TT):
                act.wait_ge(s.latq_mm, t + 1)
                act.activation(cq[:, t, :], ps[:, 4 + t, 0:QL], ACT.Square, accum_out=stat[:, t:t + 1]).then_inc(s.ssq_ready, 1)
            for t in range(TT):
                act.wait_ge(s.latkv_mm, t + 1)
                act.activation(ckv[:, t, :], ps[:, 6 + t, 0:KVL], ACT.Square, accum_out=stat[:, 6 + t:7 + t]).then_inc(s.ssq_ready, 1)
            act.wait_ge(s.cT_mm, 2)
            for k in range(2):
                act.activation(ckvT[:, k, :], ps[:, 2, k * S:(k + 1) * S], ACT.Copy, scale=gcol(V_GKV, k)).then_inc(s.ckvT_ready, 1)
            act.wait_ge(s.cT_mm, 3)
            act.copy(krT, ps[:, 3, 0:S]).then_inc(s.krT_ready, 1)
            for u in range(8):
                act.wait_ge(s.qk_mm, u + 1)
                dst = qT if u < 4 else kT
                act.copy(dst[:, 2 * (u % 4):2 * (u % 4) + 2, :], ps[:, 6 + u % 2, :].rearrange("p (k n) -> p k n", k=2)).then_inc(s.qk_ready, 1)
            for n in range(4):
                t, half = n // 2, n % 2
                act.wait_ge(s.ukv_v_mm, n + 1)
                act.copy(v_rows[:, t, half * 512:(half + 1) * 512], ps[:, n, :]).then_inc(s.v_ready, 1)
            for i in range(MH + 1):
                if i < MH:
                    act.wait_ge(s.negmax_ready, 2 * i + 2)
                    st = mstat[:, i, :]
                    act.activation(probs[:, i, 0:P], probs[:, i, 0:P], ACT.Exp, scale=MLA_SCALE, bias=st[:, 2:3],
                                   accum_out=st[:, 4:5]).then_inc(s.exp_ready, 1)
                    act.activation(probs[:, i, P:3 * P], probs[:, i, P:3 * P], ACT.Exp, scale=MLA_SCALE, bias=st[:, 3:4],
                                   accum_out=st[:, 5:6]).then_inc(s.exp_ready, 1)
                if i >= 1:
                    act.wait_ge(s.pT_mm, i)
                    if i >= 3:
                        act.wait_ge(s.pv_mm, i - 2)
                    act.copy(pT[:, (i - 1) % 2, :], ps[:, 4 + (i - 1) % 2, 0:3 * P]).then_inc(s.pT_ready, 1)
            for t in range(TT):
                act.wait_ge(s.h_attn0, 2 * t + 2)
                squares(t)
            for u in range(2 * FCH + 1):
                if u < 2 * FCH:
                    n = f_cols(u // 2)
                    act.wait_ge(s.fgu_mm, u + 1)
                    if u >= 2:
                        act.wait_ge(s.fhh_ready, u - 1)
                    act.activation(fsg[:, u % 2, 0:n], ps[:, 2 * (u % 2), 0:n], ACT.Silu).then_inc(s.fsg_ready, 1)
                if u >= 1:
                    c, t, n = (u - 1) // 2, (u - 1) % 2, f_cols((u - 1) // 2)
                    act.wait_ge(s.ftr_mm, u)
                    if c >= 2:
                        act.wait_ge(s.fdown_mm, 4 * (c - 1))
                    act.copy(fhhT[:, c % 2, 0:n // P, t * P:(t + 1) * P],
                             ps[:, 4, 0:n].rearrange("p (j n) -> p j n", n=P)).then_inc(s.fhhT_ready, 1)
            for t in range(TT):
                act.wait_ge(s.fh_added, 4 * FCH - 4 * (TT - 1 - t))
                squares(t)
            act.wait_ge(s.kT_mm, 2)
            act.activation(skT, ps[:, 4, 0:S], ACT.Identity, bias=gcol(V_KVB, 0)).then_inc(s.kT_ready, 1)
            for t in range(TT):
                act.wait_ge(s.sv_mm, t + 1)
                act.copy(sv[:, t, :], ps[:, 7 if t == 0 else 5, 0:P]).then_inc(s.sv_ready, 1)

            def sq_evac(u):
                act.wait_ge(s.sq_mm, u + 1)
                for j in range(2):
                    g = 2 * u + j
                    act.activation(sqT[:, g, :], ps[:, Q_BANK[u], j * S:(j + 1) * S], ACT.Identity, bias=gcol(V_BQ, g)).then_inc(s.sq_ready, 1)

            def sexp(i):
                act.wait_ge(s.snegmax_ready, i // 4 + 1)
                if i % 4 == 0:
                    act.activation(sstat[:, 3, :, i:i + 4], sstat[:, 2, :, i:i + 4], ACT.Exp).then_inc(s.esink_ready, 1)
                act.activation(bias0[:, i, :], bias0[:, i, :], ACT.Exp, bias=sstat[:, 1, 0, i:i + 1],
                               accum_out=sstat[:, 4, 0, i:i + 1]).then_inc(s.sexp_ready, 1)
                act.activation(bias1[:, i, :], bias1[:, i, :], ACT.Exp, bias=sstat[:, 1, 1, i:i + 1],
                               accum_out=sstat[:, 4, 1, i:i + 1]).then_inc(s.sexp_ready, 1)

            def spT_evac(i):
                act.wait_ge(s.spT_mm, i + 1)
                if i >= 2:
                    act.wait_ge(s.spv_mm, i - 1)
                act.copy(spT[:, i % 2, :], ps[:, i % 2, 0:3 * P]).then_inc(s.spT_ready, 1)

            def swa_out(i):
                g, v = i // 2, i % 2
                part = 64 * (g % 2)
                act.wait_ge(s.spv_mm, i + 1)
                act.copy(soT[part:part + 64, 4 * v + g // 2, :], ps[part:part + 64, 6 + i % 2, 0:S]).then_inc(s.soT_ready, 1)

            sq_evac(0)
            sq_evac(1)
            for q in range(5):
                if 1 <= q < 3:
                    sq_evac(q + 1)
                for j in range(4):
                    if q < 4:
                        sexp(4 * q + j)
                    if q >= 1:
                        i = 4 * (q - 1) + j
                        spT_evac(i)
                        if i >= 1:
                            swa_out(i - 1)
            swa_out(AH - 1)
            for t in range(TT):
                act.wait_ge(s.h_attn1, 2 * t + 2)
                squares(t)
            act.wait_ge(s.gate_arg, 1)
            act.activation(rt[:, :, 49:50], rt[:, :, 48:49], ACT.Exp).then_inc(s.gate_exp, 1)

            def silu_and_last(i, c, narrow):
                a = c % 2
                act.wait_ge(s.gu_mm, i * ECH + (c + 2))
                act.wait_ge(s.hh_ready, i * (2 * ECH) + (2 * max(c - 1, 0) + 1))
                if narrow:
                    act.activation(sg[0:NARROW, a, :], ps[0:NARROW, 2 * a, :], ACT.Silu).then_inc(s.sg_ready, 1)
                    act.copy(upl[0:NARROW, a, :], ps[64:64 + NARROW, 2 * a + 1, :]).then_inc(s.sg_ready, 3)
                    return
                act.activation(sg[0:SLOTS, a, :], ps[0:SLOTS, 2 * a, :], ACT.Silu).then_inc(s.sg_ready, 1)
                for g in range(SG_N):
                    src = ps[96:128, 2 * a + g // 2, (g % 2) * LASTQ:(g % 2 + 1) * LASTQ]
                    act.copy(upl[32 * g:32 * g + 32, a, 0:LASTQ], src).then_inc(s.sg_ready, 1)

            def hhT_evac(i, c, narrow):
                act.wait_ge(s.tr_mm, i * ECH + (c + 2))
                act.wait_ge(s.down_mm, i * ECH + (max(c - 1, 0) + 1))
                m = NARROW if narrow else SLOTS
                act.copy(hhT[:, c % 2, :, 0:m], ps[:, 4, 0:4 * SLOTS].rearrange("p (j n) -> p j n", j=4)[:, :, 0:m]).then_inc(s.hhT_ready, 1)

            act.sem_inc(s.sg_ready, 1)
            act.sem_inc(s.hhT_ready, 1)
            act.sem_inc(s.y_ready_a, 1)
            act.sem_inc(s.sgt_ready, 1)
            act.wait_ge(s.gath_mm, 2)
            act.copy(xgT[:, 4:8, :].rearrange("p k n -> p (k n)"), ps[:, 3, 0:4 * SLOTS]).then_inc(s.xgT_ready_a, 2)
            act.wait_ge(s.counts_ready, 1)
            items = act.value_load(n_items[0:1, 0:1], min_val=NE, max_val=ITEMS_MAX)

            def act_item(i, narrow):
                for c in range(ECH):
                    silu_and_last(i, c, narrow)
                    if c == 4:
                        act.wait_ge(s.sgt_mm, i + 2)
                        act.copy(sgt[0:SLOTS].rearrange("p t n -> p (t n)"), ps[0:SLOTS, 7, 0:S]).then_inc(s.sgt_ready, 1)
                    if c >= 1:
                        hhT_evac(i, c - 1, narrow)
                act.wait_ge(s.gath_mm, i + 3)
                act.copy(xgT[:, 4:8, :].rearrange("p k n -> p (k n)"), ps[:, 3, 0:4 * SLOTS]).then_inc(s.xgT_ready_a, 1)
                hhT_evac(i, ECH - 1, narrow)
                act.wait_ge(s.down_mm, i * ECH + (ECH + 1))
                if narrow:
                    act.copy(ysb[0:NARROW, 0:512], ps[0:NARROW, 5, :]).then_inc(s.y_ready_a, 1)
                    return
                for g in range(2):
                    act.copy(ysb[32 * g:32 * g + 32, 768:1024], ps[96:128, 5, g * LASTQ:(g + 1) * LASTQ]).then_inc(s.act_chain, 1)
                act.copy(ysb[0:SLOTS, 0:512], ps[0:SLOTS, 5, :]).then_inc(s.y_ready_a, 1)

            with act.Fori(0, items) as i:
                many = act.value_load(wide[0:1, bass.ds(i, 1)], min_val=0, max_val=1)
                with act.If(many > 0):
                    act_item(i, False)
                with act.Else():
                    act_item(i, True)
            for t in range(TT):
                act.wait_ge(s.h_added, items * 4 + (2 * t + 3))
                act.activation(xT[:].rearrange("p k n -> p (k n)")[:, t * D:(t + 1) * D], h[:, t, :], ACT.Square,
                               accum_out=stat[:, t:t + 1]).then_inc(s.ssq_ready, 1)
            orow = out[0].rearrange("(t p) d -> t p d", p=P)
            for t in range(TT):
                act.wait_ge(s.xn_ready, 9 + t)
                act.dma_start(orow[t], xn[:, t, :]).then_inc(s.out_stored, 16)

        @block.tensor
        def _(pe):
            def rows_to_T(n, t, off):
                pe.wait_ge(s.xn_ready, 2 * n + t + 1)
                for k in range(KD):
                    mm = pe.transpose(ps[:, off + 2 * t + k // 4, (k % 4) * P:(k % 4 + 1) * P], xn[:, t, k * P:(k + 1) * P], ident)
                mm.then_inc(s.xT_mm, 1)

            pe.wait_ge(s.consts_loaded, 16)
            pe.wait_ge(s.smalls_loaded, 160)
            pe.transpose(ps[:, 0, 0:V_N], vecs[:], ident[0:V_N, 0:V_N]).then_inc(s.vecT_mm, 1)
            pe.wait_ge(s.vecT_ready, 1)
            rows_to_T(0, 0, 0)
            rows_to_T(0, 1, 0)
            for name, bank, n, sem in (("win_q", 4, QL, s.latq_mm), ("win_kv", 6, KVL + ROPE, s.latkv_mm)):
                weights_here(pe, name)
                w = w_of(name)
                for t in range(TT):
                    pe.wait_ge(s.xT_ready, 2 * t + 2)
                    for k in range(KD):
                        mm = pe.matmul(ps[:, bank + t, 0:n], xT[:, k, t * P:(t + 1) * P], w[:, k, :],
                                       start=(k == 0), stop=(k == KD - 1))
                    mm.then_inc(sem, 1)
            pe.wait_ge(s.cq_ready, 2)
            for k in range(3):
                for t in range(TT):
                    mm = pe.transpose(ps[:, k // 2, (k % 2) * S + t * P:(k % 2) * S + (t + 1) * P],
                                      cq[:, t, k * P:(k + 1) * P], ident)
            mm.then_inc(s.cT_mm, 1)
            pe.wait_ge(s.ckv_ready, 2)
            for k in range(2):
                for t in range(TT):
                    mm = pe.transpose(ps[:, 2, k * S + t * P:k * S + (t + 1) * P], ckv[:, t, k * P:(k + 1) * P], ident)
            mm.then_inc(s.cT_mm, 1)
            pe.wait_ge(s.krope_ready, 2)
            for t in range(TT):
                mm = pe.transpose(ps[:, 3, t * P:(t + 1) * P], kr[:, t, :], ident)
            mm.then_inc(s.cT_mm, 1)
            pe.wait_ge(s.cqT_ready, 3)
            for half in range(2):
                weights_here(pe, "uq%d" % half)
                w = w_of("uq%d" % half)
                for u in (2 * half, 2 * half + 1):
                    if u >= 2:
                        pe.wait_ge(s.qk_ready, u - 1)
                    for j in range(2):
                        hl = 2 * (u % 2) + j
                        for k in range(3):
                            mm = pe.matmul(ps[:, 6 + u % 2, j * S:(j + 1) * S], w[:, k, hl * 192:hl * 192 + NOPE], cqT[:, k, :],
                                           start=(k == 0), stop=(k == 2))
                    mm.then_inc(s.qk_mm, 1)
                for t in range(TT):
                    for k in range(3):
                        r = w[:, k, :].rearrange("p (h n) -> p h n", n=192)[:, :, NOPE:192]
                        mm = pe.matmul(ps[:, 4 + t, half * S:(half + 1) * S], cqT[:, k, t * P:(t + 1) * P], r,
                                       start=(k == 0), stop=(k == 2))
                    mm.then_inc(s.qrope_mm, 1)
            pe.wait_ge(s.ckvT_ready, 2)
            weights_here(pe, "ukv")
            w = w_of("ukv")
            for u in range(4, 8):
                pe.wait_ge(s.qk_ready, u - 1)
                for j in range(2):
                    hd = 2 * (u - 4) + j
                    for k in range(2):
                        mm = pe.matmul(ps[:, 6 + u % 2, j * S:(j + 1) * S], w[:, k, hd * 256:hd * 256 + NOPE], ckvT[:, k, :],
                                       start=(k == 0), stop=(k == 1))
                mm.then_inc(s.qk_mm, 1)
            pe.wait_ge(s.krT_ready, 1)
            for n in range(4):
                t, half = n // 2, n % 2
                for k in range(2):
                    r = w[:, k, :].rearrange("p (h n) -> p h n", n=256)[:, 4 * half:4 * half + 4, NOPE:256]
                    mm = pe.matmul(ps[:, n, :], ckvT[:, k, t * P:(t + 1) * P], r, start=(k == 0), stop=(k == 1))
                mm.then_inc(s.ukv_v_mm, 1)
            pe.wait_ge(s.qrope_ready, 4)
            for k in range(4):
                for t in range(TT):
                    mm = pe.transpose(ps[:, 4 + k // 2, (k % 2) * S + t * P:(k % 2) * S + (t + 1) * P],
                                      qr[:, t, k * P:(k + 1) * P], ident)
            mm.then_inc(s.qrT_mm, 1)

            def scores(i):
                b, part = i % 4, 64 * (i % 2)
                if i >= 4:
                    pe.wait_ge(s.s_ready, i - 3)
                for t, c0, n in ((0, 0, P), (1, P, 2 * P)):
                    pe.matmul(ps[:, b, c0:c0 + n], qT[:, i, t * P:(t + 1) * P], kT[:, i, 0:n], start=True, stop=False)
                    mm = pe.matmul(ps[:, b, c0:c0 + n], qrT[part:part + 64, i // 2, t * P:(t + 1) * P], krT[part:part + 64, 0:n],
                                   start=False, stop=True)
                mm.then_inc(s.score_mm, 1)

            def probs_T(i):
                pe.wait_ge(s.p_ready, 2 * i + 2)
                if i >= 2:
                    pe.wait_ge(s.pT_ready, i - 1)
                for b in range(3):
                    mm = pe.transpose(ps[:, 4 + i % 2, b * P:(b + 1) * P], probs[:, i, b * P:(b + 1) * P], ident)
                mm.then_inc(s.pT_mm, 1)

            def pv(i):
                pe.wait_ge(s.pT_ready, i + 1)
                if i >= 2:
                    pe.wait_ge(s.oT_ready, i - 1)
                o = ps[:, 6 + i % 2, :]
                v0, v1 = (v_rows[:, t, i * VH:(i + 1) * VH] for t in range(TT))
                pe.matmul(o[:, 0:P], v0, pT[:, i % 2, 0:P], start=True, stop=True)
                pe.matmul(o[:, P:S], v0, pT[:, i % 2, P:S], start=True, stop=False)
                pe.matmul(o[:, P:S], v1, pT[:, i % 2, S:3 * P], start=False, stop=True).then_inc(s.pv_mm, 1)

            pe.wait_ge(s.qk_ready, 8)
            pe.wait_ge(s.v_ready, 4)
            pe.wait_ge(s.qrT_ready, 4)
            for i in range(4):
                scores(i)
            for i in range(MH + 1):
                if i < MH:
                    probs_T(i)
                if i >= 1:
                    pv(i - 1)
                if i + 4 < MH:
                    scores(i + 4)
            pe.wait_ge(s.oT_ready, MH)
            weights_here(pe, "wo0")
            weights_here(pe, "wo1")

            def out_product(name, T, t, half, sem):
                w = w_of("%s%d" % (name, half))
                for k in range(KD):
                    mm = pe.matmul(ps[:, 2 * t + half, :], T[:, k, t * P:(t + 1) * P], w[:, k, :], start=(k == 0), stop=(k == KD - 1))
                mm.then_inc(sem, 1)

            out_product("wo", oT, 0, 0, s.wo_mm)
            out_product("wo", oT, 0, 1, s.wo_mm)
            out_product("wo", oT, 1, 0, s.wo_mm)
            rows_to_T(1, 0, 4)
            out_product("wo", oT, 1, 1, s.wo_mm)

            def ffn_products(c, t):
                u, n = 2 * c + t, f_cols(c)
                if c == 0:
                    pe.wait_ge(s.xT_ready, 6 + 2 * t)
                weights_here(pe, "fg%d" % c)
                weights_here(pe, "fu%d" % c)
                if u >= 2:
                    pe.wait_ge(s.fhh_ready, u - 1)
                rounds = list(bias_rounds(u))
                for b, name in ((0, "fg%d" % c), (1, "fu%d" % c)):
                    w = w_of(name)
                    for k in range(KD):
                        mm = pe.matmul(ps[:, 2 * t + b, 0:n], xT[:, k, t * P:(t + 1) * P], w[:, k, :], start=(k == 0), stop=(k == KD - 1))
                        if k % 4 == 2 and rounds:
                            bias_round(rounds.pop(0))
                mm.then_inc(s.fgu_mm, 1)

            def ffn_T(c, t):
                u = 2 * c + t
                pe.wait_ge(s.fhh_ready, u + 1)
                if u >= 1:
                    pe.wait_ge(s.fhhT_ready, u)
                for j in range(f_cols(c) // P):
                    mm = pe.transpose(ps[:, 4, j * P:(j + 1) * P], fhh[:, t, j * P:(j + 1) * P], ident)
                mm.then_inc(s.ftr_mm, 1)

            def ffn_down(n):
                c, t, half = downs[n]
                weights_here(pe, "fd%d" % c)
                w, nj = w_of("fd%d" % c), f_cols(c) // P
                pe.wait_ge(s.fhhT_ready, 2 * c + t + 1)
                if n >= 2:
                    pe.wait_ge(s.fh_added, n - 1)
                for j in range(nj):
                    mm = pe.matmul(ps[:, 5 + n % 2, :], fhhT[:, c % 2, j, t * P:(t + 1) * P], w[:, j, half * 512:(half + 1) * 512],
                                   start=(j == 0), stop=(j == nj - 1))
                mm.then_inc(s.fdown_mm, 1)

            def bias_round(r):
                pe.wait_ge(s.onehot_ready, 4 * r // 2 + 2)
                if r == 0:
                    pe.wait_ge(s.delta_ready, 1)
                else:
                    pe.wait_ge(s.bias_ready, 2 * r)
                for j in range(2):
                    pe.matmul(ps[:, 7, j * 64:(j + 1) * 64], onehot[:, r % 2, j, P:S], tabs[:], start=True, stop=True)
                    mm = pe.matmul(ps[:, 7, 128 + j * 32:128 + (j + 1) * 32], onehot[0:64, r % 2, j, 0:P], tabs[0:64, 0:32],
                                   start=True, stop=True)
                mm.then_inc(s.bias_mm, 1)

            for c in range(FCH):
                ffn_products(c, 0)
                if c == 0:
                    rows_to_T(1, 1, 4)
                if c >= 1:
                    ffn_T(c - 1, 1)
                ffn_products(c, 1)
                ffn_T(c, 0)
                if 1 <= c < FCH - 1:
                    for n in range(4 * (c - 1), 4 * c):
                        ffn_down(n)
            n0 = 4 * (FCH - 2)
            for n in range(n0, n0 + 4):
                ffn_down(n)
            ffn_T(FCH - 1, 1)
            ffn_down(n0 + 4)
            ffn_down(n0 + 5)
            rows_to_T(2, 0, 0)
            ffn_down(n0 + 6)
            ffn_down(n0 + 7)

            weights_here(pe, "kvw")
            pe.wait_ge(s.fhhT_ready, 2 * FCH)
            pe.wait_ge(s.biasrows_loaded, 16 * 8)
            w = w_of("kvw")
            for t in range(TT):
                if t == 1:
                    rows_to_T(2, 1, 0)
                pe.wait_ge(s.xT_ready, 10 + 4 * t)
                for k in range(KD):
                    mm = pe.matmul(ps[:, 4, t * P:(t + 1) * P], w[:, k, 0:P], xT2[:, k, t * P:(t + 1) * P], start=(k == 0), stop=(k == KD - 1))
                mm.then_inc(s.kT_mm, 1)
                b = 7 if t == 0 else 5
                for k in range(KD):
                    pe.matmul(ps[:, b, 0:P], xT2[:, k, t * P:(t + 1) * P], w[:, k, P:2 * P], start=(k == 0), stop=False)
                pe.matmul(ps[:, b, 0:P], cst[0:1, C_ONE:C_ONE + P], kvb_row[0:1, :], start=False, stop=True).then_inc(s.sv_mm, 1)
            pe.wait_ge(s.xT_ready, 16)
            weights_here(pe, "wq0")
            weights_here(pe, "wq1")
            wq = [w_of("wq0"), w_of("wq1")]

            def sq_products(u):
                if u == 1:
                    pe.wait_ge(s.sv_ready, 2)
                if u >= 2:
                    pe.wait_ge(s.sq_ready, 2 * u)
                for j in range(2):
                    g = 2 * u + j
                    for k in range(KD):
                        for v in range(KVH):
                            c0 = (v * G + g) * HD
                            mm = pe.matmul(ps[v * HD:(v + 1) * HD, Q_BANK[u], j * S:(j + 1) * S], wq[k // 4][:, k % 4, c0:c0 + HD],
                                           xT[:, k, :], start=(k == 0), stop=(k == KD - 1))
                mm.then_inc(s.sq_mm, 1)

            def sscores(i):
                g, v = i // 2, i % 2
                if i % 4 == 0:
                    pe.wait_ge(s.sq_ready, i // 2 + 2)
                if i >= 3:
                    pe.wait_ge(s.ss_ready, 2 * (i - 2))
                b, part = 2 + i % 3, 64 * v
                for t, c0, n in ((0, 0, P), (1, P, 2 * P)):
                    mm = pe.matmul(ps[:, b, c0:c0 + n], sqT[part:part + 64, g, t * P:(t + 1) * P], skT[part:part + 64, 0:n],
                                   start=True, stop=True)
                mm.then_inc(s.sscore_mm, 1)

            def sprobs_T(i):
                pe.wait_ge(s.sp_ready, 2 * i + 2)
                if i >= 2:
                    pe.wait_ge(s.spT_ready, i - 1)
                pe.transpose(ps[:, i % 2, 0:P], bias0[:, i, :], ident)
                pe.transpose(ps[:, i % 2, P:2 * P], bias1[:, i, 0:P], ident)
                pe.transpose(ps[:, i % 2, 2 * P:3 * P], bias1[:, i, P:2 * P], ident).then_inc(s.spT_mm, 1)

            def spv(i):
                g, v = i // 2, i % 2
                pe.wait_ge(s.spT_ready, i + 1)
                if i >= 2:
                    pe.wait_ge(s.soT_ready, i - 1)
                part = 64 * (g % 2)
                o = ps[part:part + 64, 6 + i % 2, :]
                v0, v1 = (sv[:, t, v * HD:(v + 1) * HD] for t in range(TT))
                pe.matmul(o[:, 0:P], v0, spT[:, i % 2, 0:P], start=True, stop=True)
                pe.matmul(o[:, P:S], v0, spT[:, i % 2, P:S], start=True, stop=False)
                pe.matmul(o[:, P:S], v1, spT[:, i % 2, S:3 * P], start=False, stop=True).then_inc(s.spv_mm, 1)

            sq_products(0)
            sq_products(1)
            pe.wait_ge(s.kT_ready, 1)
            for i in range(4):
                sscores(i)
            for q in range(4):
                if q < 2:
                    sq_products(q + 2)
                if q < 3:
                    for j in range(4):
                        sscores(4 * (q + 1) + j)
                for i in range(4 * q, 4 * q + 4):
                    sprobs_T(i)
                    if i >= 1:
                        spv(i - 1)
            spv(AH - 1)
            pe.wait_ge(s.soT_ready, AH)
            weights_here(pe, "swo0")
            weights_here(pe, "swo1")
            out_product("swo", soT, 0, 0, s.swo_mm)
            out_product("swo", soT, 0, 1, s.swo_mm)
            out_product("swo", soT, 1, 0, s.swo_mm)
            rows_to_T(3, 0, 4)
            out_product("swo", soT, 1, 1, s.swo_mm)

            for t in range(TT):
                if t == 1:
                    rows_to_T(3, 1, 4)
                pe.wait_ge(s.xT_ready, 18 + 2 * t)
                for k in range(KD):
                    mm = pe.matmul(ps[:, 0, t * NE:(t + 1) * NE], xT[:, k, t * P:(t + 1) * P], wr[:, k, :], start=(k == 0), stop=(k == KD - 1))
                mm.then_inc(s.router_mm, 1)
            pe.wait_ge(s.route_mask, 1)
            tri, ones = cst[:, C_TRI:C_TRI + P], cst[:, C_ONE:C_ONE + P]
            m0, m1 = rt[:, 0, 8:16], rt[:, 1, 8:16]
            pe.matmul(ps[:, 1, 0:8], tri, m0, start=True, stop=True)
            pe.matmul(ps[:, 1, 8:16], ones, m0, start=True, stop=False)
            pe.matmul(ps[:, 1, 8:16], tri, m1, start=False, stop=True)
            pe.matmul(ps[:, 1, 16:24], ones, m0, start=True, stop=False)
            pe.matmul(ps[:, 1, 16:24], ones, m1, start=False, stop=True).then_inc(s.route_cum_mm, 1)

            def gather():
                for k in range(KD):
                    for t in range(TT):
                        mm = pe.matmul(ps[:, 2 + k // 4, (k % 4) * SLOTS:(k % 4 + 1) * SLOTS], xn[:, t, k * P:(k + 1) * P], sel[:, t, :],
                                       start=(t == 0), stop=(t == TT - 1))
                mm.then_inc(s.gath_mm, 1)

            def grouped(bank, stationary, streams, first, last):
                for g in range(SG_N):
                    lhs = stationary[:, 32 * g:32 * g + 32]
                    for b, rhs in enumerate(streams[:-1]):
                        pe.matmul(ps[32 * g:32 * g + 32, bank + b, 0:rhs.shape[1]], lhs, rhs, start=first, stop=last,
                                  skip_group_check=True)
                for g in range(SG_N):
                    mm = pe.matmul(ps[96:128, bank + g // 2, (g % 2) * LASTQ:(g % 2 + 1) * LASTQ],
                                   stationary[:, 32 * g:32 * g + 32], streams[-1], start=(first and g % 2 == 0), stop=last,
                                   skip_group_check=True)
                return mm

            def products(i, c, narrow):
                a = c % 2
                piece_here(pe, i, "g", c)
                piece_here(pe, i, "u", c)
                if c == 0:
                    pe.wait_ge(s.xgT_ready_a, i + 2)
                    pe.wait_ge(s.xgT_ready_v, i + 2)
                if c != 1:
                    pe.wait_ge(s.hh_ready, i * (2 * ECH) + (2 * max(c - 1, 0) + 1))
                wg, wu = piece("g", c), piece("u", c)
                for k in range(KD):
                    if narrow:
                        lhs = xgT[:, k, 0:NARROW]
                        pe.matmul(ps[0:NARROW, 2 * a, :], lhs, wg[:, k, :], start=(k == 0), stop=(k == KD - 1))
                        mm = pe.matmul(ps[64:64 + NARROW, 2 * a + 1, :], lhs, wu[:, k, :], start=(k == 0), stop=(k == KD - 1))
                        continue
                    mm = grouped(2 * a, xgT[:, k, :], [wg[:, k, :], wu[:, k, 0:LASTQ], wu[:, k, LASTQ:FC]], k == 0, k == KD - 1)
                mm.then_inc(s.gu_mm, 1)

            def scatter(i, j):
                t, half = j // 2, j % 2
                if j == 0:
                    pe.wait_ge(s.y_ready_a, i + 1)
                    pe.wait_ge(s.y_ready_v, i + 1)
                    pe.wait_ge(s.sgt_ready, i + 1)
                else:
                    pe.wait_ge(s.h_added, i * 4 + (j + 1))
                pe.matmul(ps[:, 7, :], sgt[0:SLOTS, t, :], ysb[0:SLOTS, half * 512:(half + 1) * 512], start=True, stop=True).then_inc(s.scat_mm, 1)

            def scatter_T(i):
                pe.wait_ge(s.selg_ready, i * 2 + 3)
                pe.wait_ge(s.h_added, i * 4 + 5)
                pe.transpose(ps[0:SLOTS, 7, 0:P], selg[:, 0, :], ident)
                pe.transpose(ps[0:SLOTS, 7, P:2 * P], selg[:, 1, :], ident).then_inc(s.sgt_mm, 1)

            def hidden_T(i, c):
                pe.wait_ge(s.hh_ready, i * (2 * ECH) + (2 * c + 3))
                pe.wait_ge(s.hhT_ready, i * ECH + (c + 1))
                for j in range(4):
                    mm = pe.transpose(ps[:, 4, j * SLOTS:(j + 1) * SLOTS], hh[0:SLOTS, c % 2, j * P:(j + 1) * P], ident[0:SLOTS, 0:SLOTS])
                mm.then_inc(s.tr_mm, 1)

            def down(i, c, narrow):
                piece_here(pe, i, "d", c)
                pe.wait_ge(s.hhT_ready, i * ECH + (c + 2))
                if c == 0:
                    pe.wait_ge(s.y_ready_a, i + 1)
                    pe.wait_ge(s.y_ready_v, i + 1)
                w = piece("d", c)
                for j in range(4):
                    if narrow:
                        lhs = hhT[:, c % 2, j, 0:NARROW]
                        first, last = c == 0 and j == 0, c == ECH - 1 and j == 3
                        pe.matmul(ps[0:NARROW, 5, :], lhs, w[:, j, 0:512], start=first, stop=last)
                        mm = pe.matmul(ps[64:64 + NARROW, 6, :], lhs, w[:, j, 512:1024], start=first, stop=last)
                        continue
                    mm = grouped(5, hhT[:, c % 2, j, :], [w[:, j, 0:512], w[:, j, 512:768], w[:, j, 768:1024]],
                                 c == 0 and j == 0, c == ECH - 1 and j == 3)
                mm.then_inc(s.down_mm, 1)

            for q in (s.gu_mm, s.tr_mm, s.down_mm, s.gath_mm, s.sgt_mm, s.scat_mm):
                pe.sem_inc(q, 1)
            pe.wait_ge(s.sel_ready, 3)
            gather()
            pe.wait_ge(s.counts_ready, 1)
            items = pe.value_load(n_items[0:1, 0:1], min_val=NE, max_val=ITEMS_MAX)

            def pe_item(i, narrow):
                for c in range(ECH):
                    products(i, c, narrow)
                    if c < 4:
                        scatter(i, c)
                    if c == 4:
                        scatter_T(i)
                    if c >= 1:
                        hidden_T(i, c - 1)
                    if c >= 2:
                        down(i, c - 2, narrow)
                pe.wait_ge(s.sel_ready, i * 2 + 5)
                pe.wait_ge(s.hh_ready, i * (2 * ECH) + (2 * (ECH - 1) + 1))
                gather()
                hidden_T(i, ECH - 1)
                down(i, ECH - 2, narrow)
                down(i, ECH - 1, narrow)

            with pe.Fori(0, items) as i:
                many = pe.value_load(wide[0:1, bass.ds(i, 1)], min_val=0, max_val=1)
                with pe.If(many > 0):
                    pe_item(i, False)
                with pe.Else():
                    pe_item(i, True)
            for j in range(4):
                scatter(items, j)

        @block.vector
        def _(dve):
            chain = [0]

            def link(ins):
                chain[0] += 1
                ins.then_inc(s.dve_chain, 1)
                dve.wait_ge(s.dve_chain, chain[0])

            squares, norms = [0], [0]

            def mean_squares(dst, src, width, n=1, tiles=1):
                squares[0] += tiles
                norms[0] += 1
                dve.wait_ge(s.ssq_ready, squares[0])
                dve.tensor_scalar(stat[:, dst:dst + n], stat[:, src:src + n], 1.0 / width, EPS, ALU.mult, ALU.add).then_inc(s.ms_ready, 1)

            def norm_rows(t, gain=None):
                mean_squares(2 + t, t, D)
                dve.wait_ge(s.rstd_ready, norms[0])
                if gain is None:
                    dve.tensor_scalar(xn[:, t, :], h[:, t, :], stat[:, 4 + t:5 + t], None, ALU.mult).then_inc(s.xn_ready, 1)
                else:
                    dve.scalar_tensor_tensor(out=xn[:, t, :], in0=h[:, t, :], scalar=stat[:, 4 + t:5 + t], in1=gain,
                                             op0=ALU.mult, op1=ALU.mult).then_inc(s.xn_ready, 1)

            def evac_xT(n, t, off, dst, gain):
                dve.wait_ge(s.xT_mm, 2 * n + t + 1)
                for b in range(2):
                    src = ps[:, off + 2 * t + b, :].rearrange("p (k n) -> p k n", k=4)
                    o = dst[:, 4 * b:4 * b + 4, t * P:(t + 1) * P]
                    if gain is None:
                        dve.tensor_copy(o, src).then_inc(s.xT_ready, 1)
                    else:
                        g = vecT[:, gain + 4 * b:gain + 4 * b + 4].unsqueeze(2).to_broadcast([P, 4, P])
                        dve.tensor_tensor(o, src, g, ALU.mult).then_inc(s.xT_ready, 1)

            dve.wait_ge(s.consts_loaded, 16)
            dve.wait_ge(s.smalls_loaded, 160)
            link(dve.tensor_copy(pos_f[:], pos_i[:]))
            for t in range(TT):
                link(dve.tensor_scalar(ang[:, 0, t, :], cst[:, C_INV:C_INV + HALF], pos_f[:, t:t + 1], None, ALU.mult))

            def reduced(dst, quarter):
                link(dve.tensor_scalar(ang[:, 1], ang[:, 0], float(1 / TWO_PI), quarter, ALU.mult, ALU.add))
                link(dve.tensor_scalar(ang[:, 1], ang[:, 1], MAGIC, MAGIC, ALU.add, ALU.subtract))
                link(dve.scalar_tensor_tensor(out=ang[:, 2], in0=ang[:, 1], scalar=-C1, in1=ang[:, 0], op0=ALU.mult, op1=ALU.add))
                link(dve.scalar_tensor_tensor(out=ang[:, 2], in0=ang[:, 1], scalar=-C2, in1=ang[:, 2], op0=ALU.mult, op1=ALU.add))
                link(dve.scalar_tensor_tensor(out=ang[:, 2], in0=ang[:, 1], scalar=-C3, in1=ang[:, 2], op0=ALU.mult, op1=ALU.add))
                link(dve.tensor_scalar(ang[:, 2], ang[:, 2], quarter * TWO_PI, PI_LO, ALU.add, ALU.min))
                dve.tensor_scalar(ang[:, dst], ang[:, 2], -PI_LO, None, ALU.max).then_inc(s.rope_arg, 1)

            norm_rows(0)
            norm_rows(1)
            dve.wait_ge(s.vecT_ready, 1)
            evac_xT(0, 0, 0, xT, V_GA0)
            evac_xT(0, 1, 0, xT, V_GA0)
            reduced(4, 0.0)
            dve.wait_ge(s.rope_arg, 1)
            reduced(5, 0.25)
            mean_squares(8, 0, QL, 2, 2)
            mean_squares(10, 6, KVL, 2, 2)
            dve.wait_ge(s.rstd_ready, 3)
            for t in range(TT):
                dve.tensor_scalar(cq[:, t, :], ps[:, 4 + t, 0:QL], stat[:, 12 + t:13 + t], None, ALU.mult).then_inc(s.cq_ready, 1)
            dve.wait_ge(s.rstd_ready, 4)
            for t in range(TT):
                dve.tensor_scalar(ckv[:, t, :], ps[:, 6 + t, 0:KVL], stat[:, 14 + t:15 + t], None, ALU.mult).then_inc(s.ckv_ready, 1)

            dve.wait_ge(s.sincos_ready, 2)
            for t in range(TT):
                x1, x2 = ps[:, 6 + t, KVL:KVL + HALF], ps[:, 6 + t, KVL + HALF:KVL + ROPE]
                cos, sin = cosn[:, t, 0:HALF], cosn[:, t, HALF:2 * HALF]
                a, b, c, d = (rtmp[:, 0, n * HALF:(n + 1) * HALF] for n in range(4))
                dve.tensor_tensor(a, x1, cos, ALU.mult)
                dve.tensor_tensor(b, x2, sin, ALU.mult)
                dve.tensor_tensor(c, x2, cos, ALU.mult)
                link(dve.tensor_tensor(d, x1, sin, ALU.mult))
                krv = kr[:, t, :].rearrange("p (r n) -> p r n", r=2)
                link(dve.tensor_tensor(krv[:, 0, 0:HALF], a, b, ALU.subtract))
                link(dve.tensor_tensor(krv[:, 0, HALF:ROPE], c, d, ALU.add))
                dve.tensor_copy(krv[:, 1, :], krv[:, 0, :]).then_inc(s.krope_ready, 1)
            dve.wait_ge(s.cT_mm, 1)
            for k in range(3):
                dve.tensor_scalar(cqT[:, k, :], ps[:, k // 2, (k % 2) * S:(k % 2 + 1) * S], gcol(V_GQ, k), None, ALU.mult).then_inc(s.cqT_ready, 1)
            for t in range(TT):
                dve.wait_ge(s.qrope_mm, 3 + t)
                q = ps[:, 4 + t, :].rearrange("p (h n) -> p h n", n=ROPE)
                x1, x2 = q[:, :, 0:HALF], q[:, :, HALF:ROPE]
                o = qr[:, t, :].rearrange("p (h n) -> p h n", n=ROPE)
                cos = cosn[:, t:t + 1, 0:HALF].to_broadcast([P, MH, HALF])
                sin = cosn[:, t:t + 1, HALF:2 * HALF].to_broadcast([P, MH, HALF])
                a = rtmp[:, 0, :].rearrange("p (h n) -> p h n", n=HALF)
                b = rtmp[:, 1, :].rearrange("p (h n) -> p h n", n=HALF)
                link(dve.tensor_tensor(a, x1, cos, ALU.mult))
                link(dve.tensor_tensor(b, x2, sin, ALU.mult))
                dve.tensor_tensor(o[:, :, 0:HALF], a, b, ALU.subtract).then_inc(s.qrope_ready, 1)
                dve.wait_ge(s.qrope_ready, 2 * t + 1)
                link(dve.tensor_tensor(a, x2, cos, ALU.mult))
                link(dve.tensor_tensor(b, x1, sin, ALU.mult))
                dve.tensor_tensor(o[:, :, HALF:ROPE], a, b, ALU.add).then_inc(s.qrope_ready, 1)
                dve.wait_ge(s.qrope_ready, 2 * t + 2)
            dve.wait_ge(s.qrT_mm, 1)
            for k in range(4):
                dve.tensor_copy(qrT[:, k, :], ps[:, 4 + k // 2, (k % 2) * S:(k % 2 + 1) * S]).then_inc(s.qrT_ready, 1)

            def mla_max(i):
                dve.wait_ge(s.score_mm, i + 1)
                st = mstat[:, i, :]
                dve.tensor_tensor(probs[:, i, :], ps[:, i % 4, 0:3 * P], cst[:, C_MLA:C_MLA + 3 * P], ALU.add).then_inc(s.s_ready, 1)
                dve.wait_ge(s.s_ready, i + 1)
                dve.tensor_reduce(st[:, 0:1], probs[:, i, 0:P], AX.X, ALU.max, negate=True)
                link(dve.tensor_reduce(st[:, 1:2], probs[:, i, P:3 * P], AX.X, ALU.max, negate=True))
                dve.tensor_scalar(st[:, 2:4], st[:, 0:2], MLA_SCALE, None, ALU.mult).then_inc(s.negmax_ready, 2)

            def mla_norm(i):
                st = mstat[:, i, :]
                dve.wait_ge(s.exp_ready, 2 * i + 2)
                link(dve.reciprocal(st[:, 6:8], st[:, 4:6]))
                dve.tensor_scalar(probs[:, i, 0:P], probs[:, i, 0:P], st[:, 6:7], None, ALU.mult).then_inc(s.p_ready, 1)
                dve.tensor_scalar(probs[:, i, P:3 * P], probs[:, i, P:3 * P], st[:, 7:8], None, ALU.mult).then_inc(s.p_ready, 1)

            def mla_out(i):
                dve.wait_ge(s.pv_mm, i + 1)
                dve.tensor_copy(oT[:, i, :], ps[:, 6 + i % 2, 0:S]).then_inc(s.oT_ready, 1)

            for i in range(MH + 3):
                if i < MH:
                    mla_max(i)
                if 1 <= i <= MH:
                    mla_norm(i - 1)
                if i >= 3:
                    mla_out(i - 3)
            dve.wait_ge(s.biasrows_loaded, 16 * 8)
            link(dve.tensor_copy(posq[:], posq_i[:]))
            link(dve.tensor_copy(posk[:], posk_i[:]))
            link(dve.tensor_scalar(posk[:], posk[:], cst[:, C_THR:C_THR + 1], None, ALU.add))
            dve.wait_ge(s.rel_loaded, 16 * 8)
            by_h = [tabs_h[:, n, :].rearrange("p (k v g) -> p k v g", k=4, v=KVH) for n in range(2)]
            dve.tensor_tensor(tabs[:].rearrange("p (k g v) -> p k v g", k=4, v=KVH), by_h[0], by_h[1], ALU.subtract).then_inc(s.delta_ready, 1)
            link(dve.tensor_copy(sinks[:].rearrange("p (g v) -> p v g", v=KVH), sinks_h[:].rearrange("p (v g) -> p v g", v=KVH)))

            def add_out(n, mm, done):
                t, half = n // 2, n % 2
                dve.wait_ge(mm, n + 1)
                hv = h[:, t, half * 512:(half + 1) * 512]
                dve.tensor_tensor(hv, hv, ps[:, n, :], ALU.add).then_inc(done, 1)

            add_out(0, s.wo_mm, s.h_attn0)
            add_out(1, s.wo_mm, s.h_attn0)
            norm_rows(0)
            add_out(2, s.wo_mm, s.h_attn0)
            evac_xT(1, 0, 4, xT, V_GF0)
            add_out(3, s.wo_mm, s.h_attn0)
            norm_rows(1)
            evac_xT(1, 1, 4, xT, V_GF0)

            def onehots(r):
                if r >= 2:
                    dve.wait_ge(s.bias_mm, r - 1)
                for j in range(2):
                    dve.tensor_scalar(onehot[:, r % 2, j, :], posq[:], posk[:, 2 * r + j:2 * r + j + 1], None, ALU.is_ge).then_inc(s.onehot_ready, 1)

            def bias_out(r):
                dve.wait_ge(s.bias_mm, r + 1)
                for dst, c0, nk, m in ((bias1, 0, 4, C_WIN), (bias0, 128, 2, C_WIN + P)):
                    src = ps[:, 7, c0:c0 + nk * 32].rearrange("p (j k h) -> p j k h", j=2, k=nk)
                    mask = cst[:, m:m + nk * 64].rearrange("p (k j) -> p j k", k=nk)[:, 2 * r:2 * r + 2, :]
                    o = dst.rearrange("p h (k j) -> p j k h", k=nk)[:, 2 * r:2 * r + 2]
                    dve.tensor_tensor(o, src, mask.unsqueeze(3).to_broadcast([P, 2, nk, AH]), ALU.add).then_inc(s.bias_ready, 1)

            def ffn_hidden(u):
                n = f_cols(u // 2)
                dve.wait_ge(s.fsg_ready, u + 1)
                if u >= 2:
                    dve.wait_ge(s.ftr_mm, u - 1)
                dve.tensor_tensor(fhh[:, u % 2, 0:n], fsg[:, u % 2, 0:n], ps[:, 2 * (u % 2) + 1, 0:n], ALU.mult).then_inc(s.fhh_ready, 1)

            def ffn_add(n):
                c, t, half = downs[n]
                dve.wait_ge(s.fdown_mm, n + 1)
                hv = h[:, t, half * 512:(half + 1) * 512]
                before = [m for m in range(n) if downs[m][1:] == (t, half)]
                if before:
                    dve.wait_ge(s.fh_added, before[-1] + 1)
                dve.tensor_tensor(hv, hv, ps[:, 5 + n % 2, :], ALU.add).then_inc(s.fh_added, 1)

            onehots(0)
            for u in range(2 * FCH):
                c = u // 2
                for r in bias_rounds(u):
                    if r + 1 < BIAS_ROUNDS:
                        onehots(r + 1)
                    bias_out(r)
                ffn_hidden(u)
                if u % 2 == 1 and 1 <= c < FCH - 1:
                    for n in range(4 * (c - 1), 4 * c):
                        ffn_add(n)
            n0 = 4 * (FCH - 2)
            for n in range(n0, n0 + 4):
                ffn_add(n)
            norm_rows(0)
            ffn_add(n0 + 4)
            ffn_add(n0 + 5)
            evac_xT(2, 0, 0, xT2, V_KVG)
            evac_xT(2, 0, 0, xT, V_GA1)
            ffn_add(n0 + 6)
            ffn_add(n0 + 7)
            norm_rows(1)
            evac_xT(2, 1, 0, xT2, V_KVG)
            evac_xT(2, 1, 0, xT, V_GA1)

            def swa_scores(q):
                for i in range(4 * q, 4 * q + 4):
                    dve.wait_ge(s.sscore_mm, i + 1)
                    b = 2 + i % 3
                    dve.scalar_tensor_tensor(out=bias0[:, i, :], in0=ps[:, b, 0:P], scalar=SWA_SCALE, in1=bias0[:, i, :],
                                             op0=ALU.mult, op1=ALU.add).then_inc(s.ss_ready, 1)
                    dve.scalar_tensor_tensor(out=bias1[:, i, :], in0=ps[:, b, P:3 * P], scalar=SWA_SCALE, in1=bias1[:, i, :],
                                             op0=ALU.mult, op1=ALU.add).then_inc(s.ss_ready, 1)
                c = slice(4 * q, 4 * q + 4)
                dve.wait_ge(s.ss_ready, 8 * q + 8)
                dve.tensor_reduce(sstat[:, 0, 0, c], bias0[:, c, :], AX.X, ALU.max)
                link(dve.tensor_reduce(sstat[:, 0, 1, c], bias1[:, c, :], AX.X, ALU.max))
                sk = sinks[:, c].unsqueeze(1).to_broadcast([P, 2, 4])
                link(dve.tensor_tensor(sstat[:, 5, :, c], sstat[:, 0, :, c], sk, ALU.max))
                link(dve.tensor_tensor(sstat[:, 2, :, c], sk, sstat[:, 5, :, c], ALU.subtract))
                dve.tensor_scalar(sstat[:, 1, :, c], sstat[:, 5, :, c], -1.0, None, ALU.mult).then_inc(s.snegmax_ready, 1)

            def swa_norm(q):
                c = slice(4 * q, 4 * q + 4)
                dve.wait_ge(s.sexp_ready, 8 * q + 8)
                dve.wait_ge(s.esink_ready, q + 1)
                link(dve.tensor_tensor(sstat[:, 6, :, c], sstat[:, 4, :, c], sstat[:, 3, :, c], ALU.add))
                link(dve.reciprocal(sstat[:, 7, :, c], sstat[:, 6, :, c]))
                for i in range(4 * q, 4 * q + 4):
                    dve.tensor_scalar(bias0[:, i, :], bias0[:, i, :], sstat[:, 7, 0, i:i + 1], None, ALU.mult).then_inc(s.sp_ready, 1)
                    dve.tensor_scalar(bias1[:, i, :], bias1[:, i, :], sstat[:, 7, 1, i:i + 1], None, ALU.mult).then_inc(s.sp_ready, 1)

            for q in range(5):
                if q < 4:
                    swa_scores(q)
                if q >= 1:
                    swa_norm(q - 1)
            dve.wait_ge(s.bo_added, 2)
            dve.wait_ge(s.rel_loaded, 16 * 11)
            add_out(0, s.swo_mm, s.h_attn1)
            add_out(1, s.swo_mm, s.h_attn1)
            norm_rows(0, grow)
            add_out(2, s.swo_mm, s.h_attn1)
            evac_xT(3, 0, 4, xT, None)
            add_out(3, s.swo_mm, s.h_attn1)
            norm_rows(1, grow)
            dve.memset(ysb[:], 0.0).then_inc(s.y_last, 1)
            dve.memset(sgt[:], 0.0).then_inc(s.y_last, 1)
            dve.memset(hh[:], 0.0).then_inc(s.y_last, 1)
            dve.memset(slots[:, :, ITEMS_MAX:ITEMS_MAX + 1], -1.0).then_inc(s.y_last, 1)
            dve.memset(gates[:, :, ITEMS_MAX:ITEMS_MAX + 1], 0.0).then_inc(s.y_last, 1)
            evac_xT(3, 1, 4, xT, None)
            lg, mask, top, idx = (rt[:, :, 8 * n:8 * n + 8] for n in range(4))
            o1, o2, z, g1 = (rt[:, :, 8 * n:8 * n + 8] for n in range(4, 8))
            e8 = cst[:, C_E8:C_E8 + NE].unsqueeze(1).to_broadcast([P, TT, NE])
            dve.wait_ge(s.router_mm, 2)
            link(dve.tensor_copy(lg, ps[:, 0, 0:TT * NE].rearrange("p (t n) -> p t n", t=TT)))
            dve.max(top[:, 0, :], lg[:, 0, :])
            link(dve.max(top[:, 1, :], lg[:, 1, :]))
            dve.max_index(ridx[:, 0, :], top[:, 0, :], lg[:, 0, :])
            link(dve.max_index(ridx[:, 1, :], top[:, 1, :], lg[:, 1, :]))
            link(dve.tensor_copy(idx, ridx[:]))
            dve.tensor_tensor(o1, e8, idx[:, :, 0:1].to_broadcast([P, TT, NE]), ALU.is_equal)
            link(dve.tensor_tensor(o2, e8, idx[:, :, 1:2].to_broadcast([P, TT, NE]), ALU.is_equal))
            dve.tensor_tensor(mask, o1, o2, ALU.add).then_inc(s.route_mask, 1)
            dve.tensor_tensor(z[:, :, 0:1], top[:, :, 1:2], top[:, :, 0:1], ALU.subtract).then_inc(s.gate_arg, 1)
            dve.wait_ge(s.route_cum_mm, 1)
            cum = rt[:, :, 64:72]
            link(dve.scalar_tensor_tensor(out=cum, in0=ps[:, 1, 0:TT * NE].rearrange("p (t n) -> p t n", t=TT), scalar=1.0, in1=mask,
                                          op0=ALU.add, op1=ALU.mult))
            for w in range(SWEEPS):
                link(dve.tensor_scalar(slots[:, :, w * NE:(w + 1) * NE], cum, -1.0 - w * SLOTS, None, ALU.add))
                if w == 0:
                    for q in (s.sel_ready, s.selg_ready, s.hh_ready, s.y_ready_v, s.xgT_ready_v, s.h_added):
                        dve.sem_inc(q, 1)
                    for t in range(TT):
                        dve.tensor_scalar(sel[:, t, :], cst[:, C_IOTA:C_IOTA + SLOTS], slots[:, t, 0:1], None, ALU.is_equal).then_inc(s.sel_ready, 1)
            counts, top_count, more = ps[:, 1, 16:24], rt[:, 0, 24:25], rt[:, 0, 25:25 + SWEEPS - 1]
            link(dve.tensor_reduce(top_count, counts, AX.X, ALU.max))
            for w in range(1, SWEEPS):
                link(dve.tensor_scalar(more[:, w - 1:w], top_count, w * SLOTS + 0.5, float(NE), ALU.is_ge, ALU.mult))
            link(dve.tensor_reduce(rt[:, 0, 28:29], more, AX.X, ALU.add))
            link(dve.tensor_scalar(n_items[:, 0:1], rt[:, 0, 28:29], float(NE), None, ALU.add))
            for w in range(SWEEPS):
                wide_w = dve.tensor_scalar(wide[:, w * NE:(w + 1) * NE], counts, w * SLOTS + NARROW + 0.5, None, ALU.is_ge)
                if w < SWEEPS - 1:
                    link(wide_w)
            wide_w.then_inc(s.counts_ready, 1)
            dve.wait_ge(s.counts_ready, 1)
            dve.wait_ge(s.gath_mm, 2)
            dve.tensor_copy(xgT[:, 0:4, :].rearrange("p k n -> p (k n)"), ps[:, 2, 0:4 * SLOTS]).then_inc(s.xgT_ready_v, 1)
            dve.wait_ge(s.gate_exp, 1)
            link(dve.tensor_scalar(z[:, :, 2:3], z[:, :, 1:2], 1.0, None, ALU.add))
            link(dve.reciprocal(z[:, :, 3:4], z[:, :, 2:3]))
            link(dve.tensor_tensor(z[:, :, 4:5], z[:, :, 1:2], z[:, :, 3:4], ALU.mult))
            link(dve.tensor_tensor(g1, o1, z[:, :, 3:4].to_broadcast([P, TT, NE]), ALU.mult))
            link(dve.tensor_tensor(o2, o2, z[:, :, 4:5].to_broadcast([P, TT, NE]), ALU.mult))
            for w in range(SWEEPS):
                link(dve.tensor_tensor(gates[:, :, w * NE:(w + 1) * NE], g1, o2, ALU.add))

            iota = cst[:, C_IOTA:C_IOTA + SLOTS]

            items = dve.value_load(n_items[0:1, 0:1], min_val=NE, max_val=ITEMS_MAX)

            def add_rows(i, j):
                t, half = j // 2, j % 2
                dve.wait_ge(s.scat_mm, i * 4 + (j + 2))
                hv = h[:, t, half * 512:(half + 1) * 512]
                dve.tensor_tensor(hv, hv, ps[:, 7, :], ALU.add).then_inc(s.h_added, 1)


            def dve_item(i, narrow):
                dve.wait_ge(s.sgt_mm, i + 1)
                for t in range(TT):
                    dve.tensor_scalar(selg[:, t, :], iota, slots[:, t, bass.ds(i, 1)], gates[:, t, bass.ds(i, 1)], ALU.is_equal, ALU.mult).then_inc(s.selg_ready, 1)
                dve.wait_ge(s.gath_mm, i + 2)
                for t in range(TT):
                    dve.tensor_scalar(sel[:, t, :], iota, slots[:, t, bass.ds(i + 1, 1)], None, ALU.is_equal).then_inc(s.sel_ready, 1)
                for c in range(ECH):
                    a = c % 2
                    dve.wait_ge(s.sg_ready, i * (4 * ECH) + (4 * c + 5))
                    dve.wait_ge(s.tr_mm, i * ECH + (max(c - 1, 0) + 1))
                    if narrow:
                        dve.tensor_tensor(hh[0:NARROW, a, :], sg[0:NARROW, a, :], upl[0:NARROW, a, :], ALU.mult).then_inc(s.hh_ready, 2)
                    else:
                        dve.tensor_tensor(hh[0:SLOTS, a, 0:LASTQ], sg[0:SLOTS, a, 0:LASTQ], ps[0:SLOTS, 2 * a + 1, 0:LASTQ], ALU.mult).then_inc(s.hh_ready, 1)
                        dve.tensor_tensor(hh[0:SLOTS, a, LASTQ:FC], sg[0:SLOTS, a, LASTQ:FC], upl[0:SLOTS, a, 0:LASTQ], ALU.mult).then_inc(s.hh_ready, 1)
                    if c < 4:
                        add_rows(i, c)
                dve.wait_ge(s.gath_mm, i + 3)
                dve.tensor_copy(xgT[:, 0:4, :].rearrange("p k n -> p (k n)"), ps[:, 2, 0:4 * SLOTS]).then_inc(s.xgT_ready_v, 1)
                dve.wait_ge(s.down_mm, i * ECH + (ECH + 1))
                if narrow:
                    dve.tensor_copy(ysb[0:NARROW, 512:1024], ps[64:64 + NARROW, 6, :]).then_inc(s.y_ready_v, 1)
                else:
                    dve.tensor_copy(ysb[64:96, 768:1024], ps[96:128, 6, 0:LASTQ]).then_inc(s.y_last, 1)
                    dve.tensor_copy(ysb[0:SLOTS, 512:768], ps[0:SLOTS, 6, 0:LASTQ]).then_inc(s.y_ready_v, 1)

            with dve.Fori(0, items) as i:
                many = dve.value_load(wide[0:1, bass.ds(i, 1)], min_val=0, max_val=1)
                with dve.If(many > 0):
                    dve_item(i, False)
                with dve.Else():
                    dve_item(i, True)
            for j in range(4):
                add_rows(items, j)
            for t in range(TT):
                norm_rows(t, gfin)


_INS = ["x", "positions", "mla_w_in", "mla_g_q", "mla_g_kv", "mla_w_uq", "mla_w_ukv", "mla_w_o", "kv_g", "kv_w", "kv_b",
        "swa_w_q", "swa_b_q", "swa_sinks", "swa_w_o", "swa_b_o", "rel_bias", "g_attn", "g_ffn", "ffn_w_gate", "ffn_w_up",
        "ffn_w_down", "moe_w_router", "moe_w_gate", "moe_w_up", "moe_w_down", "g_final"]


def kernel(**inputs):
    import concourse.bacc as bacc
    from concourse.bass_utils import run_bass_kernel_spmd

    nc = bacc.Bacc("TRN2", target_bir_lowering=False, num_devices=1)
    arrays, args = {}, []
    for name in _INS:
        a = np.ascontiguousarray(inputs[name])
        arrays["in_" + name] = a
        args.append(nc.dram_tensor("in_" + name, a.shape, mybir.dt.from_np(a.dtype), kind="ExternalInput").ap())
    arrays["consts"] = constants()
    args.append(nc.dram_tensor("consts", (P, C_N), F32, kind="ExternalInput").ap())
    args.append(nc.dram_tensor("out_0", (1, S, D), F32, kind="ExternalOutput").ap())
    build(nc, *args)
    r = run_bass_kernel_spmd(nc, [arrays], core_ids=[0])
    return r.results[0]["out_0"]
```

```python
from contextlib import ExitStack

import numpy as np
import concourse.bass as bass
from concourse import mybir

ALU = mybir.AluOpType
ACT = mybir.ActivationFunctionType
AX = mybir.AxisListType
F32 = mybir.dt.float32
F32R = mybir.dt.float32r
BF16 = mybir.dt.bfloat16
I32 = mybir.dt.int32
U32 = mybir.dt.uint32

P = 128
D = 1024
KD = D // P
S = 256
TT = S // P
EPS = 1e-6
NEG = -1e30

MH, NOPE, ROPE, VH = 8, 128, 64, 128
HALF = ROPE // 2
QL, KVL = 384, 256
MLA_SCALE = float((NOPE + ROPE) ** -0.5)

AH, KVH, HD = 16, 2, 64
G = AH // KVH
SWA_SCALE = float(HD ** -0.5)
WINDOW = 128
BUCKETS = 32

DFF = 2816
FC = 512
FCH = (DFF + FC - 1) // FC
NE, DFE = 8, 3584
ECH = DFE // FC

SLOTS = 96
NARROW = 64
REST = SLOTS - NARROW
SWEEPS = -(-S // SLOTS)
ITEMS_MAX = NE * SWEEPS
LASTQ = 256

RING = 7
SLOT = 4096

C_ID, C_TRI, C_ONE, C_MLA, C_WIN, C_IOTA = 0, 128, 256, 384, 768, 1024
C_E8 = C_IOTA + SLOTS
C_THR = C_E8 + NE
C_INV = C_THR + 1
C_MH = C_INV + HALF
C_N = C_MH + TT

V_GA0, V_GF0, V_GA1, V_KVG, V_GQ, V_GKV, V_KVB, V_BQ = 0, 8, 16, 24, 32, 35, 37, 38
V_N = V_BQ + G

MAGIC = 1.5 * 2.0 ** 23
TWO_PI = 2 * np.pi
C1 = float(np.float32(6.28125))
C2 = float(np.float32(np.round((TWO_PI - 6.28125) * 2 ** 20) / 2 ** 20))
C3 = float(np.float32(TWO_PI - 6.28125 - np.round((TWO_PI - 6.28125) * 2 ** 20) / 2 ** 20))
PI_LO = float(np.nextafter(np.float32(np.pi), np.float32(0)))


def constants():
    c = np.zeros((P, C_N), np.float32)
    r = np.arange(P)
    c[:, C_ID:C_ID + P] = np.eye(P)
    c[:, C_TRI:C_TRI + P] = r[:, None] < r[None, :]
    c[:, C_ONE:C_ONE + P] = 1.0
    causal = np.where(r[None, :] <= r[:, None], 0.0, NEG)
    c[:, C_MLA:C_MLA + P] = causal
    c[:, C_MLA + 2 * P:C_MLA + 3 * P] = causal
    c[:, C_WIN:C_WIN + P] = np.where(r[:, None] + P - r[None, :] < WINDOW, 0.0, NEG)
    c[:, C_WIN + P:C_WIN + 2 * P] = causal
    c[:, C_IOTA:C_IOTA + SLOTS] = np.arange(SLOTS)
    c[:, C_E8:C_E8 + NE] = np.arange(NE)
    exact = BUCKETS // 2
    log = [int(np.ceil(exact * 8.0 ** (j / 16) - 1e-9)) for j in range(1, BUCKETS - exact)]
    thr = [-1e9] + list(range(1, exact + 1)) + log
    c[:, C_THR] = np.tile(np.array(thr, np.float32), P // BUCKETS)
    c[:, C_INV:C_INV + HALF] = (10000.0 ** (-np.arange(HALF) / HALF)).astype(np.float32)
    c[:, C_MH:C_MH + TT] = -0.5
    return c


class Semaphores:
    def __init__(self, sem):
        self.consts_loaded = sem("consts_loaded")
        self.x_loaded0 = sem("x_loaded0")
        self.x_loaded1 = sem("x_loaded1")
        self.smalls_loaded = sem("smalls_loaded")
        self.biasrows_loaded = sem("biasrows_loaded")
        self.rel_loaded = sem("rel_loaded")
        self.out_stored = sem("out_stored")
        self.slot0 = sem("slot0")
        self.slot1 = sem("slot1")
        self.slot2 = sem("slot2")
        self.slot3 = sem("slot3")
        self.slot4 = sem("slot4")
        self.slot5 = sem("slot5")
        self.slot6 = sem("slot6")
        self.dve_chain = sem("dve_chain")
        self.act_chain = sem("act_chain")
        self.pool_chain = sem("pool_chain")
        self.vecT_mm = sem("vecT_mm")
        self.vecT_ready = sem("vecT_ready")
        self.ssq_ready = sem("ssq_ready")
        self.ms_ready = sem("ms_ready")
        self.rstd_ready = sem("rstd_ready")
        self.xn_ready = sem("xn_ready")
        self.xT_mm = sem("xT_mm")
        self.xT_ready = sem("xT_ready")
        self.rope_arg = sem("rope_arg")
        self.sincos_ready = sem("sincos_ready")
        self.latq_mm = sem("latq_mm")
        self.latkv_mm = sem("latkv_mm")
        self.cq_ready = sem("cq_ready")
        self.ckv_ready = sem("ckv_ready")
        self.krope_ready = sem("krope_ready")
        self.cT_mm = sem("cT_mm")
        self.cqT_ready = sem("cqT_ready")
        self.ckvT_ready = sem("ckvT_ready")
        self.krT_ready = sem("krT_ready")
        self.qk_mm = sem("qk_mm")
        self.qk_ready = sem("qk_ready")
        self.qrope_mm = sem("qrope_mm")
        self.qrope_ready = sem("qrope_ready")
        self.ukv_v_mm = sem("ukv_v_mm")
        self.v_ready = sem("v_ready")
        self.qrT_mm = sem("qrT_mm")
        self.qrT_ready = sem("qrT_ready")
        self.score_mm = sem("score_mm")
        self.s_ready = sem("s_ready")
        self.negmax_ready = sem("negmax_ready")
        self.exp_ready = sem("exp_ready")
        self.p_ready = sem("p_ready")
        self.pT_mm = sem("pT_mm")
        self.pT_ready = sem("pT_ready")
        self.pv_mm = sem("pv_mm")
        self.oT_ready = sem("oT_ready")
        self.wo_mm = sem("wo_mm")
        self.h_attn0 = sem("h_attn0")
        self.fgu_mm = sem("fgu_mm")
        self.fsg_ready = sem("fsg_ready")
        self.fhh_ready = sem("fhh_ready")
        self.ftr_mm = sem("ftr_mm")
        self.fhhT_hi_ready = sem("fhhT_hi_ready")
        self.fhhT_lo_ready = sem("fhhT_lo_ready")
        self.whi_ready = sem("whi_ready")
        self.wlo_ready = sem("wlo_ready")
        self.xg_ready = sem("xg_ready")
        self.xhi_ready = sem("xhi_ready")
        self.fdown_mm = sem("fdown_mm")
        self.fh_added = sem("fh_added")
        self.table_step = sem("table_step")
        self.delta_ready = sem("delta_ready")
        self.onehot_ready = sem("onehot_ready")
        self.bias_mm = sem("bias_mm")
        self.bias_ready = sem("bias_ready")
        self.kT_mm = sem("kT_mm")
        self.kT_ready = sem("kT_ready")
        self.sv_mm = sem("sv_mm")
        self.sv_ready = sem("sv_ready")
        self.sq_mm = sem("sq_mm")
        self.sq_ready = sem("sq_ready")
        self.bo_added = sem("bo_added")
        self.sscore_mm = sem("sscore_mm")
        self.ss_ready = sem("ss_ready")
        self.snegmax_ready = sem("snegmax_ready")
        self.sexp_ready = sem("sexp_ready")
        self.esink_ready = sem("esink_ready")
        self.sp_ready = sem("sp_ready")
        self.spT_mm = sem("spT_mm")
        self.spT_ready = sem("spT_ready")
        self.spv_mm = sem("spv_mm")
        self.soT_ready = sem("soT_ready")
        self.swo_mm = sem("swo_mm")
        self.h_attn1 = sem("h_attn1")
        self.router_mm = sem("router_mm")
        self.route_mask = sem("route_mask")
        self.gate_arg = sem("gate_arg")
        self.gate_exp = sem("gate_exp")
        self.route_cum_mm = sem("route_cum_mm")
        self.counts_ready = sem("counts_ready")
        self.ahead_loaded = sem("ahead_loaded")
        self.gu_mm = sem("gu_mm")
        self.sg_ready = sem("sg_ready")
        self.hh_ready = sem("hh_ready")
        self.hh_first = sem("hh_first")
        self.tr_mm = sem("tr_mm")
        self.hhT_ready = sem("hhT_ready")
        self.down_mm = sem("down_mm")
        self.y_ready_a = sem("y_ready_a")
        self.y_ready_v = sem("y_ready_v")
        self.y_last = sem("y_last")
        self.sel_ready = sem("sel_ready")
        self.gath_mm = sem("gath_mm")
        self.xgT_ready_a = sem("xgT_ready_a")
        self.xgT_ready_v = sem("xgT_ready_v")
        self.selg_ready = sem("selg_ready")
        self.sgt_mm = sem("sgt_mm")
        self.sgt_ready = sem("sgt_ready")
        self.scat_mm = sem("scat_mm")
        self.h_added = sem("h_added")


def build(nc, x, positions, w_in, g_q, g_kv, w_uq, w_ukv, w_o, kv_g, kv_w, kv_b, swa_w_q, swa_b_q,
          swa_sinks, swa_w_o, swa_b_o, rel_bias, g_attn, g_ffn, f_gate, f_up, f_down, w_router,
          e_gate, e_up, e_down, g_final, consts, out):
    with ExitStack() as ctx:
        at = {}

        def sb(name, shape, dt=F32):
            t = ctx.enter_context(nc.sbuf_tensor(name, shape, dt))
            at[name] = nc.sbuf_base - 4 * int(np.prod(shape[1:]))
            return t

        def over(name, shape, under, columns):
            return nc.alloc_sbuf_tensor_at(name, shape, F32R, offset=at[under] + 4 * columns)

        ps = ctx.enter_context(nc.psum_tensor("ps", [P, 8, 512], F32))
        s = Semaphores(lambda name: ctx.enter_context(nc.semaphore(name)))
        slot_landed = [s.slot0, s.slot1, s.slot2, s.slot3, s.slot4, s.slot5, s.slot6]

        ring = sb("ring", [P, RING, SLOT])
        h = sb("h", [P, TT, D])
        xn = sb("xn", [P, TT, D])
        xT = sb("xT", [P, KD, S])
        xT2 = sb("xT2", [P, KD, S])
        arena = sb("arena", [P, 12288])
        cst = sb("cst", [P, C_N])
        vecs = sb("vecs", [V_N, P])
        vecT = sb("vecT", [P, V_N])
        pos_i = sb("pos_i", [P, TT], I32)
        pos_f = sb("pos_f", [P, TT])
        stat = sb("stat", [P, 16])
        wr = sb("wr", [P, KD, NE])
        kvb_row = sb("kvb_row", [1, P])
        sinks_h = sb("sinks_h", [P, AH])
        sinks = sb("sinks", [P, AH])
        n_items = sb("n_items", [P, 2], I32)
        wide = sb("wide", [P, ITEMS_MAX], I32)
        slots = sb("slots", [P, TT, ITEMS_MAX + 1])
        gates = sb("gates", [P, TT, ITEMS_MAX + 1])
        rt = sb("rt", [P, TT, 72])
        ridx = sb("ridx", [P, TT, 8], U32)

        ident = cst[:, C_ID:C_ID + P]

        def gcol(base, k):
            return vecT[:, base + k:base + k + 1]

        used = [0]

        def carve(n, pattern=None, **dims):
            v = arena[:, used[0]:used[0] + n]
            used[0] += n
            return v.rearrange(pattern, **dims) if pattern else v

        cq = carve(TT * QL, "p (t n) -> p t n", t=TT)
        ckv = carve(TT * KVL, "p (t n) -> p t n", t=TT)
        cqT = carve(3 * S, "p (k n) -> p k n", k=3)
        ckvT = carve(2 * S, "p (k n) -> p k n", k=2)
        qT = carve(MH * S, "p (k n) -> p k n", k=MH)
        qr = carve(TT * MH * ROPE, "p (t n) -> p t n", t=TT)
        qrT = carve(4 * S, "p (k n) -> p k n", k=4)
        krT = carve(S)
        kr = carve(TT * P, "p (t n) -> p t n", t=TT)
        probs = carve(MH * 3 * P, "p (k n) -> p k n", k=MH)
        pT = carve(2 * 3 * P, "p (k n) -> p k n", k=2)
        cosn = carve(TT * 2 * HALF, "p (t n) -> p t n", t=TT)
        ang = carve(6 * TT * HALF, "p (a t n) -> p a t n", a=6, t=TT)
        rtmp = carve(2 * MH * HALF, "p (a n) -> p a n", a=2)
        mstat = carve(MH * 8, "p (k n) -> p k n", k=MH)
        QK_BANK = (2, 3, 6, 7, 6, 7, 6, 7)
        kT = xn[:].rearrange("p t n -> p (t n)").rearrange("p (k n) -> p k n", k=MH)
        v_rows = xT[:].rearrange("p k n -> p (k n)").rearrange("p (t n) -> p t n", t=TT)
        oT = xT2
        used[0] = 2 * 6 * S
        fhhT_hi = over("fhhT_hi", [P, 6, S], "arena", 0)
        fhhT_lo = over("fhhT_lo", [P, 6, S], "arena", 6 * S)
        xT_hi = over("xT_hi", [P, KD, S], "xT", 0)
        xT_lo = over("xT_lo", [P, KD, S], "xT2", 0)
        w_hi = over("w_hi", [P, 2, SLOT // 2], "ring", 5 * SLOT)
        w_lo = over("w_lo", [P, 2, SLOT // 2], "ring", 6 * SLOT)
        fhh = carve(2 * FC, "p (a n) -> p a n", a=2)
        fsg = carve(2 * FC, "p (a n) -> p a n", a=2)
        BIAS0 = used[0]
        bias0 = carve(AH * P, "p (k n) -> p k n", k=AH)
        bias1 = carve(AH * S, "p (k n) -> p k n", k=AH)
        onehot = sb("onehot", [P, 2, 3, P], BF16)
        assert used[0] <= 12288
        posq_i = sb("posq_i", [P, S], I32)
        posq = sb("posq", [P, S])
        posk_i = sb("posk_i", [P, 96], I32)
        posk = sb("posk", [P, 96])
        tabs_h = sb("tabs_h", [P, 2, 64])
        tabs = sb("tabs", [P, 64])
        tab_parts = sb("tab_parts", [P, 3, 64], BF16)
        used[0] = 0
        SCATTER_BANK = (7, 5, 6, 2)
        SWO_BANK = (5, 3, 0, 1)
        Q_BANK = (0, 5, 5, 5)
        sqT = carve(G * S, "p (k n) -> p k n", k=G)
        skT = carve(S)
        sv = carve(TT * P, "p (t n) -> p t n", t=TT)
        spT = carve(2 * 3 * P, "p (k n) -> p k n", k=2)
        grow = carve(D)
        assert used[0] <= BIAS0
        used[0] = BIAS0 + AH * 3 * P
        sstat = carve(8 * 2 * AH, "p (a b n) -> p a b n", a=8, b=2)
        soT = xT2
        bo_row = xn[:, 0, :]
        used[0] = 0
        sel = carve(TT * SLOTS, "p (t n) -> p t n", t=TT)
        selg = carve(TT * SLOTS, "p (t n) -> p t n", t=TT)
        sgt = carve(TT * P, "p (t n) -> p t n", t=TT)
        xgT = carve(KD * SLOTS, "p (k n) -> p k n", k=KD)
        hh = carve(2 * FC, "p (a n) -> p a n", a=2)
        sg = carve(2 * FC, "p (a n) -> p a n", a=2)
        upl = carve(2 * FC, "p (a n) -> p a n", a=2)
        hhT = carve(2 * 4 * SLOTS, "p (a j n) -> p a j n", a=2, j=4)
        ysb = carve(D)
        gfin = xT2[:].rearrange("p k n -> p (k n)")[:, 0:D]
        AHEAD = RING
        ahead = arena[:, 12288 - SLOT:12288]
        assert used[0] <= 12288 - SLOT

        BIAS_ROUNDS = S // 8

        def rows_of(w):
            return w.rearrange("(k p) n -> p k n", p=P)

        win, wuq, wukv, wo = (rows_of(w[0]) for w in (w_in, w_uq, w_ukv, w_o))
        fg, fu, fd = (rows_of(w[0]) for w in (f_gate, f_up, f_down))
        kvw, swq, swo = rows_of(kv_w), rows_of(swa_w_q[0]), rows_of(swa_w_o[0])
        stream = [
            ("win_q", win[:, :, 0:QL], KD, QL, s.latq_mm, 2),
            ("win_kv", win[:, :, QL:QL + KVL + ROPE], KD, KVL + ROPE, s.latkv_mm, 2),
            ("uq0", wuq[:, :, 0:768], 3, 768, s.qrope_mm, 2),
            ("uq1", wuq[:, :, 768:1536], 3, 768, s.qrope_mm, 4),
            ("ukv", wukv, 2, 2048, s.ukv_v_mm, 4),
            ("wo0", wo[:, :, 0:512], KD, 512, s.wo_mm, 4),
            ("wo1", wo[:, :, 512:1024], KD, 512, s.wo_mm, 4),
        ]

        def f_cols(c):
            return min(FC, DFF - c * FC)

        units = []
        for c in range(FCH):
            nk = SLOT // 2 // f_cols(c)
            for kind in "gu":
                units += [(kind, c, k0, nk, f_cols(c)) for k0 in range(0, KD, nk)]
            if c >= 1:
                units += [("d", c - 1, half, f_cols(c - 1) // P, 512) for half in range(2)]
        units.append(("d", FCH - 1, 0, f_cols(FCH - 1) // P, D))
        NU = len(units)

        def units_of(kind, c):
            return [q for q, u in enumerate(units) if u[0] == kind and u[1] == c]

        downs = [(c, t, half, units_of("d", c)[half]) for c in range(FCH - 1) for half in range(2) for t in range(TT)]
        downs += [(FCH - 1, t, half, NU - 1) for t in range(TT) for half in range(2)]

        def used_up(q):
            if units[q][0] == "d":
                return s.fdown_mm, 1 + max(n for n, d in enumerate(downs) if d[3] == q)
            return s.fgu_mm, sum(1 for u in units[:q + 1] if u[0] != "d")

        rows_T_after = {(0, 0): units_of("g", 1)[0], (0, 1): units_of("g", 1)[1]}
        for c in range(1, FCH - 1):
            rows_T_after[(c, 0)] = units_of("d", c - 1)[1]
            rows_T_after[(c, 1)] = units_of("g", c + 1)[0]
        for t in range(TT):
            rows_T_after[(FCH - 1, t)] = units_of("d", FCH - 2)[0]

        def rows_T_of(q):
            return [ct for ct in rows_T_after if rows_T_after[ct] == q]

        BIAS_UNIT0 = 1
        assert BIAS_UNIT0 + BIAS_ROUNDS <= NU

        def bias_round_of(q):
            return q - BIAS_UNIT0 if 0 <= q - BIAS_UNIT0 < BIAS_ROUNDS else None

        def ffn_piece(kind, c):
            name, n, last = "f%s%d" % (kind, c), f_cols(c), units_of(kind, c)[-1]
            if kind == "d":
                return (name, fd[:, 4 * c:4 * c + n // P, :], n // P, D, s.wlo_ready, last + 1)
            return (name, (fg if kind == "g" else fu)[:, :, c * FC:c * FC + n], KD, n, s.wlo_ready, last + 1)

        for c in range(FCH):
            stream += [ffn_piece("g", c), ffn_piece("u", c)]
            if c >= 1:
                stream.append(ffn_piece("d", c - 1))
        stream.append(ffn_piece("d", FCH - 1))
        stream += [
            ("kvw", kvw, KD, 256, s.sv_mm, 2),
            ("wq0", swq[:, 0:4, :], 4, D, s.sq_mm, 4),
            ("wq1", swq[:, 4:8, :], 4, D, s.sq_mm, 4),
            ("swo0", swo[:, :, 0:512], KD, 512, s.swo_mm, 4),
            ("swo1", swo[:, :, 512:1024], KD, 512, s.swo_mm, 4),
        ]
        DENSE = len(stream)
        where = {t[0]: n for n, t in enumerate(stream)}
        slot_of = [5, 6] + [n % 5 for n in range(DENSE - 2)]
        fill_of = [sum(1 for m in range(n + 1) if slot_of[m] == slot_of[n]) for n in range(DENSE)]
        expert_slots = [5, 6] + [slot_of[n] for n in range(DENSE - 5, DENSE)]
        assert sorted(expert_slots) == list(range(RING))

        def earlier_fill(n, slot):
            return max([m for m in range(n) if slot_of[m] == slot], default=None)

        def w_of(name):
            n = where[name]
            _, _, k, cols, _, _ = stream[n]
            return ring[:, slot_of[n], 0:k * cols].rearrange("p (k n) -> p k n", k=k)

        def weights_here(eng, name):
            n = where[name]
            eng.wait_ge(slot_landed[slot_of[n]], 16 * fill_of[n])

        def unit_of_weights(q):
            kind, c, k0, nk, cols = units[q]
            w = w_of("f%s%d" % (kind, c))
            w = w[:, :, k0 * cols:(k0 + 1) * cols] if kind == "d" else w[:, k0:k0 + nk, :]
            return [w] + [v[:, q % 2, 0:nk * cols].rearrange("p (k n) -> p k n", k=nk) for v in (w_hi, w_lo)]

        pieces = [("g", 0), ("u", 0), ("g", 1), ("u", 1)]
        for c in range(2, ECH):
            pieces += [("g", c), ("u", c), ("d", c - 2)]
        pieces += [("d", ECH - 2), ("d", ECH - 1)]
        NP = len(pieces)
        assert NP % RING == 0
        ppos = {p_: m for m, p_ in enumerate(pieces)}
        dense_fills = [slot_of.count(sl) for sl in range(RING)]

        def piece_here(eng, i, kind, c):
            m = ppos[(kind, c)]
            sl = expert_slots[m % RING]
            eng.wait_ge(slot_landed[sl], i * (16 * NP // RING) + 16 * (dense_fills[sl] + m // RING + 1))

        def piece(kind, c):
            sl = expert_slots[ppos[(kind, c)] % RING]
            return ring[:, sl, :].rearrange("p (k n) -> p k n", k=4 if kind == "d" else KD)

        eg = e_gate[0].rearrange("e (k p) f -> p e k f", p=P)
        eu = e_up[0].rearrange("e (k p) f -> p e k f", p=P)
        ed = e_down[0].rearrange("e (k p) n -> p e k n", p=P)

        def x_gained(t, b):
            v = (fsg if t == 0 else fhh)[:, b, :]
            return v.rearrange("p (k n) -> p k n", k=4)

        def hidden_T_place(part, c, t):
            j0 = 0 if c < FCH - 1 else 4
            return part[:, j0:j0 + f_cols(c) // P, t * P:(t + 1) * P]

        def hidden_T_rows(part, c):
            j0 = 0 if c < FCH - 1 else 4
            return part[:, j0:j0 + f_cols(c) // P, :]

        def hidden_T_bank(c, t):
            c0 = 0 if c < FCH - 1 else t * f_cols(c)
            return ps[:, 4, c0:c0 + f_cols(c)].rearrange("p (j n) -> p j n", n=P)

        def both_or(c, t):
            return 2 * FCH if c == FCH - 1 else 2 * c + t + 1

        block = ctx.enter_context(nc.Block())

        @block.sync
        def _(sp):
            for t, landed in enumerate((s.x_loaded0, s.x_loaded1)):
                sp.dma_start(h[:, t, :], x[0, t * P:(t + 1) * P, :]).then_inc(landed, 16)
            loads = [
                (vecs[V_GA0:V_GA0 + 8, :], g_attn[0].rearrange("(k n) -> k n", n=P)),
                (vecs[V_GF0:V_GF0 + 8, :], g_ffn[0].rearrange("(k n) -> k n", n=P)),
                (vecs[V_GA1:V_GA1 + 8, :], g_attn[1].rearrange("(k n) -> k n", n=P)),
                (vecs[V_KVG:V_KVG + 8, :], kv_g.rearrange("(k n) -> k n", n=P)),
                (vecs[V_GQ:V_GQ + 3, :], g_q[0].rearrange("(k n) -> k n", n=P)),
                (vecs[V_GKV:V_GKV + 2, :], g_kv[0].rearrange("(k n) -> k n", n=P)),
                (vecs[V_KVB:V_KVB + 1, :], kv_b[0:P].rearrange("(k n) -> k n", n=P)),
                (vecs[V_BQ:V_BQ + G, 0:HD], swa_b_q[0, 0:512].rearrange("(k n) -> k n", n=HD)),
                (vecs[V_BQ:V_BQ + G, HD:P], swa_b_q[0, 512:1024].rearrange("(k n) -> k n", n=HD)),
                (pos_i[:], positions[0].rearrange("(t p) -> p t", p=P)),
            ]
            sp.dma_start(cst[:], consts).then_inc(s.consts_loaded, 16)
            for dst, src in loads:
                sp.dma_start(dst, src, allow_slow_non_contiguous=dst.dtype == I32).then_inc(s.smalls_loaded, 16)
            for n, (name, src, k, cols, _, _) in enumerate(stream):
                old = earlier_fill(n, slot_of[n])
                if old is not None:
                    sp.wait_ge(stream[old][4], stream[old][5])
                sp.dma_start(w_of(name), src).then_inc(slot_landed[slot_of[n]], 16)

            def load_item(i, expert, first):
                for m, (kind, c) in enumerate(pieces):
                    if first and m == RING - 2:
                        sp.wait_ge(s.spT_mm, AH)
                        k0, c0 = pieces[AHEAD]
                        assert k0 == "g"
                        sp.dma_start(ahead.rearrange("p (k n) -> p k n", k=KD),
                                     eg[:, expert, :, c0 * FC:(c0 + 1) * FC]).then_inc(s.ahead_loaded, 16)
                    if first and m == AHEAD:
                        continue
                    if m < RING:
                        if first:
                            old = earlier_fill(DENSE, expert_slots[m])
                            sp.wait_ge(*(stream[old][4:6] if m >= 2 else used_up(NU - 1)))
                        else:
                            k0, c0 = pieces[m - RING + NP]
                            sp.wait_ge(s.down_mm if k0 == "d" else s.gu_mm, i * ECH + (c0 + 2 - ECH))
                    else:
                        k0, c0 = pieces[m - RING]
                        sp.wait_ge(s.down_mm if k0 == "d" else s.gu_mm, i * ECH + (c0 + 2))
                    if kind == "d":
                        src = ed[:, expert, 4 * c:4 * c + 4, :]
                    else:
                        src = (eg if kind == "g" else eu)[:, expert, :, c * FC:(c + 1) * FC]
                    sp.dma_start(piece(kind, c), src).then_inc(slot_landed[expert_slots[m % RING]], 16)

            load_item(0, 0, True)
            with sp.Fori(1, NE) as i:
                load_item(i, i, False)
            sp.wait_ge(s.counts_ready, 1)
            items = sp.value_load(n_items[0:1, 0:1], min_val=NE, max_val=ITEMS_MAX)
            for sweep in range(1, SWEEPS):
                with sp.If(items > sweep * NE):
                    with sp.Fori(0, NE) as e:
                        load_item(e + sweep * NE, e, False)
                with sp.Else():
                    sp.nop()
            sp.wait_ge(s.out_stored, 32)

        @block.gpsimd
        def _(pool):
            more = [
                (posq_i[:], positions[0:1, :].to_broadcast([P, S])),
                (kvb_row[:], kv_b[P:2 * P].rearrange("(a n) -> a n", a=1)),
                (wr[:], w_router[0].rearrange("(k p) e -> p k e", p=P)),
                (sinks_h[:], swa_sinks[0:1, :].to_broadcast([P, AH])),
            ]
            for kk in range(4):
                more.append((posk_i[32 * kk:32 * kk + 32, 0:64], positions[0:1, 64 * kk:64 * kk + 64].to_broadcast([32, 64])))
                more.append((posk_i[32 * kk:32 * kk + 32, 64:96], positions[0:1, 32 * kk:32 * kk + 32].to_broadcast([32, 32])))
            done = [0]

            def rstd(dst, src, n=1):
                done[0] += 1
                pool.wait_ge(s.ms_ready, done[0])
                nc.gpsimd.tensor_tensor(stat[:, dst:dst + n], stat[:, src:src + n], cst[:, C_MH:C_MH + n], ALU.pow).then_inc(s.rstd_ready, 1)

            def rstd_rows():
                for t in range(TT):
                    rstd(4 + t, 2 + t)

            pool.wait_ge(s.consts_loaded, 16)
            rstd_rows()
            for dst, src in more:
                pool.dma_start(dst, src).then_inc(s.biasrows_loaded, 16)
            rstd(12, 8, 2)
            rstd(14, 10, 2)
            nc.gpsimd.memset(tabs_h[:], 0.0).then_inc(s.pool_chain, 1)
            pool.wait_ge(s.pool_chain, 1)
            for kk in range(4):
                c = slice(AH * kk, AH * kk + AH)
                pool.dma_start(tabs_h[32 * kk:32 * kk + 32, 0, c], rel_bias).then_inc(s.rel_loaded, 16)
                pool.dma_start(tabs_h[32 * kk + 1:32 * kk + 32, 1, c], rel_bias[0:31, :]).then_inc(s.rel_loaded, 16)
            rstd_rows()
            rstd_rows()
            pool.wait_ge(s.sv_mm, 2)
            pool.dma_start(bo_row, swa_b_o[0:1, :].to_broadcast([P, D])).then_inc(s.rel_loaded, 16)
            pool.dma_start(grow, g_ffn[1:2, :].to_broadcast([P, D])).then_inc(s.rel_loaded, 16)
            pool.wait_ge(s.rel_loaded, 16 * 10)
            pool.wait_ge(s.xn_ready, 6)
            for t in range(TT):
                nc.gpsimd.tensor_tensor(h[:, t, :], h[:, t, :], bo_row, ALU.add).then_inc(s.bo_added, 1)
            rstd_rows()
            pool.wait_ge(s.swo_mm, 4)
            pool.dma_start(gfin, g_final.rearrange("(a n) -> a n", a=1).to_broadcast([P, D])).then_inc(s.rel_loaded, 16)
            pool.wait_ge(s.ahead_loaded, 16)
            pool.wait_ge(s.gu_mm, 2)
            nc.gpsimd.tensor_copy(ring[:, expert_slots[AHEAD % RING], :], ahead).then_inc(slot_landed[expert_slots[AHEAD % RING]], 16)
            rstd_rows()

        @block.scalar
        def _(act):
            def squares(t):
                act.activation(xn[:, t, :], h[:, t, :], ACT.Square, accum_out=stat[:, t:t + 1]).then_inc(s.ssq_ready, 1)

            act.wait_ge(s.x_loaded0, 16)
            squares(0)
            act.wait_ge(s.x_loaded1, 16)
            squares(1)
            act.wait_ge(s.vecT_mm, 1)
            act.copy(vecT[:], ps[:, 0, 0:V_N]).then_inc(s.vecT_ready, 1)
            act.wait_ge(s.rope_arg, 2)
            act.activation(cosn[:, :, HALF:2 * HALF], ang[:, 4], ACT.Sin).then_inc(s.sincos_ready, 1)
            act.activation(cosn[:, :, 0:HALF], ang[:, 5], ACT.Sin).then_inc(s.sincos_ready, 1)

            for t in range(TT):
                act.wait_ge(s.latq_mm, t + 1)
                act.activation(cq[:, t, :], ps[:, 4 + t, 0:QL], ACT.Square, accum_out=stat[:, t:t + 1]).then_inc(s.ssq_ready, 1)
            for t in range(TT):
                act.wait_ge(s.latkv_mm, t + 1)
                act.activation(ckv[:, t, :], ps[:, 6 + t, 0:KVL], ACT.Square, accum_out=stat[:, 6 + t:7 + t]).then_inc(s.ssq_ready, 1)
            for u in range(8):
                if u == 2:
                    act.wait_ge(s.cT_mm, 2)
                    for k in range(2):
                        act.activation(ckvT[:, k, :], ps[:, 0, k * S:(k + 1) * S], ACT.Copy, scale=gcol(V_GKV, k)).then_inc(s.ckvT_ready, 1)
                    act.wait_ge(s.cT_mm, 3)
                    act.copy(krT, ps[:, 1, 0:S]).then_inc(s.krT_ready, 1)
                act.wait_ge(s.qk_mm, u + 1)
                dst = qT if u < 4 else kT
                act.copy(dst[:, 2 * (u % 4):2 * (u % 4) + 2, :], ps[:, QK_BANK[u], :].rearrange("p (k n) -> p k n", k=2)).then_inc(s.qk_ready, 1)
            for n in range(4):
                t, half = n // 2, n % 2
                act.wait_ge(s.ukv_v_mm, n + 1)
                act.copy(v_rows[:, t, half * 512:(half + 1) * 512], ps[:, n, :]).then_inc(s.v_ready, 1)
            for i in range(MH + 1):
                if i < MH:
                    act.wait_ge(s.negmax_ready, 2 * i + 2)
                    st = mstat[:, i, :]
                    act.activation(probs[:, i, 0:P], probs[:, i, 0:P], ACT.Exp, scale=MLA_SCALE, bias=st[:, 2:3],
                                   accum_out=st[:, 4:5]).then_inc(s.exp_ready, 1)
                    act.activation(probs[:, i, P:3 * P], probs[:, i, P:3 * P], ACT.Exp, scale=MLA_SCALE, bias=st[:, 3:4],
                                   accum_out=st[:, 5:6]).then_inc(s.exp_ready, 1)
                if i >= 1:
                    act.wait_ge(s.pT_mm, i)
                    if i >= 3:
                        act.wait_ge(s.pv_mm, i - 2)
                    act.copy(pT[:, (i - 1) % 2, :], ps[:, 4 + (i - 1) % 2, 0:3 * P]).then_inc(s.pT_ready, 1)
            def w_hi_part(q):
                w, hi, _ = unit_of_weights(q)
                weights_here(act, "f%s%d" % units[q][:2])
                if q >= 2:
                    act.wait_ge(*used_up(q - 2))
                act.copy(hi, w).then_inc(s.whi_ready, 1)

            w_hi_part(0)
            w_hi_part(1)
            for t in range(TT):
                act.wait_ge(s.h_attn0, 2 * t + 2)
                squares(t)
                for b in range(2):
                    act.wait_ge(s.xg_ready, 2 * t + b + 1)
                    act.copy(xT_hi[:, 4 * b:4 * b + 4, t * P:(t + 1) * P], x_gained(t, b)).then_inc(s.xhi_ready, 1)
            for q in range(2, NU + 2):
                if q < NU:
                    w_hi_part(q)
                kind, c = units[q - 2][:2]
                if kind == "g" and q - 2 == units_of("g", c)[-1]:
                    n = f_cols(c)
                    act.wait_ge(*used_up(q - 2))
                    if c >= 1:
                        act.wait_ge(s.fhh_ready, 2 * c)
                    for t in range(TT):
                        act.activation(fsg[:, t, 0:n], ps[:, 2 * t, 0:n], ACT.Silu).then_inc(s.fsg_ready, 1)
                for c, t in rows_T_of(q - 2):
                    act.wait_ge(s.ftr_mm, both_or(c, t))
                    if 1 <= c < FCH - 1:
                        act.wait_ge(*used_up(units_of("d", c - 1)[-1]))
                    act.copy(hidden_T_place(fhhT_hi, c, t), hidden_T_bank(c, t)).then_inc(s.fhhT_hi_ready, 1)
            for t in range(TT):
                act.wait_ge(s.fh_added, 4 * FCH - 2 * (TT - 1 - t))
                squares(t)
            act.wait_ge(s.kT_mm, 2)
            act.activation(skT, ps[:, 4, 0:S], ACT.Identity, bias=gcol(V_KVB, 0)).then_inc(s.kT_ready, 1)
            for t in range(TT):
                act.wait_ge(s.sv_mm, t + 1)
                act.copy(sv[:, t, :], ps[:, 7 if t == 0 else 5, 0:P]).then_inc(s.sv_ready, 1)

            def sq_evac(u):
                act.wait_ge(s.sq_mm, u + 1)
                for j in range(2):
                    g = 2 * u + j
                    act.activation(sqT[:, g, :], ps[:, Q_BANK[u], j * S:(j + 1) * S], ACT.Identity, bias=gcol(V_BQ, g)).then_inc(s.sq_ready, 1)

            def sexp(i):
                act.wait_ge(s.snegmax_ready, i // 4 + 1)
                if i % 4 == 0:
                    act.activation(sstat[:, 3, :, i:i + 4], sstat[:, 2, :, i:i + 4], ACT.Exp).then_inc(s.esink_ready, 1)
                act.activation(bias0[:, i, :], bias0[:, i, :], ACT.Exp, bias=sstat[:, 1, 0, i:i + 1],
                               accum_out=sstat[:, 4, 0, i:i + 1]).then_inc(s.sexp_ready, 1)
                act.activation(bias1[:, i, :], bias1[:, i, :], ACT.Exp, bias=sstat[:, 1, 1, i:i + 1],
                               accum_out=sstat[:, 4, 1, i:i + 1]).then_inc(s.sexp_ready, 1)

            def spT_evac(i):
                act.wait_ge(s.spT_mm, i + 1)
                if i >= 2:
                    act.wait_ge(s.spv_mm, i - 1)
                act.copy(spT[:, i % 2, :], ps[:, i % 2, 0:3 * P]).then_inc(s.spT_ready, 1)

            def swa_out(i):
                g, v = i // 2, i % 2
                part = 64 * (g % 2)
                act.wait_ge(s.spv_mm, i + 1)
                act.copy(soT[part:part + 64, 4 * v + g // 2, :], ps[part:part + 64, 6 + i % 2, 0:S]).then_inc(s.soT_ready, 1)

            sq_evac(0)
            sq_evac(1)

            def quad_exp(q):
                for j in range(4):
                    sexp(4 * q + j)

            def quad_out(q, pending, last):
                for i in range(4 * q, 4 * q + 4):
                    spT_evac(i)
                    if i > 4 * q or pending:
                        swa_out(i - 1)
                if last:
                    swa_out(4 * q + 3)

            quad_exp(0)
            sq_evac(2)
            quad_out(0, False, False)
            quad_exp(1)
            sq_evac(3)
            quad_out(1, True, True)
            quad_exp(2)
            quad_out(2, False, True)
            quad_exp(3)
            quad_out(3, False, True)
            for t in range(TT):
                act.wait_ge(s.h_attn1, 2 * t + 2)
                squares(t)
            act.wait_ge(s.gate_arg, 1)
            act.activation(rt[:, :, 49:50], rt[:, :, 48:49], ACT.Exp).then_inc(s.gate_exp, 1)

            def silu_and_last(i, c, narrow):
                a = c % 2
                act.wait_ge(s.gu_mm, i * ECH + (c + 2))
                act.wait_ge(s.hh_ready, i * (2 * ECH) + (2 * max(c - 1, 0) + 1))
                if narrow:
                    act.activation(sg[0:NARROW, a, :], ps[0:NARROW, 2 * a, :], ACT.Silu).then_inc(s.sg_ready, 1)
                    act.copy(upl[0:NARROW, a, :], ps[64:64 + NARROW, 2 * a + 1, :]).then_inc(s.sg_ready, 3)
                    return
                act.activation(sg[0:SLOTS, a, :], ps[0:SLOTS, 2 * a, :], ACT.Silu).then_inc(s.sg_ready, 1)
                act.copy(upl[0:NARROW, a, LASTQ:FC], ps[64:64 + NARROW, 2 * a + 1, 0:LASTQ]).then_inc(s.sg_ready, 1)
                act.copy(upl[NARROW:SLOTS, a, :], ps[SLOTS:P, 2 * a, :]).then_inc(s.sg_ready, 2)

            def hhT_evac(i, c, narrow):
                act.wait_ge(s.tr_mm, i * ECH + (c + 2))
                act.wait_ge(s.down_mm, i * ECH + (max(c - 1, 0) + 1))
                m = NARROW if narrow else SLOTS
                act.copy(hhT[:, c % 2, :, 0:m], ps[:, 4, 0:4 * SLOTS].rearrange("p (j n) -> p j n", j=4)[:, :, 0:m]).then_inc(s.hhT_ready, 1)

            act.sem_inc(s.sg_ready, 1)
            act.sem_inc(s.hhT_ready, 1)
            act.sem_inc(s.y_ready_a, 1)
            act.sem_inc(s.sgt_ready, 1)
            act.wait_ge(s.gath_mm, 2)
            act.copy(xgT[:, 4:8, :].rearrange("p k n -> p (k n)"), ps[:, 3, 0:4 * SLOTS]).then_inc(s.xgT_ready_a, 2)
            act.wait_ge(s.counts_ready, 1)
            items = act.value_load(n_items[0:1, 0:1], min_val=NE, max_val=ITEMS_MAX)

            def act_item(i, narrow):
                for c in range(ECH):
                    silu_and_last(i, c, narrow)
                    if c == 4:
                        act.wait_ge(s.sgt_mm, i + 2)
                        act.copy(sgt[0:SLOTS].rearrange("p t n -> p (t n)"), ps[0:SLOTS, 7, 0:S]).then_inc(s.sgt_ready, 1)
                    if c >= 1:
                        hhT_evac(i, c - 1, narrow)
                act.wait_ge(s.gath_mm, i + 3)
                act.copy(xgT[:, 4:8, :].rearrange("p k n -> p (k n)"), ps[:, 3, 0:4 * SLOTS]).then_inc(s.xgT_ready_a, 1)
                hhT_evac(i, ECH - 1, narrow)
                act.wait_ge(s.down_mm, i * ECH + (ECH + 1))
                if narrow:
                    act.copy(ysb[0:NARROW, 0:512], ps[0:NARROW, 5, :]).then_inc(s.y_ready_a, 1)
                    return
                act.copy(ysb[NARROW:SLOTS, 512:1024], ps[SLOTS:P, 5, :]).then_inc(s.act_chain, 1)
                act.copy(ysb[0:SLOTS, 0:512], ps[0:SLOTS, 5, :]).then_inc(s.y_ready_a, 1)

            with act.Fori(0, items) as i:
                many = act.value_load(wide[0:1, bass.ds(i, 1)], min_val=0, max_val=1)
                with act.If(many > 0):
                    act_item(i, False)
                with act.Else():
                    act_item(i, True)
            for t in range(TT):
                act.wait_ge(s.h_added, items * 4 + (2 * t + 3))
                act.activation(xT[:].rearrange("p k n -> p (k n)")[:, t * D:(t + 1) * D], h[:, t, :], ACT.Square,
                               accum_out=stat[:, t:t + 1]).then_inc(s.ssq_ready, 1)
            orow = out[0].rearrange("(t p) d -> t p d", p=P)
            for t in range(TT):
                act.wait_ge(s.xn_ready, 9 + t)
                act.dma_start(orow[t], xn[:, t, :]).then_inc(s.out_stored, 16)

        @block.tensor
        def _(pe):
            def rows_to_T(n, t, off):
                pe.wait_ge(s.xn_ready, 2 * n + t + 1)
                for k in range(KD):
                    mm = pe.transpose(ps[:, off + 2 * t + k // 4, (k % 4) * P:(k % 4 + 1) * P], xn[:, t, k * P:(k + 1) * P], ident)
                mm.then_inc(s.xT_mm, 1)

            pe.wait_ge(s.consts_loaded, 16)
            pe.wait_ge(s.smalls_loaded, 160)
            pe.transpose(ps[:, 0, 0:V_N], vecs[:], ident[0:V_N, 0:V_N]).then_inc(s.vecT_mm, 1)
            pe.wait_ge(s.vecT_ready, 1)
            rows_to_T(0, 0, 0)
            rows_to_T(0, 1, 0)
            for name, bank, n, sem in (("win_q", 4, QL, s.latq_mm), ("win_kv", 6, KVL + ROPE, s.latkv_mm)):
                weights_here(pe, name)
                w = w_of(name)
                for t in range(TT):
                    pe.wait_ge(s.xT_ready, 2 * t + 2)
                    for k in range(KD):
                        mm = pe.matmul(ps[:, bank + t, 0:n], xT[:, k, t * P:(t + 1) * P], w[:, k, :],
                                       start=(k == 0), stop=(k == KD - 1))
                    mm.then_inc(sem, 1)
            pe.wait_ge(s.cq_ready, 2)
            for k in range(3):
                for t in range(TT):
                    mm = pe.transpose(ps[:, k // 2, (k % 2) * S + t * P:(k % 2) * S + (t + 1) * P],
                                      cq[:, t, k * P:(k + 1) * P], ident)
            mm.then_inc(s.cT_mm, 1)
            pe.wait_ge(s.cqT_ready, 3)
            for half in range(2):
                if half == 1:
                    pe.wait_ge(s.ckv_ready, 2)
                    for k in range(2):
                        for t in range(TT):
                            mm = pe.transpose(ps[:, 0, k * S + t * P:k * S + (t + 1) * P], ckv[:, t, k * P:(k + 1) * P], ident)
                    mm.then_inc(s.cT_mm, 1)
                    pe.wait_ge(s.krope_ready, 2)
                    for t in range(TT):
                        mm = pe.transpose(ps[:, 1, t * P:(t + 1) * P], kr[:, t, :], ident)
                    mm.then_inc(s.cT_mm, 1)
                weights_here(pe, "uq%d" % half)
                w = w_of("uq%d" % half)
                for u in (2 * half, 2 * half + 1):
                    if u >= 2:
                        pe.wait_ge(s.qk_ready, u - 1)
                    for j in range(2):
                        hl = 2 * (u % 2) + j
                        for k in range(3):
                            mm = pe.matmul(ps[:, QK_BANK[u], j * S:(j + 1) * S], w[:, k, hl * 192:hl * 192 + NOPE], cqT[:, k, :],
                                           start=(k == 0), stop=(k == 2))
                    mm.then_inc(s.qk_mm, 1)
                for t in range(TT):
                    for k in range(3):
                        r = w[:, k, :].rearrange("p (h n) -> p h n", n=192)[:, :, NOPE:192]
                        mm = pe.matmul(ps[:, 4 + t, half * S:(half + 1) * S], cqT[:, k, t * P:(t + 1) * P], r,
                                       start=(k == 0), stop=(k == 2))
                    mm.then_inc(s.qrope_mm, 1)
            pe.wait_ge(s.ckvT_ready, 2)
            weights_here(pe, "ukv")
            w = w_of("ukv")
            for u in range(4, 8):
                pe.wait_ge(s.qk_ready, u - 1)
                for j in range(2):
                    hd = 2 * (u - 4) + j
                    for k in range(2):
                        mm = pe.matmul(ps[:, QK_BANK[u], j * S:(j + 1) * S], w[:, k, hd * 256:hd * 256 + NOPE], ckvT[:, k, :],
                                       start=(k == 0), stop=(k == 1))
                mm.then_inc(s.qk_mm, 1)
            pe.wait_ge(s.krT_ready, 1)
            for n in range(4):
                t, half = n // 2, n % 2
                for k in range(2):
                    r = w[:, k, :].rearrange("p (h n) -> p h n", n=256)[:, 4 * half:4 * half + 4, NOPE:256]
                    mm = pe.matmul(ps[:, n, :], ckvT[:, k, t * P:(t + 1) * P], r, start=(k == 0), stop=(k == 1))
                mm.then_inc(s.ukv_v_mm, 1)
            pe.wait_ge(s.qrope_ready, 4)
            for k in range(4):
                for t in range(TT):
                    mm = pe.transpose(ps[:, 4 + k // 2, (k % 2) * S + t * P:(k % 2) * S + (t + 1) * P],
                                      qr[:, t, k * P:(k + 1) * P], ident)
            mm.then_inc(s.qrT_mm, 1)

            def scores(i):
                b, part = i % 4, 64 * (i % 2)
                if i >= 4:
                    pe.wait_ge(s.s_ready, i - 3)
                for t, c0, n in ((0, 0, P), (1, P, 2 * P)):
                    pe.matmul(ps[:, b, c0:c0 + n], qT[:, i, t * P:(t + 1) * P], kT[:, i, 0:n], start=True, stop=False)
                    mm = pe.matmul(ps[:, b, c0:c0 + n], qrT[part:part + 64, i // 2, t * P:(t + 1) * P], krT[part:part + 64, 0:n],
                                   start=False, stop=True)
                mm.then_inc(s.score_mm, 1)

            def probs_T(i):
                pe.wait_ge(s.p_ready, 2 * i + 2)
                if i >= 2:
                    pe.wait_ge(s.pT_ready, i - 1)
                for b in range(3):
                    mm = pe.transpose(ps[:, 4 + i % 2, b * P:(b + 1) * P], probs[:, i, b * P:(b + 1) * P], ident)
                mm.then_inc(s.pT_mm, 1)

            def pv(i):
                pe.wait_ge(s.pT_ready, i + 1)
                if i >= 2:
                    pe.wait_ge(s.oT_ready, i - 1)
                o = ps[:, 6 + i % 2, :]
                v0, v1 = (v_rows[:, t, i * VH:(i + 1) * VH] for t in range(TT))
                pe.matmul(o[:, 0:P], v0, pT[:, i % 2, 0:P], start=True, stop=True)
                pe.matmul(o[:, P:S], v0, pT[:, i % 2, P:S], start=True, stop=False)
                pe.matmul(o[:, P:S], v1, pT[:, i % 2, S:3 * P], start=False, stop=True).then_inc(s.pv_mm, 1)

            pe.wait_ge(s.qk_ready, 8)
            pe.wait_ge(s.v_ready, 4)
            pe.wait_ge(s.qrT_ready, 4)
            for i in range(4):
                scores(i)
            for i in range(MH + 1):
                if i < MH:
                    probs_T(i)
                if i >= 1:
                    pv(i - 1)
                if i + 4 < MH:
                    scores(i + 4)
            pe.wait_ge(s.oT_ready, MH)
            weights_here(pe, "wo0")
            weights_here(pe, "wo1")

            def out_product(name, T, t, half, sem):
                w = w_of("%s%d" % (name, half))
                for k in range(KD):
                    mm = pe.matmul(ps[:, 2 * t + half, :], T[:, k, t * P:(t + 1) * P], w[:, k, :], start=(k == 0), stop=(k == KD - 1))
                mm.then_inc(sem, 1)

            out_product("wo", oT, 0, 0, s.wo_mm)
            out_product("wo", oT, 0, 1, s.wo_mm)
            out_product("wo", oT, 1, 0, s.wo_mm)
            rows_to_T(1, 0, 4)
            out_product("wo", oT, 1, 1, s.wo_mm)

            def ffn_passes(out, lhs, rhs_hi, rhs_lo, nk, first, last, t):
                c = slice(t * P, (t + 1) * P)
                for k in range(nk):
                    pe.matmul(out, lhs[0][:, k, c], rhs_hi[:, k, :], start=(first and k == 0), stop=False)
                    pe.matmul(out, lhs[1][:, k, c], rhs_hi[:, k, :], start=False, stop=False)
                yield
                for k in range(nk):
                    mm = pe.matmul(out, lhs[0][:, k, c], rhs_lo[:, k, :], start=False, stop=(last and k == nk - 1))
                yield mm

            def gu_passes(q, t):
                kind, c, k0, nk, cols = units[q]
                _, hi, lo = unit_of_weights(q)
                x = [v[:, k0:k0 + nk, :] for v in (xT_hi, xT_lo)]
                return ffn_passes(ps[:, 2 * t + (kind == "u"), 0:cols], x, hi, lo, nk, k0 == 0, k0 + nk == KD, t)

            def gu_unit(q):
                kind, c, k0, _, _ = units[q]
                if k0 == 0 and c >= 1:
                    pe.wait_ge(*((s.fsg_ready, 2 * c) if kind == "g" else (s.fhh_ready, 2 * c)))
                pe.wait_ge(s.whi_ready, q + 1)
                passes = [gu_passes(q, t) for t in range(TT)]
                for p_ in passes:
                    next(p_)
                bias_round(bias_round_of(q))
                pe.wait_ge(s.wlo_ready, q + 1)
                for p_ in passes:
                    mm = next(p_)
                mm.then_inc(s.fgu_mm, 1)

            def d_unit(q):
                c, nk = units[q][1], units[q][3]
                _, hi, lo = unit_of_weights(q)
                hid = [hidden_T_rows(v, c) for v in (fhhT_hi, fhhT_lo)]
                pe.wait_ge(s.whi_ready, q + 1)
                for n, (_, t, half, qd) in enumerate(downs):
                    if qd != q:
                        continue
                    pe.wait_ge(s.fhhT_hi_ready, 2 * c + t + 1)
                    pe.wait_ge(s.fhhT_lo_ready, 2 * c + t + 1)
                    if n >= 2:
                        pe.wait_ge(s.fh_added, n - 1)
                    h0 = half * 512 if c == FCH - 1 else 0
                    p_ = ffn_passes(ps[:, 5 + n % 2, :], hid, hi[:, :, h0:h0 + 512], lo[:, :, h0:h0 + 512], nk, True, True, t)
                    next(p_)
                    if n == 0 or downs[n - 1][3] != q:
                        bias_round(bias_round_of(q))
                        pe.wait_ge(s.wlo_ready, q + 1)
                    next(p_).then_inc(s.fdown_mm, 1)

            def ffn_T(c, t):
                pe.wait_ge(s.fhh_ready, 2 * c + t + 1)
                if (c, t) not in ((0, 0), (FCH - 1, 1)):
                    pe.wait_ge(s.fhhT_hi_ready, 2 * c + t)
                    pe.wait_ge(s.fhhT_lo_ready, 2 * c + t)
                bank = hidden_T_bank(c, t)
                for j in range(f_cols(c) // P):
                    mm = pe.transpose(bank[:, j, :], fhh[:, t, j * P:(j + 1) * P], ident)
                mm.then_inc(s.ftr_mm, 1)

            def bias_round(r):
                if r is None:
                    return
                pe.wait_ge(s.onehot_ready, 3 * r + 3)
                if r == 0:
                    pe.wait_ge(s.delta_ready, 3)
                else:
                    pe.wait_ge(s.bias_ready, 2 * r)
                for j in range(3):
                    for n in range(3):
                        mm = pe.matmul(ps[:, 7, j * 64:(j + 1) * 64], onehot[:, r % 2, j, :], tab_parts[:, n, :], start=(n == 0), stop=(n == 2))
                mm.then_inc(s.bias_mm, 1)

            pe.wait_ge(s.xT_ready, 6)
            pe.wait_ge(s.whi_ready, 2)
            pe.wait_ge(s.wlo_ready, 2)
            for t in range(TT):
                if t == 1:
                    rows_to_T(1, 1, 4)
                    pe.wait_ge(s.xT_ready, 8)
                for q in range(2):
                    p_ = gu_passes(q, t)
                    next(p_)
                    mm = next(p_)
                    if t == 1:
                        mm.then_inc(s.fgu_mm, 1)
            bias_round(bias_round_of(1))
            for q in range(2, NU):
                (d_unit if units[q][0] == "d" else gu_unit)(q)
                for c, t in rows_T_of(q):
                    ffn_T(c, t)
            rows_to_T(2, 0, 0)

            weights_here(pe, "kvw")
            pe.wait_ge(s.biasrows_loaded, 16 * 12)
            w = w_of("kvw")
            for t in range(TT):
                if t == 1:
                    rows_to_T(2, 1, 0)
                pe.wait_ge(s.xT_ready, 10 + 4 * t)
                for k in range(KD):
                    mm = pe.matmul(ps[:, 4, t * P:(t + 1) * P], w[:, k, 0:P], xT2[:, k, t * P:(t + 1) * P], start=(k == 0), stop=(k == KD - 1))
                mm.then_inc(s.kT_mm, 1)
                b = 7 if t == 0 else 5
                for k in range(KD):
                    pe.matmul(ps[:, b, 0:P], xT2[:, k, t * P:(t + 1) * P], w[:, k, P:2 * P], start=(k == 0), stop=False)
                pe.matmul(ps[:, b, 0:P], cst[0:1, C_ONE:C_ONE + P], kvb_row[0:1, :], start=False, stop=True).then_inc(s.sv_mm, 1)
            pe.wait_ge(s.xT_ready, 16)
            weights_here(pe, "wq0")
            weights_here(pe, "wq1")
            wq = [w_of("wq0"), w_of("wq1")]

            def sq_products(u):
                if u == 1:
                    pe.wait_ge(s.sv_ready, 2)
                if u >= 2:
                    pe.wait_ge(s.sq_ready, 2 * u)
                for j in range(2):
                    g = 2 * u + j
                    for k in range(KD):
                        for v in range(KVH):
                            c0 = (v * G + g) * HD
                            mm = pe.matmul(ps[v * HD:(v + 1) * HD, Q_BANK[u], j * S:(j + 1) * S], wq[k // 4][:, k % 4, c0:c0 + HD],
                                           xT[:, k, :], start=(k == 0), stop=(k == KD - 1))
                mm.then_inc(s.sq_mm, 1)

            def sscores(i):
                g, v = i // 2, i % 2
                if i % 4 == 0:
                    pe.wait_ge(s.sq_ready, i // 2 + 2)
                if i >= 3:
                    pe.wait_ge(s.ss_ready, 2 * (i - 2))
                b, part = 2 + i % 3, 64 * v
                for t, c0, n in ((0, 0, P), (1, P, 2 * P)):
                    mm = pe.matmul(ps[:, b, c0:c0 + n], sqT[part:part + 64, g, t * P:(t + 1) * P], skT[part:part + 64, 0:n],
                                   start=True, stop=True)
                mm.then_inc(s.sscore_mm, 1)

            def sprobs_T(i):
                pe.wait_ge(s.sp_ready, 2 * i + 2)
                if i >= 2:
                    pe.wait_ge(s.spT_ready, i - 1)
                pe.transpose(ps[:, i % 2, 0:P], bias0[:, i, :], ident)
                pe.transpose(ps[:, i % 2, P:2 * P], bias1[:, i, 0:P], ident)
                pe.transpose(ps[:, i % 2, 2 * P:3 * P], bias1[:, i, P:2 * P], ident).then_inc(s.spT_mm, 1)

            def spv(i):
                g, v = i // 2, i % 2
                pe.wait_ge(s.spT_ready, i + 1)
                if i >= 2:
                    pe.wait_ge(s.soT_ready, i - 1)
                part = 64 * (g % 2)
                o = ps[part:part + 64, 6 + i % 2, :]
                v0, v1 = (sv[:, t, v * HD:(v + 1) * HD] for t in range(TT))
                pe.matmul(o[:, 0:P], v0, spT[:, i % 2, 0:P], start=True, stop=True)
                pe.matmul(o[:, P:S], v0, spT[:, i % 2, P:S], start=True, stop=False)
                pe.matmul(o[:, P:S], v1, spT[:, i % 2, S:3 * P], start=False, stop=True).then_inc(s.spv_mm, 1)

            def quad_scores(q):
                for i in range(4 * q, 4 * q + 4):
                    sscores(i)

            def quad_out(q, pending):
                for i in range(4 * q, 4 * q + 4):
                    sprobs_T(i)
                    if i > 4 * q or pending:
                        spv(i - 1)

            def swo_product(n, tiles, first, last):
                t, half = n // 2, n % 2
                w = w_of("swo%d" % half)
                for k in tiles:
                    mm = pe.matmul(ps[:, SWO_BANK[n], :], soT[:, k, t * P:(t + 1) * P], w[:, k, :],
                                   start=(first and k == tiles[0]), stop=(last and k == tiles[-1]))
                if last:
                    mm.then_inc(s.swo_mm, 1)

            sq_products(0)
            sq_products(1)
            pe.wait_ge(s.kT_ready, 1)
            quad_scores(0)
            sq_products(2)
            quad_scores(1)
            quad_out(0, False)
            sq_products(3)
            quad_scores(2)
            quad_out(1, True)
            spv(7)
            quad_scores(3)
            weights_here(pe, "swo0")
            weights_here(pe, "swo1")
            pe.wait_ge(s.soT_ready, 8)
            pe.wait_ge(s.sq_ready, 2 * 4)
            swo_product(0, (0, 4, 1, 5), True, False)
            quad_out(2, False)
            spv(11)
            pe.wait_ge(s.ss_ready, 2 * AH)
            pe.wait_ge(s.soT_ready, 12)
            swo_product(0, (2, 6), False, False)
            swo_product(1, (0, 4, 1, 5, 2, 6), True, False)
            quad_out(3, False)
            spv(AH - 1)
            pe.wait_ge(s.soT_ready, AH)
            swo_product(0, (3, 7), False, True)
            swo_product(1, (3, 7), False, True)
            swo_product(2, range(KD), True, True)
            rows_to_T(3, 0, 4)
            swo_product(3, range(KD), True, True)

            for t in range(TT):
                if t == 1:
                    rows_to_T(3, 1, 4)
                pe.wait_ge(s.xT_ready, 18 + 2 * t)
                for k in range(KD):
                    mm = pe.matmul(ps[:, 2, t * NE:(t + 1) * NE], xT[:, k, t * P:(t + 1) * P], wr[:, k, :], start=(k == 0), stop=(k == KD - 1))
                mm.then_inc(s.router_mm, 1)
            pe.wait_ge(s.route_mask, 1)
            tri, ones = cst[:, C_TRI:C_TRI + P], cst[:, C_ONE:C_ONE + P]
            m0, m1 = rt[:, 0, 8:16], rt[:, 1, 8:16]
            pe.matmul(ps[:, 1, 0:8], tri, m0, start=True, stop=True)
            pe.matmul(ps[:, 1, 8:16], ones, m0, start=True, stop=False)
            pe.matmul(ps[:, 1, 8:16], tri, m1, start=False, stop=True)
            pe.matmul(ps[:, 1, 16:24], ones, m0, start=True, stop=False)
            pe.matmul(ps[:, 1, 16:24], ones, m1, start=False, stop=True).then_inc(s.route_cum_mm, 1)

            def gather():
                for k in range(KD):
                    for t in range(TT):
                        mm = pe.matmul(ps[:, 2 + k // 4, (k % 4) * SLOTS:(k % 4 + 1) * SLOTS], xn[:, t, k * P:(k + 1) * P], sel[:, t, :],
                                       start=(t == 0), stop=(t == TT - 1))
                mm.then_inc(s.gath_mm, 1)

            def wide_step(bank, slots, left, right, first, last):
                lo, hi = slots[:, 0:NARROW], slots[:, NARROW:SLOTS]
                pe.matmul(ps[0:NARROW, bank, :], lo, left, start=first, stop=last)
                pe.matmul(ps[NARROW:SLOTS, bank, :], hi, left, start=first, stop=last)
                pe.matmul(ps[SLOTS:P, bank, :], hi, right, start=first, stop=last)
                pe.matmul(ps[0:NARROW, bank + 1, 0:LASTQ], lo, right[:, 0:LASTQ], start=first, stop=last)
                return pe.matmul(ps[64:64 + NARROW, bank + 1, 0:LASTQ], lo, right[:, LASTQ:2 * LASTQ], start=first, stop=last)

            def products(i, c, narrow):
                a = c % 2
                piece_here(pe, i, "g", c)
                piece_here(pe, i, "u", c)
                if c == 0:
                    pe.wait_ge(s.xgT_ready_a, i + 2)
                    pe.wait_ge(s.xgT_ready_v, i + 2)
                if c == 1:
                    pe.wait_ge(s.h_added, i * 4 + 5)
                else:
                    pe.wait_ge(s.hh_ready, i * (2 * ECH) + (2 * max(c - 1, 0) + 1))
                wg, wu = piece("g", c), piece("u", c)
                for k in range(KD):
                    if narrow:
                        lhs = xgT[:, k, 0:NARROW]
                        pe.matmul(ps[0:NARROW, 2 * a, :], lhs, wg[:, k, :], start=(k == 0), stop=(k == KD - 1))
                        mm = pe.matmul(ps[64:64 + NARROW, 2 * a + 1, :], lhs, wu[:, k, :], start=(k == 0), stop=(k == KD - 1))
                        continue
                    mm = wide_step(2 * a, xgT[:, k, :], wg[:, k, :], wu[:, k, :], k == 0, k == KD - 1)
                mm.then_inc(s.gu_mm, 1)

            def scatter(i):
                pe.wait_ge(s.y_ready_a, i + 1)
                pe.wait_ge(s.y_ready_v, i + 1)
                pe.wait_ge(s.sgt_ready, i + 1)
                for j in range(4):
                    t, half = j // 2, j % 2
                    if j == 3:
                        pe.wait_ge(s.xgT_ready_v, i + 2)
                    pe.matmul(ps[:, SCATTER_BANK[j], :], sgt[0:SLOTS, t, :], ysb[0:SLOTS, half * 512:(half + 1) * 512],
                              start=True, stop=True).then_inc(s.scat_mm, 1)

            def scatter_T(i):
                pe.wait_ge(s.selg_ready, i * 2 + 3)
                pe.wait_ge(s.h_added, i * 4 + 5)
                pe.transpose(ps[0:SLOTS, 7, 0:P], selg[:, 0, :], ident)
                pe.transpose(ps[0:SLOTS, 7, P:2 * P], selg[:, 1, :], ident).then_inc(s.sgt_mm, 1)

            def hidden_T(i, c):
                pe.wait_ge(s.hh_ready, i * (2 * ECH) + (2 * c + 3))
                pe.wait_ge(s.hhT_ready, i * ECH + (c + 1))
                for j in range(4):
                    mm = pe.transpose(ps[:, 4, j * SLOTS:(j + 1) * SLOTS], hh[0:SLOTS, c % 2, j * P:(j + 1) * P], ident[0:SLOTS, 0:SLOTS])
                mm.then_inc(s.tr_mm, 1)

            def down(i, c, narrow):
                piece_here(pe, i, "d", c)
                pe.wait_ge(s.hhT_ready, i * ECH + (c + 2))
                if c == 0:
                    pe.wait_ge(s.y_ready_a, i + 1)
                    pe.wait_ge(s.y_ready_v, i + 1)
                    pe.wait_ge(s.h_added, i * 4 + 4)
                w = piece("d", c)
                for j in range(4):
                    if narrow:
                        lhs = hhT[:, c % 2, j, 0:NARROW]
                        first, last = c == 0 and j == 0, c == ECH - 1 and j == 3
                        pe.matmul(ps[0:NARROW, 5, :], lhs, w[:, j, 0:512], start=first, stop=last)
                        mm = pe.matmul(ps[64:64 + NARROW, 6, :], lhs, w[:, j, 512:1024], start=first, stop=last)
                        continue
                    mm = wide_step(5, hhT[:, c % 2, j, :], w[:, j, 0:512], w[:, j, 512:1024],
                                   c == 0 and j == 0, c == ECH - 1 and j == 3)
                mm.then_inc(s.down_mm, 1)

            for q in (s.gu_mm, s.tr_mm, s.down_mm, s.gath_mm, s.sgt_mm, s.scat_mm):
                pe.sem_inc(q, 1)
            pe.wait_ge(s.sel_ready, 3)
            gather()
            pe.wait_ge(s.counts_ready, 1)
            items = pe.value_load(n_items[0:1, 0:1], min_val=NE, max_val=ITEMS_MAX)

            def pe_item(i, narrow):
                scatter(i)
                for c in range(ECH):
                    products(i, c, narrow)
                    if c == 4:
                        scatter_T(i)
                    if c >= 1:
                        hidden_T(i, c - 1)
                    if c >= 2:
                        down(i, c - 2, narrow)
                pe.wait_ge(s.sel_ready, i * 2 + 5)
                pe.wait_ge(s.hh_ready, i * (2 * ECH) + (2 * (ECH - 1) + 1))
                gather()
                hidden_T(i, ECH - 1)
                down(i, ECH - 2, narrow)
                down(i, ECH - 1, narrow)

            with pe.Fori(0, items) as i:
                many = pe.value_load(wide[0:1, bass.ds(i, 1)], min_val=0, max_val=1)
                with pe.If(many > 0):
                    pe_item(i, False)
                with pe.Else():
                    pe_item(i, True)
            scatter(items)

        @block.vector
        def _(dve):
            chain = [0]

            def link(ins):
                chain[0] += 1
                ins.then_inc(s.dve_chain, 1)
                dve.wait_ge(s.dve_chain, chain[0])

            squares, norms = [0], [0]

            def mean_squares(dst, src, width, n=1, tiles=1):
                squares[0] += tiles
                norms[0] += 1
                dve.wait_ge(s.ssq_ready, squares[0])
                dve.tensor_scalar(stat[:, dst:dst + n], stat[:, src:src + n], 1.0 / width, EPS, ALU.mult, ALU.add).then_inc(s.ms_ready, 1)

            def norm_rows(t, gain=None):
                mean_squares(2 + t, t, D)
                dve.wait_ge(s.rstd_ready, norms[0])
                if gain is None:
                    dve.tensor_scalar(xn[:, t, :], h[:, t, :], stat[:, 4 + t:5 + t], None, ALU.mult).then_inc(s.xn_ready, 1)
                else:
                    dve.scalar_tensor_tensor(out=xn[:, t, :], in0=h[:, t, :], scalar=stat[:, 4 + t:5 + t], in1=gain,
                                             op0=ALU.mult, op1=ALU.mult).then_inc(s.xn_ready, 1)

            def evac_xT(n, t, off, dst, gain):
                dve.wait_ge(s.xT_mm, 2 * n + t + 1)
                for b in range(2):
                    src = ps[:, off + 2 * t + b, :].rearrange("p (k n) -> p k n", k=4)
                    o = dst[:, 4 * b:4 * b + 4, t * P:(t + 1) * P]
                    if gain is None:
                        dve.tensor_copy(o, src).then_inc(s.xT_ready, 1)
                    else:
                        g = vecT[:, gain + 4 * b:gain + 4 * b + 4].unsqueeze(2).to_broadcast([P, 4, P])
                        dve.tensor_tensor(o, src, g, ALU.mult).then_inc(s.xT_ready, 1)

            dve.wait_ge(s.consts_loaded, 16)
            dve.wait_ge(s.smalls_loaded, 160)
            link(dve.tensor_copy(pos_f[:], pos_i[:]))
            for t in range(TT):
                link(dve.tensor_scalar(ang[:, 0, t, :], cst[:, C_INV:C_INV + HALF], pos_f[:, t:t + 1], None, ALU.mult))

            def reduced(dst, quarter):
                link(dve.tensor_scalar(ang[:, 1], ang[:, 0], float(1 / TWO_PI), quarter, ALU.mult, ALU.add))
                link(dve.tensor_scalar(ang[:, 1], ang[:, 1], MAGIC, MAGIC, ALU.add, ALU.subtract))
                link(dve.scalar_tensor_tensor(out=ang[:, 2], in0=ang[:, 1], scalar=-C1, in1=ang[:, 0], op0=ALU.mult, op1=ALU.add))
                link(dve.scalar_tensor_tensor(out=ang[:, 2], in0=ang[:, 1], scalar=-C2, in1=ang[:, 2], op0=ALU.mult, op1=ALU.add))
                link(dve.scalar_tensor_tensor(out=ang[:, 2], in0=ang[:, 1], scalar=-C3, in1=ang[:, 2], op0=ALU.mult, op1=ALU.add))
                link(dve.tensor_scalar(ang[:, 2], ang[:, 2], quarter * TWO_PI, PI_LO, ALU.add, ALU.min))
                dve.tensor_scalar(ang[:, dst], ang[:, 2], -PI_LO, None, ALU.max).then_inc(s.rope_arg, 1)

            norm_rows(0)
            norm_rows(1)
            dve.wait_ge(s.vecT_ready, 1)
            evac_xT(0, 0, 0, xT, V_GA0)
            evac_xT(0, 1, 0, xT, V_GA0)
            reduced(4, 0.0)
            dve.wait_ge(s.rope_arg, 1)
            reduced(5, 0.25)
            mean_squares(8, 0, QL, 2, 2)
            dve.wait_ge(s.rstd_ready, 3)
            for t in range(TT):
                dve.tensor_scalar(cq[:, t, :], ps[:, 4 + t, 0:QL], stat[:, 12 + t:13 + t], None, ALU.mult).then_inc(s.cq_ready, 1)
            mean_squares(10, 6, KVL, 2, 2)
            dve.wait_ge(s.cT_mm, 1)
            for k in range(3):
                dve.tensor_scalar(cqT[:, k, :], ps[:, k // 2, (k % 2) * S:(k % 2 + 1) * S], gcol(V_GQ, k), None, ALU.mult).then_inc(s.cqT_ready, 1)
            dve.wait_ge(s.rstd_ready, 4)
            for t in range(TT):
                dve.tensor_scalar(ckv[:, t, :], ps[:, 6 + t, 0:KVL], stat[:, 14 + t:15 + t], None, ALU.mult).then_inc(s.ckv_ready, 1)

            dve.wait_ge(s.sincos_ready, 2)
            for t in range(TT):
                x1, x2 = ps[:, 6 + t, KVL:KVL + HALF], ps[:, 6 + t, KVL + HALF:KVL + ROPE]
                cos, sin = cosn[:, t, 0:HALF], cosn[:, t, HALF:2 * HALF]
                a, b, c, d = (rtmp[:, 0, n * HALF:(n + 1) * HALF] for n in range(4))
                dve.tensor_tensor(a, x1, cos, ALU.mult)
                dve.tensor_tensor(b, x2, sin, ALU.mult)
                dve.tensor_tensor(c, x2, cos, ALU.mult)
                link(dve.tensor_tensor(d, x1, sin, ALU.mult))
                krv = kr[:, t, :].rearrange("p (r n) -> p r n", r=2)
                link(dve.tensor_tensor(krv[:, 0, 0:HALF], a, b, ALU.subtract))
                link(dve.tensor_tensor(krv[:, 0, HALF:ROPE], c, d, ALU.add))
                dve.tensor_copy(krv[:, 1, :], krv[:, 0, :]).then_inc(s.krope_ready, 1)
            for t in range(TT):
                dve.wait_ge(s.qrope_mm, 3 + t)
                q = ps[:, 4 + t, :].rearrange("p (h n) -> p h n", n=ROPE)
                x1, x2 = q[:, :, 0:HALF], q[:, :, HALF:ROPE]
                o = qr[:, t, :].rearrange("p (h n) -> p h n", n=ROPE)
                cos = cosn[:, t:t + 1, 0:HALF].to_broadcast([P, MH, HALF])
                sin = cosn[:, t:t + 1, HALF:2 * HALF].to_broadcast([P, MH, HALF])
                a = rtmp[:, 0, :].rearrange("p (h n) -> p h n", n=HALF)
                b = rtmp[:, 1, :].rearrange("p (h n) -> p h n", n=HALF)
                link(dve.tensor_tensor(a, x1, cos, ALU.mult))
                link(dve.tensor_tensor(b, x2, sin, ALU.mult))
                dve.tensor_tensor(o[:, :, 0:HALF], a, b, ALU.subtract).then_inc(s.qrope_ready, 1)
                dve.wait_ge(s.qrope_ready, 2 * t + 1)
                link(dve.tensor_tensor(a, x2, cos, ALU.mult))
                link(dve.tensor_tensor(b, x1, sin, ALU.mult))
                dve.tensor_tensor(o[:, :, HALF:ROPE], a, b, ALU.add).then_inc(s.qrope_ready, 1)
                dve.wait_ge(s.qrope_ready, 2 * t + 2)
            dve.wait_ge(s.qrT_mm, 1)
            for k in range(4):
                dve.tensor_copy(qrT[:, k, :], ps[:, 4 + k // 2, (k % 2) * S:(k % 2 + 1) * S]).then_inc(s.qrT_ready, 1)

            def mla_max(i):
                dve.wait_ge(s.score_mm, i + 1)
                st = mstat[:, i, :]
                dve.tensor_tensor(probs[:, i, :], ps[:, i % 4, 0:3 * P], cst[:, C_MLA:C_MLA + 3 * P], ALU.add).then_inc(s.s_ready, 1)
                dve.wait_ge(s.s_ready, i + 1)
                dve.tensor_reduce(st[:, 0:1], probs[:, i, 0:P], AX.X, ALU.max, negate=True)
                link(dve.tensor_reduce(st[:, 1:2], probs[:, i, P:3 * P], AX.X, ALU.max, negate=True))
                dve.tensor_scalar(st[:, 2:4], st[:, 0:2], MLA_SCALE, None, ALU.mult).then_inc(s.negmax_ready, 2)

            def mla_norm(i):
                st = mstat[:, i, :]
                dve.wait_ge(s.exp_ready, 2 * i + 2)
                link(dve.reciprocal(st[:, 6:8], st[:, 4:6]))
                dve.tensor_scalar(probs[:, i, 0:P], probs[:, i, 0:P], st[:, 6:7], None, ALU.mult).then_inc(s.p_ready, 1)
                dve.tensor_scalar(probs[:, i, P:3 * P], probs[:, i, P:3 * P], st[:, 7:8], None, ALU.mult).then_inc(s.p_ready, 1)

            def mla_out(i):
                dve.wait_ge(s.pv_mm, i + 1)
                dve.tensor_copy(oT[:, i, :], ps[:, 6 + i % 2, 0:S]).then_inc(s.oT_ready, 1)

            for i in range(MH + 3):
                if i < MH:
                    mla_max(i)
                if 1 <= i <= MH:
                    mla_norm(i - 1)
                if i >= 3:
                    mla_out(i - 3)
            dve.wait_ge(s.biasrows_loaded, 16 * 12)
            link(dve.tensor_copy(posq[:], posq_i[:]))
            link(dve.tensor_copy(posk[:], posk_i[:]))
            link(dve.tensor_scalar(posk[:], posk[:], cst[:, C_THR:C_THR + 1], None, ALU.add))
            dve.wait_ge(s.rel_loaded, 16 * 8)
            by_h = [tabs_h[:, n, :].rearrange("p (k v g) -> p k v g", k=4, v=KVH) for n in range(2)]
            dve.tensor_tensor(tabs[:].rearrange("p (k g v) -> p k v g", k=4, v=KVH), by_h[0], by_h[1], ALU.subtract).then_inc(s.table_step, 1)
            for n in range(3):
                dve.wait_ge(s.table_step, 2 * n + 1)
                dve.tensor_copy(tab_parts[:, n, :], tabs[:]).then_inc(s.delta_ready, 1)
                if n < 2:
                    dve.wait_ge(s.delta_ready, n + 1)
                    dve.tensor_tensor(tabs[:], tabs[:], tab_parts[:, n, :], ALU.subtract).then_inc(s.table_step, 2)
            link(dve.tensor_copy(sinks[:].rearrange("p (g v) -> p v g", v=KVH), sinks_h[:].rearrange("p (v g) -> p v g", v=KVH)))

            def add_out(n, mm, done, bank=(0, 1, 2, 3)):
                t, half = n // 2, n % 2
                dve.wait_ge(mm, n + 1)
                hv = h[:, t, half * 512:(half + 1) * 512]
                dve.tensor_tensor(hv, hv, ps[:, bank[n], :], ALU.add).then_inc(done, 1)

            def w_lo_part(q):
                w, hi, lo = unit_of_weights(q)
                weights_here(dve, "f%s%d" % units[q][:2])
                dve.wait_ge(s.whi_ready, q + 1)
                if q >= 2:
                    dve.wait_ge(*used_up(q - 2))
                dve.tensor_tensor(lo, w, hi.bitcast(F32), ALU.subtract).then_inc(s.wlo_ready, 1)

            def evac_xT_split(t):
                dve.wait_ge(s.xT_mm, 2 + t + 1)
                for b in range(2):
                    src = ps[:, 4 + 2 * t + b, :].rearrange("p (k n) -> p k n", k=4)
                    g = vecT[:, V_GF0 + 4 * b:V_GF0 + 4 * b + 4].unsqueeze(2).to_broadcast([P, 4, P])
                    dve.tensor_tensor(x_gained(t, b), src, g, ALU.mult).then_inc(s.xg_ready, 1)
                for b in range(2):
                    part = (slice(None), slice(4 * b, 4 * b + 4), slice(t * P, (t + 1) * P))
                    dve.wait_ge(s.xg_ready, 2 * t + b + 1)
                    dve.wait_ge(s.xhi_ready, 2 * t + b + 1)
                    dve.tensor_tensor(xT_lo[part], x_gained(t, b), xT_hi[part].bitcast(F32), ALU.subtract).then_inc(s.xT_ready, 1)

            w_lo_part(0)
            w_lo_part(1)
            add_out(0, s.wo_mm, s.h_attn0)
            add_out(1, s.wo_mm, s.h_attn0)
            norm_rows(0)
            add_out(2, s.wo_mm, s.h_attn0)
            evac_xT_split(0)
            add_out(3, s.wo_mm, s.h_attn0)
            norm_rows(1)
            evac_xT_split(1)

            def onehots(r):
                if r >= 2:
                    dve.wait_ge(s.bias_mm, r - 1)
                for j, t, col in ((0, 1, 2 * r), (1, 1, 2 * r + 1), (2, 0, 64 + r)):
                    dve.tensor_scalar(onehot[:, r % 2, j, :], posq[:, t * P:(t + 1) * P], posk[:, col:col + 1], None,
                                      ALU.is_ge).then_inc(s.onehot_ready, 1)

            def bias_out(r):
                dve.wait_ge(s.bias_mm, r + 1)
                for dst, c0, nj, m, n in ((bias1, 0, 2, C_WIN, S), (bias0, 128, 1, C_WIN + P, P)):
                    src = ps[:, 7, c0:c0 + nj * 64].rearrange("p (j k h) -> p j k h", j=nj, k=4)
                    mask = cst[:, m:m + n].rearrange("p (k j) -> p j k", k=4)[:, nj * r:nj * r + nj, :]
                    o = dst.rearrange("p h (k j) -> p j k h", k=4)[:, nj * r:nj * r + nj]
                    dve.tensor_tensor(o, src, mask.unsqueeze(3).to_broadcast([P, nj, 4, AH]), ALU.add).then_inc(s.bias_ready, 1)

            def ffn_hidden(c, t):
                n = f_cols(c)
                dve.wait_ge(s.fsg_ready, 2 * c + t + 1)
                if c >= 1:
                    dve.wait_ge(s.ftr_mm, 2 * (c - 1) + t + 1)
                dve.tensor_tensor(fhh[:, t, 0:n], fsg[:, t, 0:n], ps[:, 2 * t + 1, 0:n], ALU.mult).then_inc(s.fhh_ready, 1)

            def hidden_rows(c):
                dve.wait_ge(*used_up(units_of("u", c)[-1]))
                for t in range(TT):
                    ffn_hidden(c, t)

            def hidden_T_lo(c, t):
                dve.wait_ge(s.fhhT_hi_ready, both_or(c, t))
                dve.tensor_tensor(hidden_T_place(fhhT_lo, c, t), hidden_T_bank(c, t),
                                  hidden_T_place(fhhT_hi, c, t).bitcast(F32), ALU.subtract).then_inc(s.fhhT_lo_ready, 1)

            def ffn_add(n):
                c, t, half, _ = downs[n]
                dve.wait_ge(s.fdown_mm, n + 1)
                hv = h[:, t, half * 512:(half + 1) * 512]
                before = [m for m in range(n) if downs[m][1:3] == (t, half)]
                if before:
                    dve.wait_ge(s.fh_added, before[-1] + 1)
                dve.tensor_tensor(hv, hv, ps[:, 5 + n % 2, :], ALU.add).then_inc(s.fh_added, 1)

            for q in range(1, NU):
                if q >= 2:
                    w_lo_part(q)
                if bias_round_of(q) is not None:
                    onehots(bias_round_of(q))
                for c, t in rows_T_of(q - 2):
                    hidden_T_lo(c, t)
                c = units[q - 2][1] if q >= 2 and units[q - 2][0] == "u" and units[q - 1][0] != "u" else None
                if c == FCH - 1:
                    hidden_rows(c)
                if bias_round_of(q - 1) is not None:
                    bias_out(bias_round_of(q - 1))
                for n, d in enumerate(downs):
                    if d[3] == q - 1:
                        ffn_add(n)
                if c is not None and c < FCH - 1:
                    hidden_rows(c)
            bias_out(bias_round_of(NU - 1))
            n0 = 4 * (FCH - 1)
            ffn_add(n0)
            ffn_add(n0 + 1)
            norm_rows(0)
            ffn_add(n0 + 2)
            ffn_add(n0 + 3)
            evac_xT(2, 0, 0, xT2, V_KVG)
            evac_xT(2, 0, 0, xT, V_GA1)
            norm_rows(1)
            evac_xT(2, 1, 0, xT2, V_KVG)
            evac_xT(2, 1, 0, xT, V_GA1)

            def swa_scores(q):
                for i in range(4 * q, 4 * q + 4):
                    dve.wait_ge(s.sscore_mm, i + 1)
                    b = 2 + i % 3
                    dve.scalar_tensor_tensor(out=bias0[:, i, :], in0=ps[:, b, 0:P], scalar=SWA_SCALE, in1=bias0[:, i, :],
                                             op0=ALU.mult, op1=ALU.add).then_inc(s.ss_ready, 1)
                    dve.scalar_tensor_tensor(out=bias1[:, i, :], in0=ps[:, b, P:3 * P], scalar=SWA_SCALE, in1=bias1[:, i, :],
                                             op0=ALU.mult, op1=ALU.add).then_inc(s.ss_ready, 1)
                c = slice(4 * q, 4 * q + 4)
                dve.wait_ge(s.ss_ready, 8 * q + 8)
                dve.tensor_reduce(sstat[:, 0, 0, c], bias0[:, c, :], AX.X, ALU.max)
                link(dve.tensor_reduce(sstat[:, 0, 1, c], bias1[:, c, :], AX.X, ALU.max))
                sk = sinks[:, c].unsqueeze(1).to_broadcast([P, 2, 4])
                link(dve.tensor_tensor(sstat[:, 5, :, c], sstat[:, 0, :, c], sk, ALU.max))
                link(dve.tensor_tensor(sstat[:, 2, :, c], sk, sstat[:, 5, :, c], ALU.subtract))
                dve.tensor_scalar(sstat[:, 1, :, c], sstat[:, 5, :, c], -1.0, None, ALU.mult).then_inc(s.snegmax_ready, 1)

            def swa_norm(q):
                c = slice(4 * q, 4 * q + 4)
                dve.wait_ge(s.sexp_ready, 8 * q + 8)
                dve.wait_ge(s.esink_ready, q + 1)
                link(dve.tensor_tensor(sstat[:, 6, :, c], sstat[:, 4, :, c], sstat[:, 3, :, c], ALU.add))
                link(dve.reciprocal(sstat[:, 7, :, c], sstat[:, 6, :, c]))
                for i in range(4 * q, 4 * q + 4):
                    dve.tensor_scalar(bias0[:, i, :], bias0[:, i, :], sstat[:, 7, 0, i:i + 1], None, ALU.mult).then_inc(s.sp_ready, 1)
                    dve.tensor_scalar(bias1[:, i, :], bias1[:, i, :], sstat[:, 7, 1, i:i + 1], None, ALU.mult).then_inc(s.sp_ready, 1)

            swa_scores(0)
            swa_norm(0)
            swa_scores(1)
            swa_norm(1)
            swa_scores(2)
            swa_scores(3)
            swa_norm(2)
            swa_norm(3)
            dve.wait_ge(s.bo_added, 2)
            dve.wait_ge(s.rel_loaded, 16 * 10)
            add_out(0, s.swo_mm, s.h_attn1, SWO_BANK)
            add_out(1, s.swo_mm, s.h_attn1, SWO_BANK)
            norm_rows(0, grow)
            add_out(2, s.swo_mm, s.h_attn1, SWO_BANK)
            evac_xT(3, 0, 4, xT, None)
            add_out(3, s.swo_mm, s.h_attn1, SWO_BANK)
            norm_rows(1, grow)
            dve.memset(ysb[:], 0.0).then_inc(s.y_last, 1)
            dve.memset(sgt[:], 0.0).then_inc(s.y_last, 1)
            dve.memset(hh[:], 0.0).then_inc(s.y_last, 1)
            dve.memset(slots[:, :, ITEMS_MAX:ITEMS_MAX + 1], -1.0).then_inc(s.y_last, 1)
            dve.memset(gates[:, :, ITEMS_MAX:ITEMS_MAX + 1], 0.0).then_inc(s.y_last, 1)
            evac_xT(3, 1, 4, xT, None)
            lg, mask, top, idx = (rt[:, :, 8 * n:8 * n + 8] for n in range(4))
            o1, o2, z, g1 = (rt[:, :, 8 * n:8 * n + 8] for n in range(4, 8))
            e8 = cst[:, C_E8:C_E8 + NE].unsqueeze(1).to_broadcast([P, TT, NE])
            dve.wait_ge(s.router_mm, 2)
            link(dve.tensor_copy(lg, ps[:, 2, 0:TT * NE].rearrange("p (t n) -> p t n", t=TT)))
            dve.max(top[:, 0, :], lg[:, 0, :])
            link(dve.max(top[:, 1, :], lg[:, 1, :]))
            dve.max_index(ridx[:, 0, :], top[:, 0, :], lg[:, 0, :])
            link(dve.max_index(ridx[:, 1, :], top[:, 1, :], lg[:, 1, :]))
            link(dve.tensor_copy(idx, ridx[:]))
            dve.tensor_tensor(o1, e8, idx[:, :, 0:1].to_broadcast([P, TT, NE]), ALU.is_equal)
            link(dve.tensor_tensor(o2, e8, idx[:, :, 1:2].to_broadcast([P, TT, NE]), ALU.is_equal))
            dve.tensor_tensor(mask, o1, o2, ALU.add).then_inc(s.route_mask, 1)
            dve.tensor_tensor(z[:, :, 0:1], top[:, :, 1:2], top[:, :, 0:1], ALU.subtract).then_inc(s.gate_arg, 1)
            dve.wait_ge(s.route_cum_mm, 1)
            cum = rt[:, :, 64:72]
            link(dve.scalar_tensor_tensor(out=cum, in0=ps[:, 1, 0:TT * NE].rearrange("p (t n) -> p t n", t=TT), scalar=1.0, in1=mask,
                                          op0=ALU.add, op1=ALU.mult))
            for w in range(SWEEPS):
                link(dve.tensor_scalar(slots[:, :, w * NE:(w + 1) * NE], cum, -1.0 - w * SLOTS, None, ALU.add))
                if w == 0:
                    for q in (s.sel_ready, s.selg_ready, s.hh_ready, s.y_ready_v, s.xgT_ready_v, s.h_added):
                        dve.sem_inc(q, 1)
                    for t in range(TT):
                        dve.tensor_scalar(sel[:, t, :], cst[:, C_IOTA:C_IOTA + SLOTS], slots[:, t, 0:1], None, ALU.is_equal).then_inc(s.sel_ready, 1)
            counts, top_count, more = ps[:, 1, 16:24], rt[:, 0, 24:25], rt[:, 0, 25:25 + SWEEPS - 1]
            link(dve.tensor_reduce(top_count, counts, AX.X, ALU.max))
            for w in range(1, SWEEPS):
                link(dve.tensor_scalar(more[:, w - 1:w], top_count, w * SLOTS + 0.5, float(NE), ALU.is_ge, ALU.mult))
            link(dve.tensor_reduce(rt[:, 0, 28:29], more, AX.X, ALU.add))
            link(dve.tensor_scalar(n_items[:, 0:1], rt[:, 0, 28:29], float(NE), None, ALU.add))
            for w in range(SWEEPS):
                wide_w = dve.tensor_scalar(wide[:, w * NE:(w + 1) * NE], counts, w * SLOTS + NARROW + 0.5, None, ALU.is_ge)
                if w < SWEEPS - 1:
                    link(wide_w)
            wide_w.then_inc(s.counts_ready, 1)
            dve.wait_ge(s.counts_ready, 1)
            dve.wait_ge(s.gath_mm, 2)
            dve.tensor_copy(xgT[:, 0:4, :].rearrange("p k n -> p (k n)"), ps[:, 2, 0:4 * SLOTS]).then_inc(s.xgT_ready_v, 1)
            dve.wait_ge(s.gate_exp, 1)
            link(dve.tensor_scalar(z[:, :, 2:3], z[:, :, 1:2], 1.0, None, ALU.add))
            link(dve.reciprocal(z[:, :, 3:4], z[:, :, 2:3]))
            link(dve.tensor_tensor(z[:, :, 4:5], z[:, :, 1:2], z[:, :, 3:4], ALU.mult))
            link(dve.tensor_tensor(g1, o1, z[:, :, 3:4].to_broadcast([P, TT, NE]), ALU.mult))
            link(dve.tensor_tensor(o2, o2, z[:, :, 4:5].to_broadcast([P, TT, NE]), ALU.mult))
            for w in range(SWEEPS):
                link(dve.tensor_tensor(gates[:, :, w * NE:(w + 1) * NE], g1, o2, ALU.add))

            iota = cst[:, C_IOTA:C_IOTA + SLOTS]

            items = dve.value_load(n_items[0:1, 0:1], min_val=NE, max_val=ITEMS_MAX)

            def add_rows(i, j):
                t, half = j // 2, j % 2
                dve.wait_ge(s.scat_mm, i * 4 + (j + 2))
                hv = h[:, t, half * 512:(half + 1) * 512]
                dve.tensor_tensor(hv, hv, ps[:, SCATTER_BANK[j], :], ALU.add).then_inc(s.h_added, 1)


            def dve_item(i, narrow):
                for j in range(4):
                    add_rows(i, j)
                dve.wait_ge(s.sgt_mm, i + 1)
                for t in range(TT):
                    dve.tensor_scalar(selg[:, t, :], iota, slots[:, t, bass.ds(i, 1)], gates[:, t, bass.ds(i, 1)], ALU.is_equal, ALU.mult).then_inc(s.selg_ready, 1)
                dve.wait_ge(s.gath_mm, i + 2)
                for t in range(TT):
                    dve.tensor_scalar(sel[:, t, :], iota, slots[:, t, bass.ds(i + 1, 1)], None, ALU.is_equal).then_inc(s.sel_ready, 1)
                for c in range(ECH):
                    a = c % 2
                    dve.wait_ge(s.sg_ready, i * (4 * ECH) + (4 * c + 5))
                    dve.wait_ge(s.tr_mm, i * ECH + (max(c - 1, 0) + 1))
                    if narrow:
                        dve.tensor_tensor(hh[0:NARROW, a, :], sg[0:NARROW, a, :], upl[0:NARROW, a, :], ALU.mult).then_inc(s.hh_ready, 2)
                    else:
                        dve.tensor_tensor(hh[0:NARROW, a, 0:LASTQ], sg[0:NARROW, a, 0:LASTQ], ps[0:NARROW, 2 * a + 1, 0:LASTQ], ALU.mult).then_inc(s.hh_first, 1)
                        dve.tensor_tensor(hh[0:NARROW, a, LASTQ:FC], sg[0:NARROW, a, LASTQ:FC], upl[0:NARROW, a, LASTQ:FC], ALU.mult).then_inc(s.hh_ready, 1)
                        dve.tensor_tensor(hh[NARROW:SLOTS, a, :], sg[NARROW:SLOTS, a, :], upl[NARROW:SLOTS, a, :], ALU.mult).then_inc(s.hh_ready, 1)
                dve.wait_ge(s.gath_mm, i + 3)
                dve.tensor_copy(xgT[:, 0:4, :].rearrange("p k n -> p (k n)"), ps[:, 2, 0:4 * SLOTS]).then_inc(s.xgT_ready_v, 1)
                dve.wait_ge(s.down_mm, i * ECH + (ECH + 1))
                if narrow:
                    dve.tensor_copy(ysb[0:NARROW, 512:1024], ps[64:64 + NARROW, 6, :]).then_inc(s.y_ready_v, 1)
                else:
                    dve.tensor_copy(ysb[0:NARROW, 512:768], ps[0:NARROW, 6, 0:LASTQ]).then_inc(s.y_last, 1)
                    dve.tensor_copy(ysb[0:NARROW, 768:1024], ps[64:64 + NARROW, 6, 0:LASTQ]).then_inc(s.y_ready_v, 1)

            with dve.Fori(0, items) as i:
                many = dve.value_load(wide[0:1, bass.ds(i, 1)], min_val=0, max_val=1)
                with dve.If(many > 0):
                    dve_item(i, False)
                with dve.Else():
                    dve_item(i, True)
            for j in range(4):
                add_rows(items, j)
            dve.wait_ge(s.rel_loaded, 16 * 11)
            for t in range(TT):
                norm_rows(t, gfin)


_INS = ["x", "positions", "mla_w_in", "mla_g_q", "mla_g_kv", "mla_w_uq", "mla_w_ukv", "mla_w_o", "kv_g", "kv_w", "kv_b",
        "swa_w_q", "swa_b_q", "swa_sinks", "swa_w_o", "swa_b_o", "rel_bias", "g_attn", "g_ffn", "ffn_w_gate", "ffn_w_up",
        "ffn_w_down", "moe_w_router", "moe_w_gate", "moe_w_up", "moe_w_down", "g_final"]


def kernel(**inputs):
    import concourse.bacc as bacc
    from concourse.bass_utils import run_bass_kernel_spmd

    nc = bacc.Bacc("TRN2", target_bir_lowering=False, num_devices=1)
    arrays, args = {}, []
    for name in _INS:
        a = np.ascontiguousarray(inputs[name])
        arrays["in_" + name] = a
        args.append(nc.dram_tensor("in_" + name, a.shape, mybir.dt.from_np(a.dtype), kind="ExternalInput").ap())
    arrays["consts"] = constants()
    args.append(nc.dram_tensor("consts", (P, C_N), F32, kind="ExternalInput").ap())
    args.append(nc.dram_tensor("out_0", (1, S, D), F32, kind="ExternalOutput").ap())
    build(nc, *args)
    r = run_bass_kernel_spmd(nc, [arrays], core_ids=[0])
    return r.results[0]["out_0"]
```
